# Optimizing a Trainium2 kernel written in Bass

```python
import math
import jax, jax.numpy as jnp
from jax import lax
import numpy as np

D_MODEL = 1024
BATCH = 1
SEQ = 256
DEPTH = 2

N_A_LAYERS = (DEPTH + 1) // 2
N_B_LAYERS = DEPTH - N_A_LAYERS
HEAD_DIM = 64
MEM_HEADS = 4
MEM_WIDTH = MEM_HEADS * HEAD_DIM
PRIMARY_WIDTH = D_MODEL - MEM_WIDTH
B_HEADS = PRIMARY_WIDTH // HEAD_DIM
CONV_CH = PRIMARY_WIDTH
CONV_WIDTH = 31
D_FF = 256 * ((8 * D_MODEL // 3 + 255) // 256)
MOBA_BLOCK = 256
MOBA_TOPK = 3
Q_CHUNK = 16
ROPE_THETA = 500000.0
ROPE_DIM = HEAD_DIM // 4
EPS = 1e-6


def rms_norm(x, g):
    xf = x.astype(jnp.float32)
    y = xf * lax.rsqrt(jnp.mean(xf * xf, axis=-1, keepdims=True) + EPS)
    return (y * g.astype(jnp.float32)).astype(x.dtype)

def layer_norm(x, g, b):
    xf = x.astype(jnp.float32)
    xc = xf - jnp.mean(xf, axis=-1, keepdims=True)
    y = xc * lax.rsqrt(jnp.mean(xc * xc, axis=-1, keepdims=True) + EPS)
    return (y * g.astype(jnp.float32) + b.astype(jnp.float32)).astype(x.dtype)

def swiglu(x, w_gate, w_up, w_down):
    return (jax.nn.silu(x @ w_gate) * (x @ w_up)) @ w_down

def partial_rope(x, positions):
    half = ROPE_DIM // 2
    inv_freq = 1.0 / (ROPE_THETA ** (jnp.arange(0, ROPE_DIM, 2, dtype=jnp.float32) / ROPE_DIM))
    ang = positions.astype(jnp.float32)[..., None] * inv_freq
    cos = jnp.cos(ang)[:, :, None, :]
    sin = jnp.sin(ang)[:, :, None, :]
    xr = x[..., :ROPE_DIM].astype(jnp.float32)
    x1, x2 = xr[..., :half], xr[..., half:]
    rot = jnp.concatenate([x1 * cos - x2 * sin, x2 * cos + x1 * sin], axis=-1)
    return jnp.concatenate([rot.astype(x.dtype), x[..., ROPE_DIM:]], axis=-1)

def conformer_conv(u, dw_kernel, dw_bias, ln_g, ln_b):
    a, gate = jnp.split(u, 2, axis=-1)
    h = a * jax.nn.sigmoid(gate)
    h = lax.conv_general_dilated(h, dw_kernel.astype(h.dtype), window_strides=(1,),
                                 padding=[(CONV_WIDTH - 1, 0)],
                                 dimension_numbers=('NWC', 'WIO', 'NWC'),
                                 feature_group_count=CONV_CH) + dw_bias
    return jax.nn.silu(layer_norm(h, ln_g, ln_b))

def memory_attention(q, mem_n, w_mem_kv, q_g, k_g):
    B, S = q.shape[:2]
    M = mem_n.shape[1]
    k, v = jnp.split(mem_n @ w_mem_kv, 2, axis=-1)
    k = rms_norm(k.reshape(B, M, MEM_HEADS, HEAD_DIM), k_g)
    v = v.reshape(B, M, MEM_HEADS, HEAD_DIM)
    q = rms_norm(q.reshape(B, S, MEM_HEADS, HEAD_DIM), q_g)
    logits = jnp.einsum('bshd,bmhd->bhsm', q, k).astype(jnp.float32) * (HEAD_DIM ** -0.5)
    p = jax.nn.softmax(logits, axis=-1).astype(v.dtype)
    return jnp.einsum('bhsm,bmhd->bshd', p, v).reshape(B, S, MEM_WIDTH)

def shared_moba_kv(h, positions, kv_norm_g, w_kv, k_norm_g):
    B, S, _ = h.shape
    k, v = jnp.split(rms_norm(h, kv_norm_g) @ w_kv, 2, axis=-1)
    k = partial_rope(rms_norm(k.reshape(B, S, B_HEADS, HEAD_DIM), k_norm_g), positions)
    v = v.reshape(B, S, B_HEADS, HEAD_DIM)
    n_blocks = -(-S // MOBA_BLOCK)
    pad = n_blocks * MOBA_BLOCK - S

    def to_blocks(t):
        t = jnp.pad(t, ((0, 0), (0, pad), (0, 0), (0, 0)))
        return t.reshape(B, n_blocks, MOBA_BLOCK, B_HEADS, HEAD_DIM).transpose(0, 3, 1, 2, 4)

    k_blocks = to_blocks(k)
    v_blocks = to_blocks(v)
    k_mean = jnp.mean(k_blocks.astype(jnp.float32), axis=3).astype(k_blocks.dtype)
    return k_blocks, v_blocks, k_mean

def moba_attention(q, k_blocks, v_blocks, k_mean):
    B, S, H, Dh = q.shape
    n_blocks = k_blocks.shape[2]
    topk = min(MOBA_TOPK, n_blocks)
    n_chunks = S // Q_CHUNK
    scale = Dh ** -0.5
    q_chunks = q.reshape(B, n_chunks, Q_CHUNK, H, Dh).transpose(1, 0, 3, 2, 4)
    b_idx = jnp.arange(B)[:, None, None, None]
    h_idx = jnp.arange(H)[None, :, None, None]

    def chunk_attend(args):
        q_c, c = args
        start = c * Q_CHUNK
        own = start // MOBA_BLOCK
        gate = jnp.einsum('bhqd,bhnd->bhqn', q_c, k_mean).astype(jnp.float32)
        gate = jnp.where(jnp.arange(n_blocks) < own, gate, -jnp.inf)
        _, sel = lax.top_k(gate, topk)
        valid = jnp.arange(topk) < own
        k_sel = k_blocks[b_idx, h_idx, sel]
        v_sel = v_blocks[b_idx, h_idx, sel]
        k_own = lax.dynamic_index_in_dim(k_blocks, own, axis=2, keepdims=False)
        v_own = lax.dynamic_index_in_dim(v_blocks, own, axis=2, keepdims=False)
        s_sel = jnp.einsum('bhqd,bhqnjd->bhqnj', q_c, k_sel).astype(jnp.float32) * scale
        s_sel = jnp.where(valid[:, None], s_sel, -jnp.inf)
        s_own = jnp.einsum('bhqd,bhjd->bhqj', q_c, k_own).astype(jnp.float32) * scale
        q_pos = start + jnp.arange(Q_CHUNK)
        k_pos = own * MOBA_BLOCK + jnp.arange(MOBA_BLOCK)
        s_own = jnp.where(k_pos[None, :] <= q_pos[:, None], s_own, -jnp.inf)
        logits = jnp.concatenate([s_sel.reshape(B, H, Q_CHUNK, topk * MOBA_BLOCK), s_own], axis=-1)
        p = jax.nn.softmax(logits, axis=-1).astype(v_blocks.dtype)
        p_sel = p[..., :topk * MOBA_BLOCK].reshape(B, H, Q_CHUNK, topk, MOBA_BLOCK)
        p_own = p[..., topk * MOBA_BLOCK:]
        return (jnp.einsum('bhqnj,bhqnjd->bhqd', p_sel, v_sel)
                + jnp.einsum('bhqj,bhjd->bhqd', p_own, v_own))

    out = lax.map(chunk_attend, (q_chunks, jnp.arange(n_chunks)))
    return out.transpose(1, 0, 3, 2, 4).reshape(B, S, H * Dh)

def first_inputs(seed: int = 0) -> dict:
    key = jax.random.key(seed)
    it = iter(jax.random.split(key, 64))

    def w(shape, fan_in):
        return jax.random.normal(next(it), shape, jnp.float32) * fan_in ** -0.5

    def gain(shape):
        return 1.0 + 0.01 * jax.random.normal(next(it), shape, jnp.float32)

    def bias(shape):
        return 0.01 * jax.random.normal(next(it), shape, jnp.float32)

    x = jax.random.normal(next(it), (BATCH, SEQ, D_MODEL), jnp.float32)
    mem = jax.random.normal(next(it), (BATCH, 256, D_MODEL), jnp.float32)
    offsets = jax.random.randint(next(it), (BATCH, 1), 0, 8192, dtype=jnp.int32)
    positions = (offsets + jnp.arange(SEQ, dtype=jnp.int32)[None, :]).astype(jnp.int32)
    return {
        'x': x, 'mem': mem, 'positions': positions,
        'ffn1_norm_g': gain((DEPTH, D_MODEL)),
        'ffn1_w_gate': w((DEPTH, D_MODEL, D_FF), D_MODEL),
        'ffn1_w_up': w((DEPTH, D_MODEL, D_FF), D_MODEL),
        'ffn1_w_down': w((DEPTH, D_FF, D_MODEL), D_FF),
        'mix_norm_g': gain((DEPTH, D_MODEL)),
        'mem_norm_g': gain((DEPTH, D_MODEL)),
        'w_mem_kv': w((DEPTH, D_MODEL, 2 * MEM_WIDTH), D_MODEL),
        'mem_q_norm_g': gain((DEPTH, HEAD_DIM)),
        'mem_k_norm_g': gain((DEPTH, HEAD_DIM)),
        'w_o': w((DEPTH, PRIMARY_WIDTH + MEM_WIDTH, D_MODEL), PRIMARY_WIDTH + MEM_WIDTH),
        'ffn2_norm_g': gain((DEPTH, D_MODEL)),
        'ffn2_w_gate': w((DEPTH, D_MODEL, D_FF), D_MODEL),
        'ffn2_w_up': w((DEPTH, D_MODEL, D_FF), D_MODEL),
        'ffn2_w_down': w((DEPTH, D_FF, D_MODEL), D_FF),
        'a_w_in': w((N_A_LAYERS, D_MODEL, 2 * CONV_CH + MEM_WIDTH), D_MODEL),
        'a_dw_kernel': w((N_A_LAYERS, CONV_WIDTH, 1, CONV_CH), CONV_WIDTH),
        'a_dw_bias': bias((N_A_LAYERS, CONV_CH)),
        'a_ln_g': gain((N_A_LAYERS, CONV_CH)),
        'a_ln_b': bias((N_A_LAYERS, CONV_CH)),
        'kv_norm_g': gain((D_MODEL,)),
        'w_kv': w((D_MODEL, 2 * PRIMARY_WIDTH), D_MODEL),
        'k_norm_g': gain((HEAD_DIM,)),
        'b_w_in': w((N_B_LAYERS, D_MODEL, PRIMARY_WIDTH + MEM_WIDTH), D_MODEL),
        'b_q_norm_g': gain((N_B_LAYERS, HEAD_DIM)),
    }

def first_block(x, mem, positions, ffn1_norm_g, ffn1_w_gate, ffn1_w_up, ffn1_w_down,
              mix_norm_g, mem_norm_g, w_mem_kv, mem_q_norm_g, mem_k_norm_g, w_o,
              ffn2_norm_g, ffn2_w_gate, ffn2_w_up, ffn2_w_down,
              a_w_in, a_dw_kernel, a_dw_bias, a_ln_g, a_ln_b,
              kv_norm_g, w_kv, k_norm_g, b_w_in, b_q_norm_g):
    B, S, _ = x.shape
    h = x
    shared_kv = None
    for layer in range(DEPTH):
        if layer == N_A_LAYERS:
            shared_kv = shared_moba_kv(h, positions, kv_norm_g, w_kv, k_norm_g)
        h = h + 0.5 * swiglu(rms_norm(h, ffn1_norm_g[layer]), ffn1_w_gate[layer],
                             ffn1_w_up[layer], ffn1_w_down[layer])
        hn = rms_norm(h, mix_norm_g[layer])
        if layer < N_A_LAYERS:
            u = hn @ a_w_in[layer]
            primary = conformer_conv(u[..., :2 * CONV_CH], a_dw_kernel[layer], a_dw_bias[layer],
                                     a_ln_g[layer], a_ln_b[layer])
            q_mem = u[..., 2 * CONV_CH:]
        else:
            j = layer - N_A_LAYERS
            u = hn @ b_w_in[j]
            q = rms_norm(u[..., :PRIMARY_WIDTH].reshape(B, S, B_HEADS, HEAD_DIM), b_q_norm_g[j])
            k_blocks, v_blocks, k_mean = shared_kv
            primary = moba_attention(partial_rope(q, positions), k_blocks, v_blocks, k_mean)
            q_mem = u[..., PRIMARY_WIDTH:]
        mem_out = memory_attention(q_mem, rms_norm(mem, mem_norm_g[layer]), w_mem_kv[layer],
                                   mem_q_norm_g[layer], mem_k_norm_g[layer])
        h = h + jnp.concatenate([primary, mem_out], axis=-1) @ w_o[layer]
        h = h + 0.5 * swiglu(rms_norm(h, ffn2_norm_g[layer]), ffn2_w_gate[layer],
                             ffn2_w_up[layer], ffn2_w_down[layer])
    return h


DEPTH_2 = 1

N_HEADS_A = 4
HEAD_DIM_A = 64
W_A = N_HEADS_A * 2 * HEAD_DIM_A
N_HEADS_B = 4
HEAD_DIM_B = D_MODEL // 8
W_B = N_HEADS_B * HEAD_DIM_B
CONV_W = 4
Q_BLOCK = 128
MLSTM_CHUNK = 64
N_IN = 4 * W_A + 5 * W_B + 2 * N_HEADS_B + 2 * D_MODEL


def _rmsnorm(x, g):
    xf = x.astype(jnp.float32)
    y = xf * lax.rsqrt(jnp.mean(xf * xf, axis=-1, keepdims=True) + EPS)
    return (y * g.astype(jnp.float32)).astype(x.dtype)

def _split(t, sizes):
    idx = np.cumsum(sizes)[:-1].tolist()
    return jnp.split(t, idx, axis=-1)

def _causal_conv(x, w):
    S = x.shape[1]
    xp = jnp.pad(x, ((0, 0), (CONV_W - 1, 0), (0, 0)))
    y = xp[:, 0:S] * w[0]
    for k in range(1, CONV_W):
        y = y + xp[:, k:k + S] * w[k]
    return y

def _alibi_slopes(n_heads):
    return 2.0 ** (-8.0 * jnp.arange(1, n_heads + 1, dtype=jnp.float32) / n_heads)

def _diff_attention(q, k, v, lam):
    B, S, _ = q.shape
    H, d = N_HEADS_A, HEAD_DIM_A
    qh = q.reshape(B, S, H, 2, d).transpose(0, 2, 3, 1, 4)
    kh = k.reshape(B, S, H, 2, d).transpose(0, 2, 3, 1, 4)
    vh = v.reshape(B, S, H, 2 * d).transpose(0, 2, 1, 3)
    nb = S // Q_BLOCK
    q_blocks = qh.reshape(B, H, 2, nb, Q_BLOCK, d).transpose(3, 0, 1, 2, 4, 5)
    slopes = _alibi_slopes(H)
    s_pos = jnp.arange(S)
    scale = d ** -0.5

    def block(args):
        q_blk, i = args
        t_pos = i * Q_BLOCK + jnp.arange(Q_BLOCK)
        dist = (t_pos[:, None] - s_pos[None, :]).astype(jnp.float32)
        bias = jnp.where(dist >= 0, -slopes[:, None, None] * dist, -jnp.inf)
        scores = jnp.einsum('bhcqd,bhcsd->bhcqs', q_blk, kh,
                            preferred_element_type=jnp.float32) * scale + bias[None, :, None]
        p = jax.nn.softmax(scores, axis=-1)
        p = p[:, :, 0] - lam * p[:, :, 1]
        return jnp.einsum('bhqs,bhse->bhqe', p.astype(vh.dtype), vh)

    out = lax.map(block, (q_blocks, jnp.arange(nb)))
    return out.transpose(1, 0, 3, 2, 4).reshape(B, S, H, 2 * d)

def _mlstm(q, k, v, ig, fg):
    B, S, _ = q.shape
    H, d, L = N_HEADS_B, HEAD_DIM_B, MLSTM_CHUNK
    nc = S // L

    def heads(t):
        return t.astype(jnp.float32).reshape(B, nc, L, H, d).transpose(1, 0, 3, 2, 4)

    def gates(t):
        return t.astype(jnp.float32).reshape(B, nc, L, H).transpose(1, 0, 3, 2)

    qc, kc, vc = heads(q), heads(k) * (d ** -0.5), heads(v)
    igc = gates(ig)
    lfc = jax.nn.log_sigmoid(gates(fg))
    causal = jnp.tril(jnp.ones((L, L), dtype=bool))

    def body(carry, xs):
        C, n, m = carry
        qj, kj, vj, ij, lj = xs
        b = jnp.cumsum(lj, axis=-1)
        logD = b[..., :, None] - b[..., None, :] + ij[..., None, :]
        logD = jnp.where(causal, logD, -jnp.inf)
        inter = b + m[..., None]
        m_row = jnp.maximum(inter, jnp.max(logD, axis=-1))
        Dm = jnp.exp(logD - m_row[..., None])
        w_inter = jnp.exp(inter - m_row)
        Sm = jnp.einsum('bhjd,bhsd->bhjs', qj, kj) * Dm
        num = jnp.einsum('bhjs,bhse->bhje', Sm, vj) + w_inter[..., None] * jnp.einsum('bhjd,bhde->bhje', qj, C)
        den = jnp.sum(Sm, axis=-1) + w_inter * jnp.einsum('bhjd,bhd->bhj', qj, n)
        h = num / jnp.maximum(jnp.abs(den), jnp.exp(-m_row))[..., None]
        bL = b[..., -1]
        a = bL[..., None] - b + ij
        m_new = jnp.maximum(bL + m, jnp.max(a, axis=-1))
        decay = jnp.exp(bL + m - m_new)
        wk = jnp.exp(a - m_new[..., None])
        C_new = decay[..., None, None] * C + jnp.einsum('bhs,bhsd,bhse->bhde', wk, kj, vj)
        n_new = decay[..., None] * n + jnp.einsum('bhs,bhsd->bhd', wk, kj)
        return (C_new, n_new, m_new), h

    init = (jnp.zeros((B, H, d, d), jnp.float32), jnp.zeros((B, H, d), jnp.float32),
            jnp.zeros((B, H), jnp.float32))
    _, hs = lax.scan(body, init, (qc, kc, vc, igc, lfc))
    return hs.transpose(1, 0, 3, 2, 4).reshape(B, S, H, d)

def second_inputs(seed: int = 0) -> dict:
    key = jax.random.key(seed)
    ks = jax.random.split(key, 14)
    nrm = jax.random.normal
    x = nrm(ks[0], (BATCH, SEQ, D_MODEL), jnp.float32)
    norm_pre = 1.0 + 0.05 * nrm(ks[1], (DEPTH_2, D_MODEL), jnp.float32)
    norm_post = 1.0 + 0.05 * nrm(ks[2], (DEPTH_2, D_MODEL), jnp.float32)
    w_in = nrm(ks[3], (DEPTH_2, D_MODEL, N_IN), jnp.float32) * D_MODEL ** -0.5
    b_i = 0.1 * nrm(ks[4], (DEPTH_2, N_HEADS_B), jnp.float32)
    b_f = jnp.linspace(3.0, 6.0, N_HEADS_B, dtype=jnp.float32)[None, :] + 0.01 * nrm(ks[5], (DEPTH_2, N_HEADS_B), jnp.float32)
    b_if = jnp.concatenate([b_i, b_f], axis=-1)
    conv_qk = nrm(ks[6], (DEPTH_2, CONV_W, 2 * W_B), jnp.float32) * CONV_W ** -0.5
    lambda_qk = 0.1 * nrm(ks[7], (DEPTH_2, 4, HEAD_DIM_A), jnp.float32)
    norm_a = 1.0 + 0.05 * nrm(ks[8], (DEPTH_2, W_A), jnp.float32)
    norm_b = 1.0 + 0.05 * nrm(ks[9], (DEPTH_2, W_B), jnp.float32)
    w_a = nrm(ks[10], (DEPTH_2, W_A, D_MODEL), jnp.float32) * W_A ** -0.5
    w_b = nrm(ks[11], (DEPTH_2, W_B, D_MODEL), jnp.float32) * W_B ** -0.5
    w_out = nrm(ks[12], (DEPTH_2, D_MODEL, D_MODEL), jnp.float32) * D_MODEL ** -0.5
    return {"x": x, "norm_pre": norm_pre, "norm_post": norm_post, "w_in": w_in,
            "b_if": b_if, "conv_qk": conv_qk, "lambda_qk": lambda_qk,
            "norm_a": norm_a, "norm_b": norm_b, "w_a": w_a, "w_b": w_b, "w_out": w_out}

def second_block(x, norm_pre, norm_post, w_in, b_if, conv_qk, lambda_qk, norm_a, norm_b, w_a, w_b, w_out):
    B, S, _ = x.shape
    H_A, H_B = N_HEADS_A, N_HEADS_B
    sizes = [W_A, W_A, W_A, W_A, W_B, W_B, W_B, W_B, W_B, H_B, H_B, D_MODEL, D_MODEL]
    for l in range(DEPTH_2):
        h = _rmsnorm(x, norm_pre[l])
        proj = jnp.einsum('bsd,dn->bsn', h, w_in[l])
        qa, ka, va, za, qb, kb, vb, ob, zb, igb, fgb, ga, gb = _split(proj, sizes)

        lam_init = 0.8 - 0.6 * math.exp(-0.3 * l)
        lq = lambda_qk[l].astype(jnp.float32)
        lam = jnp.exp(jnp.sum(lq[0] * lq[1])) - jnp.exp(jnp.sum(lq[2] * lq[3])) + lam_init
        oa = _diff_attention(qa, ka, va, lam)
        oa = _rmsnorm(oa, norm_a[l].reshape(H_A, 2 * HEAD_DIM_A)) * (1.0 - lam_init)
        ya = oa.reshape(B, S, W_A) * jax.nn.silu(za)

        qk = jax.nn.silu(_causal_conv(jnp.concatenate([qb, kb], axis=-1), conv_qk[l]))
        qb_c, kb_c = qk[..., :W_B], qk[..., W_B:]
        ig = igb + b_if[l, :H_B]
        fg = fgb + b_if[l, H_B:]
        hb = _mlstm(qb_c, kb_c, vb, ig, fg)
        hb = jax.nn.sigmoid(ob.astype(jnp.float32)).reshape(B, S, H_B, HEAD_DIM_B) * hb
        hb = _rmsnorm(hb, norm_b[l].reshape(H_B, HEAD_DIM_B)).astype(x.dtype)
        yb = hb.reshape(B, S, W_B) * jax.nn.silu(zb)

        merged = (jax.nn.sigmoid(ga) * jnp.einsum('bsw,wd->bsd', ya, w_a[l])
                  + jax.nn.sigmoid(gb) * jnp.einsum('bsw,wd->bsd', yb, w_b[l]))
        out = jnp.einsum('bsd,de->bse', merged, w_out[l])
        x = x + _rmsnorm(out, norm_post[l])
    return x


def setup_inputs(seed=0):
    out = dict(first_inputs(seed))
    for name, value in second_inputs(seed + 1).items():
        if name != "x":
            out[name + "_2"] = value
    return out


def reference(
    x, mem, positions, ffn1_norm_g, ffn1_w_gate, ffn1_w_up, ffn1_w_down, mix_norm_g, mem_norm_g,
    w_mem_kv, mem_q_norm_g, mem_k_norm_g, w_o, ffn2_norm_g, ffn2_w_gate, ffn2_w_up, ffn2_w_down,
    a_w_in, a_dw_kernel, a_dw_bias, a_ln_g, a_ln_b, kv_norm_g, w_kv, k_norm_g, b_w_in,
    b_q_norm_g, norm_pre_2, norm_post_2, w_in_2, b_if_2, conv_qk_2, lambda_qk_2, norm_a_2,
    norm_b_2, w_a_2, w_b_2, w_out_2,
):
    x = first_block(
        x, mem, positions, ffn1_norm_g, ffn1_w_gate, ffn1_w_up, ffn1_w_down, mix_norm_g,
        mem_norm_g, w_mem_kv, mem_q_norm_g, mem_k_norm_g, w_o, ffn2_norm_g, ffn2_w_gate,
        ffn2_w_up, ffn2_w_down, a_w_in, a_dw_kernel, a_dw_bias, a_ln_g, a_ln_b, kv_norm_g, w_kv,
        k_norm_g, b_w_in, b_q_norm_g,
    )
    return second_block(
        x, norm_pre_2, norm_post_2, w_in_2, b_if_2, conv_qk_2, lambda_qk_2, norm_a_2, norm_b_2,
        w_a_2, w_b_2, w_out_2,
    )


_drawn_inputs = setup_inputs


def setup_inputs(seed=0):
    import zlib

    import numpy as np

    out = dict(_drawn_inputs(seed))
    spreads = {}
    factors = {'ffn1_norm_g': 7.608,
     'mix_norm_g': 7.482,
     'mem_norm_g': 8.0,
     'mem_q_norm_g': 8.0,
     'mem_k_norm_g': 8.0,
     'ffn2_norm_g': 8.0,
     'a_ln_g': 48.816,
     'a_ln_b': 41.936,
     'kv_norm_g': 35.354,
     'k_norm_g': 35.449,
     'b_q_norm_g': 40.296,
     'norm_a_2': 197.76,
     'a_dw_bias': 8.0,
     'norm_pre_2': 8.0,
     'norm_post_2': 64.0,
     'b_if_2': 8.0,
     'conv_qk_2': 56.433,
     'lambda_qk_2': 8.0,
     'norm_b_2': 64.0,
     'w_a_2': 2.699,
     'w_b_2': 6.522}
    for name, (base, spread) in spreads.items():
        noise = np.random.default_rng([zlib.crc32(name.encode()), seed]).standard_normal(out[name].shape)
        drawn = base * np.exp(spread * noise) if base else spread * noise
        out[name] = __import__('jax').numpy.asarray(drawn.astype(out[name].dtype))
    for name, factor in factors.items():
        out[name] = (out[name] * factor).astype(out[name].dtype)
    return out
```

```python
from contextlib import ExitStack

import concourse.bass as bass
from concourse import mybir

F32 = mybir.dt.float32
F32R = mybir.dt.float32r
BF16 = mybir.dt.bfloat16
I32 = mybir.dt.int32
ALU = mybir.AluOpType
ACT = mybir.ActivationFunctionType
AX = mybir.AxisListType.X

D = 1024
S = 256
FF = 2816
NEG = -1.0e30
EPS = 1e-6
SLOT = 1024
RAW, SPLIT, AHEAD = 6, 4, 3


def wide(ap, axis, n):
    v = ap.unsqueeze(axis)
    shape = list(v.shape)
    shape[axis] = n
    return v.broadcast_to(shape)


def rows128(row):
    return row.partition_broadcast(128)


class Program:

    def __init__(self, nc, ctx):
        self.nc, self.ctx = nc, ctx
        self.engines = {"pe": nc.tensor, "act": nc.scalar, "dve": nc.vector, "pool": nc.gpsimd, "sp": nc.sync}
        self.sems, self.counts = {}, {}
        self.seen = {e: {} for e in self.engines}

    def sem(self, name):
        if name not in self.sems:
            self.sems[name] = self.ctx.enter_context(self.nc.semaphore(name))
            self.counts[name] = 0
        return self.sems[name]

    def op(self, eng, fn, *waits, sem=None, by=1):
        self.wait(eng, *waits)
        name = f"{eng}_{sem}" if sem else f"{eng}_done"
        s = self.sem(name)
        self.counts[name] += by
        fn().then_inc(s, by)
        return (name, self.counts[name])

    def quiet(self, eng, fn, *waits):
        self.wait(eng, *waits)
        fn()

    def wait(self, eng, *waits):
        for w in waits:
            if w is None:
                continue
            name, n = w
            if self.seen[eng].get(name, 0) >= n:
                continue
            self.seen[eng][name] = n
            s = self.sems[name]
            self.engines[eng].wait_ge(s, n)


def program(nc, A, out, dbg=None):
    with ExitStack() as ctx:
        build(nc, ctx, A, out, dbg or {})


def build(nc, ctx, A, out, dbg):
    P = Program(nc, ctx)
    pe, act, dve, pool = nc.tensor, nc.scalar, nc.vector, nc.gpsimd

    def sb(name, shape, dt=F32, c=ctx):
        return c.enter_context(nc.sbuf_tensor(name, shape, dt))

    psum = ctx.enter_context(nc.psum_tensor("psum", [128, 8, 512], F32))
    bank = [psum[:, i, :] for i in range(8)]
    free = [[] for _ in range(8)]

    def V(fn, *w, sem=None):
        return P.op("dve", fn, *w, sem=sem)

    def C(fn, *w, sem=None):
        return P.op("act", fn, *w, sem=sem)

    def G(fn, *w, sem=None):
        return P.op("pool", fn, *w, sem=sem)

    def T(fn, *w, sem=None):
        return P.op("pe", fn, *w, sem=sem)

    def MM(o, l, r, start, stop, *w):
        P.quiet("pe", lambda: pe.matmul(o, l, r, start=start, stop=stop, skip_group_check=True), *w)

    def MMi(o, l, r, start, stop, *w):
        return T(lambda: pe.matmul(o, l, r, start=start, stop=stop, skip_group_check=True), *w)

    def take(b):
        P.wait("pe", *free[b])
        free[b] = []

    raw = sb("raw", [128, RAW, SLOT])
    whi = sb("whi", [128, SPLIT, SLOT], F32R)
    wlo = sb("wlo", [128, SPLIT, SLOT], F32R)
    hx = sb("hx", [128, 2, D])
    xg = sb("xg", [128, 2, D])
    xh = [sb(f"xh{i}", [128, 8, S], F32R) for i in range(2)]
    xl = [sb(f"xl{i}", [128, 8, S], F32R) for i in range(2)]
    gain = sb("gain", [128, 2, D])
    ident = sb("ident", [128, 128])
    ones = sb("ones", [128, 128])
    ln1 = sb("ln1", [128, 128])
    upper = sb("upper", [128, 128])
    identb = sb("identb", [128, 128], BF16)
    maskb = sb("maskb", [128, 128], BF16)
    alib = sb("alib", [128, 2, 4, S], BF16)
    mhalf = sb("mhalf", [128, 16])
    hg = sb("hg", [128, 6, 64])
    small = sb("small", [128, 320])
    kTm = [sb(f"kTm{i}", [128, 2, S]) for i in range(2)]
    mkv = [sb(f"mkv{i}", [128, 2, 512]) for i in range(2)]

    plan = []

    def slots_A(w, c0, nc_=256):
        for k in range(0, 8, 4):
            plan.append((w, k, 4, c0, nc_))

    def slots_B(w, K, c0, n):
        kk = SLOT // n
        for k in range(0, K, kk):
            plan.append((w, k, kk, c0, n))

    state = {"dma": 0, "split": 0, "used": 0}
    lo_done, hi_done, pe_done = [], [], []

    def view(t, j, nk, n):
        return t[:, j, 0:nk * n].rearrange("p (k n) -> p k n", k=nk)

    def split_to(i):
        while state["split"] <= min(i, len(plan) - 1):
            j = state["split"]
            w, k0, nk, c0, n = plan[j]
            if j >= RAW:
                P.wait("sp", lo_done[j - RAW])
            src = w[k0 * 128:(k0 + nk) * 128, c0:c0 + n].rearrange("(k p) n -> p k n", p=128)
            dst = view(raw, j % RAW, nk, n)
            t = P.op("sp", lambda d=dst, s=src: nc.sync.dma_start(d, s), sem=f"w{j % RAW}", by=16)
            r = raw[:, j % RAW, 0:nk * n]
            h = whi[:, j % SPLIT, 0:nk * n]
            lo = wlo[:, j % SPLIT, 0:nk * n]
            before = pe_done[j - SPLIT] if j >= SPLIT else None
            th = C(lambda h=h, r=r: act.copy(h, r), t, before, sem="hi")
            tl = V(lambda h=h, r=r, lo=lo: dve.tensor_tensor(lo, r, h.bitcast(F32), ALU.subtract), th, before, sem="lo")
            hi_done.append(th)
            lo_done.append(tl)
            state["split"] += 1

    class Slot:
        pass

    def next_slot(key):
        i = state["used"]
        assert plan[i][1:] == key, (plan[i], key)
        split_to(i + AHEAD)
        s = Slot()
        s.hi = view(whi, i % SPLIT, key[1], key[3])
        s.lo = view(wlo, i % SPLIT, key[1], key[3])
        s.th, s.tl = hi_done[i], lo_done[i]
        state["used"] += 1
        return s

    def lin_A(x, w, c0, b, tx):
        take(b)
        P.wait("pe", *tx)
        for k0 in range(0, 8, 4):
            s = next_slot((k0, 4, c0, 256))
            for k in range(4):
                for j in range(2):
                    o = bank[b][:, j * 256:(j + 1) * 256]
                    hi = s.hi[:, k, j * 128:(j + 1) * 128]
                    lo = s.lo[:, k, j * 128:(j + 1) * 128]
                    kc = k0 + k
                    first = kc == 0 and j == 0
                    last = kc == 7 and j == 1
                    MM(o, hi, x[0][:, kc, :], first, False, s.th)
                    MM(o, hi, x[1][:, kc, :], False, False)
                    P.wait("pe", s.tl)
                    if k == 3 and j == 1:
                        t = T(lambda o=o, lo=lo, r=x[0][:, kc, :], last=last: pe.matmul(
                            o, lo, r, start=False, stop=last, skip_group_check=True), sem="w")
                    else:
                        MM(o, lo, x[0][:, kc, :], False, last)
            pe_done.append(t)
        return t

    def lin_B(x, w, K, c0, n, banks, tx):
        kk = SLOT // n if n >= 64 else K
        for tt in range(2):
            for b in banks[tt]:
                take(b)
        P.wait("pe", *tx)
        for k0 in range(0, K, kk):
            s = next_slot((k0, kk, c0, n))
            P.wait("pe", s.th)
            for k in range(kk):
                kc = k0 + k
                for tt in range(2):
                    jobs = []
                    for xi, wi in ((0, 0), (1, 0), (0, 1)):
                        for j, b in enumerate(banks[tt]):
                            jobs.append((xi, wi, j, b))
                    for i, (xi, wi, j, b) in enumerate(jobs):
                        w0, w1 = j * 512, min(n, (j + 1) * 512)
                        o = bank[b][:, 0:w1 - w0]
                        l = x[xi][:, kc, tt * 128:(tt + 1) * 128]
                        r = (s.lo if wi else s.hi)[:, k, w0:w1]
                        st = kc == 0 and xi == 0 and wi == 0
                        sp_ = kc == K - 1 and wi == 1
                        if wi:
                            P.wait("pe", s.tl)
                        if k == kk - 1 and tt == 1 and i == len(jobs) - 1:
                            t = T(lambda o=o, l=l, r=r, sp_=sp_: pe.matmul(
                                o, l, r, start=False, stop=sp_, skip_group_check=True), sem="w")
                        else:
                            MM(o, l, r, st, sp_)
            pe_done.append(t)
            yield t

    def run(g):
        t = None
        for t in g:
            pass
        return t

    def load(dst, src, *w, slow=False):
        n = state.setdefault("loads", 0)
        state["loads"] += 1
        return P.op("sp", lambda: nc.sync.dma_start(dst, src, allow_slow_non_contiguous=slow), *w, sem=f"l{n}", by=16)

    gain_free = [None, None]

    def load_gain(src, n=D):
        i = state.setdefault("gains", 0)
        state["gains"] += 1
        src = rows128(src)
        t = P.op("act", lambda: nc.scalar.dma_start(gain[:, i % 2, 0:n], src), gain_free[i % 2], sem=f"g{i % 2}", by=16)
        return gain[:, i % 2, 0:n], t, i % 2

    t = G(lambda: pool.memset(ident[:], 0.0))
    t_ident = G(lambda: pool.affine_select(out=ident[:], in_=ident[:], compare_op=ALU.not_equal, fill=1.0,
                                           base=0, pattern=[[-1, 128]], channel_multiplier=1), t)
    t = G(lambda: pool.memset(ones[:], 1.0))
    t_ones = t
    t_ln1 = G(lambda: pool.memset(ln1[:], 1.0 / 768))
    t_upper = G(lambda: pool.affine_select(out=upper[:], in_=ones[:], compare_op=ALU.is_ge, fill=0.0,
                                           base=0, pattern=[[1, 128]], channel_multiplier=-1), t)
    t_identb = G(lambda: pool.tensor_copy(identb[:], ident[:]), t_ident)
    t = G(lambda: pool.memset(maskb[:], 0.0))
    t_mask = G(lambda: pool.affine_select(out=maskb[:], in_=maskb[:], compare_op=ALU.is_ge, fill=NEG,
                                          base=0, pattern=[[-1, 128]], channel_multiplier=1), t)
    t_half = G(lambda: pool.memset(mhalf[:], -0.5))
    t = None
    for tt in range(2):
        ti = G(lambda tt=tt: pool.iota(kTm[0][:, 0, :], pattern=[[1, S]], base=-128 * tt, channel_multiplier=-1,
                                       allow_small_or_imprecise_dtypes=True), t)
        for h in range(4):
            c = 8.0 * 2.0 ** (-2 * (h + 1))
            t = G(lambda tt=tt, h=h, c=c: pool.tensor_scalar(alib[:, tt, h, :], kTm[0][:, 0, :], c, None, ALU.mult), ti)
    t_alib = G(lambda: pool.affine_select(out=alib[:, 0], in_=alib[:, 0], compare_op=ALU.is_ge, fill=NEG, base=0,
                                          pattern=[[0, 4], [-1, S]], channel_multiplier=1), t)
    t_alib = G(lambda: pool.affine_select(out=alib[:, 1], in_=alib[:, 1], compare_op=ALU.is_ge, fill=NEG, base=128,
                                          pattern=[[0, 4], [-1, S]], channel_multiplier=1), t)

    t_x = load(hx[:], A["x"][0].rearrange("(t p) d -> p t d", p=128))
    h_ready = [t_x, t_x]

    rst = {"n": 0}
    xg_free = [None, None]

    def col():
        rst["n"] += 1
        return rst["n"]

    def rstd_of(ss, rs, n, t, width=1):
        t = G(lambda: pool.tensor_scalar(rs, ss, 1.0 / n, EPS, ALU.mult, ALU.add), t)
        return G(lambda: pool.tensor_tensor(rs, rs, mhalf[:, 0:width], ALU.pow), t)


    def sumsq(src, c0, ready, tt):
        s = small[:, c0:c0 + 1]
        t = C(lambda: act.activation(xg[:, tt, :], src, ACT.Square, accum_out=s), ready, xg_free[tt])
        xg_free[tt] = t
        return rstd_of(s, small[:, c0 + 1:c0 + 2], D, t)


    def to_T(src_of, n_chunks, dst, d0, ready, banks, tt, skip=0):
        res = []
        for i, c in enumerate(range(0, n_chunks, 4)):
            m = min(4, n_chunks - c)
            b = banks[i % len(banks)]
            take(b)
            P.wait("pe", t_ident, *ready)
            for j in range(m):
                f = lambda b=b, j=j, c=c: pe.transpose(bank[b][:, j * 128:(j + 1) * 128], src_of(c + j), ident[:])
                if j == m - 1:
                    t = T(f)
                else:
                    P.quiet("pe", f)
            src = bank[b][:, 0:m * 128].rearrange("p (k n) -> p k n", k=m)
            oh = dst[0][:, d0 + c:d0 + c + m, tt * 128:(tt + 1) * 128]
            ol = dst[1][:, d0 + c:d0 + c + m, tt * 128:(tt + 1) * 128]
            th = C(lambda oh=oh, src=src: act.copy(oh, src), t)
            tl = V(lambda oh=oh, ol=ol, src=src: dve.tensor_tensor(ol, src, oh.bitcast(F32), ALU.subtract), th)
            free[b] = [th, tl]
            res += [th, tl]
        last_T[0] = t
        return res

    last_T = [None]

    def normed(src, ready, g, tg, gi, dst, banks, rs, free_dst=()):
        P.wait("act", *free_dst)
        P.wait("dve", *free_dst)
        res = []
        for tt in range(2):
            c0, t = rs[tt]
            t = V(lambda tt=tt, c0=c0: dve.scalar_tensor_tensor(
                out=xg[:, tt, :], in0=src[:, tt, :], scalar=small[:, c0 + 1:c0 + 2], in1=g,
                op0=ALU.mult, op1=ALU.mult), t, tg, ready[tt], xg_free[tt])
            gain_free[gi] = t
            res += to_T(lambda c, tt=tt: xg[:, tt, c * 128:(c + 1) * 128], 8, dst, 0, [t], banks[tt], tt)
            xg_free[tt] = last_T[0]
        return res

    def stats(src, ready):
        r = []
        for tt in range(2):
            c0 = 2 * (col() % 16)
            r.append((c0, sumsq(src[:, tt, :], c0, ready[tt], tt)))
        return r

    def ffn(i, wg, wu, wd, x, tx, gT):
        gh, gl, sg, pr = gT
        tg = []
        sgf = [[None], [None]]
        for p in range(FF // 256):
            bg, bu = (0, 1) if p % 2 == 0 else (2, 3)
            lin_A(x, wg, p * 256, bg, tx)
            t1 = pe_done[-1]
            lin_A(x, wu, p * 256, bu, tx)
            t2 = pe_done[-1]
            s, q = sg[:, p % 2, :], pr[:, p % 2, :]
            ts = C(lambda s=s, bg=bg: act.activation(s, bank[bg][:], ACT.Silu), t1, *sgf[p % 2])
            free[bg] = [ts]
            tm = V(lambda s=s, q=q, bu=bu: dve.tensor_tensor(q, s, bank[bu][:], ALU.mult), ts, t2, *sgf[p % 2])
            free[bu] = [tm]
            oh = gh[:, 2 * p:2 * p + 2, :].rearrange("p a b -> p (a b)")
            ol = gl[:, 2 * p:2 * p + 2, :].rearrange("p a b -> p (a b)")
            th = C(lambda oh=oh, q=q: act.copy(oh, q), tm)
            tl = V(lambda oh=oh, ol=ol, q=q: dve.tensor_tensor(ol, q, oh.bitcast(F32), ALU.subtract), th)
            sgf[p % 2] = [th, tl]
            tg += [th, tl]
        banks = [[4, 5], [6, 7]]
        x_last = pe_done[-1]
        t = run(lin_B((gh, gl), wd, FF // 128, 0, D, banks, [tg[-1], tg[-2]]))
        add_to_h(banks, 0.5, t)
        return x_last

    def add_to_h(banks, scale, t):
        for tt in range(2):
            for j, b in enumerate(banks[tt]):
                h = hx[:, tt, j * 512:(j + 1) * 512]
                u = V(lambda h=h, b=b: dve.scalar_tensor_tensor(out=h, in0=bank[b][:], scalar=scale, in1=h,
                                                                op0=ALU.mult, op1=ALU.add), t, h_ready[tt])
                free[b] = [u]
            h_ready[tt] = u

    def head_rms(src, nh, c0, g, tg, dst, ready, sq):
        ss = small[:, c0:c0 + nh]
        rs = small[:, c0 + 16:c0 + 16 + nh]
        v = src.rearrange("p (h d) -> p h d", d=64)
        o = dst.rearrange("p (h d) -> p h d", d=64)
        q = sq.rearrange("p (h d) -> p h d", d=64)
        t = V(lambda: dve.tensor_tensor(q, v, v, ALU.mult), *ready)
        t = V(lambda: dve.reduce_sum(ss, q, AX), t)
        t = rstd_of(ss, rs, 64, t, nh)
        t = V(lambda: dve.tensor_tensor(o, v, wide(rs, 2, 64), ALU.mult), t)
        return V(lambda: dve.tensor_tensor(o, o, wide(g, 1, nh), ALU.mult), t, tg)

    def plain_T(src_of, n, dst_of, ready, b, eng="act"):
        take(b)
        P.wait("pe", t_ident, *ready)
        for j in range(n):
            f = lambda j=j: pe.transpose(bank[b][:, j * 128:(j + 1) * 128], src_of(j), ident[:])
            if j == n - 1:
                t = T(f)
            else:
                P.quiet("pe", f)
        src = bank[b][:, 0:n * 128].rearrange("p (k n) -> p k n", k=n)
        if eng == "act":
            t = C(lambda: act.copy(dst_of, src), t)
        else:
            t = V(lambda: dve.tensor_copy(dst_of, src), t)
        free[b] = [t]
        return t

    def attend(jobs, pbuf, ptbuf, att, sbase):
        n = len(jobs)
        st = [dict() for _ in jobs]
        pf, ptf = [None] * 3, [None] * 2
        done = []

        def scores(i):
            tt, causal, heads, oc, ready = jobs[i]
            kw = 128 * (tt + 1) if causal else 256
            b = 2 * (i % 2)
            take(b)
            take(b + 1)
            P.wait("pe", *ready)
            ps = psum[:, b:b + 2, 0:kw]
            for h, (qT, kT, vv) in enumerate(heads):
                t = MMi(ps[:, h, :], qT(tt), kT(kw), True, not causal)
            if causal:
                for h in range(2):
                    t = MMi(ps[:, h, kw - 128:kw], identb[:], maskb[:], False, True, t_identb, t_mask)
            c = sbase + 8 * (i % 3)
            mx, nb, sm, rc = (small[:, c + 2 * q:c + 2 * q + 2] for q in range(4))
            t = V(lambda: dve.reduce_max(mx, ps, AX), t, st[i - 3]["fin"] if i >= 3 else None)
            t = V(lambda: dve.tensor_scalar(nb, mx, -0.125, None, ALU.mult), t)
            p = pbuf[:, i % 3, 0:2 * kw].rearrange("p (h k) -> p h k", h=2)
            P.wait("act", pf[i % 3])
            for h in range(2):
                te = C(lambda h=h: act.activation(p[:, h, :], ps[:, h, :], ACT.Exp, bias=nb[:, h:h + 1], scale=0.125,
                                                  accum_out=sm[:, h:h + 1]), t)
            free[b] = free[b + 1] = [te]
            st[i].update(p=p, kw=kw, sm=sm, rc=rc, te=te)

        def turn(i):
            s = st[i]
            nk = s["kw"] // 128
            b = 4 + i % 2
            take(b)
            P.wait("pe", s["te"], t_ident)
            m = 2 * nk
            for j in range(m):
                f = lambda j=j: pe.transpose(bank[b][:, j * 128:(j + 1) * 128],
                                             s["p"][:, j // nk, (j % nk) * 128:(j % nk + 1) * 128], ident[:])
                if j == m - 1:
                    t = T(f)
                else:
                    P.quiet("pe", f)
            pf[i % 3] = t
            dst = ptbuf[:, i % 2, 0:m * 128]
            s["tr"] = V(lambda: dve.reciprocal(s["rc"], s["sm"]), s["te"])
            eng = V if i % 2 else C
            if i % 2:
                t = V(lambda: dve.tensor_copy(dst, bank[b][:, 0:m * 128]), t, ptf[i % 2])
            else:
                t = C(lambda: act.copy(dst, bank[b][:, 0:m * 128]), t, ptf[i % 2])
            free[b] = [t]
            s["pt"] = t

        def values(i):
            tt, causal, heads, oc, ready = jobs[i]
            s = st[i]
            nk = s["kw"] // 128
            b = 6 + i % 2
            take(b)
            P.wait("pe", s["pt"])
            for h, (qT, kT, vv) in enumerate(heads):
                for k in range(nk):
                    l = ptbuf[:, i % 2, (h * nk + k) * 128:(h * nk + k + 1) * 128]
                    f = lambda l=l, h=h, k=k, vv=vv: pe.matmul(bank[b][:, h * 64:(h + 1) * 64], l, vv(k),
                                                               start=k == 0, stop=k == nk - 1,
                                                               skip_group_check=True)
                    if h == 1 and k == nk - 1:
                        t = T(f)
                    else:
                        P.quiet("pe", f)
            ptf[i % 2] = t
            o = att[:, tt, oc:oc + 128].rearrange("p (h d) -> p h d", h=2)
            src = bank[b][:, 0:128].rearrange("p (h d) -> p h d", h=2)
            t = V(lambda: dve.tensor_tensor(o, src, wide(s["rc"], 2, 64), ALU.mult), t, s["tr"])
            free[b] = [t]
            s["fin"] = t
            done.append(t)

        for i in range(n + 2):
            if i < n:
                scores(i)
            if 0 <= i - 1 < n:
                turn(i - 1)
            if 0 <= i - 2 < n:
                values(i - 2)
            yield done[-1] if done else None

    def dump(name, ap, *w):
        if name in dbg:
            t = load(dbg[name], ap, *w)
            dumps.append(t)

    dumps = []
    DA = {k: A[k] for k in A}

    def plan_ffn(which, l):
        for p in range(FF // 256):
            slots_A(DA[which + "_w_gate"][l], p * 256)
            slots_A(DA[which + "_w_up"][l], p * 256)
        slots_B(DA[which + "_w_down"][l], 22, 0, D)

    ain = DA["a_w_in"][0]
    win = DA["w_in_2"][0]
    plan_ffn("ffn1", 0)
    for p in range(3):
        slots_A(ain, p * 256)
        slots_A(ain, 768 + p * 256)
    slots_B(ain, 8, 1536, 256)
    for l in range(2):
        slots_B(DA["w_mem_kv"][l], 8, 0, 512)
    slots_B(DA["w_o"][0], 8, 0, D)
    plan_ffn("ffn2", 0)
    for c in range(3):
        slots_B(DA["w_kv"], 8, c * 512, 512)
    plan_ffn("ffn1", 1)
    slots_B(DA["b_w_in"][0], 8, 0, D)
    slots_B(DA["w_o"][1], 8, 0, D)
    plan_ffn("ffn2", 1)
    for c in range(4):
        slots_A(win, 2048 + c * 256)
    plan.append((win, 0, 8, 4608, 8))
    for c in range(4):
        slots_A(win, c * 256)
    slots_B(win, 8, 3072, 512)
    slots_B(win, 8, 1024, 512)
    for c0 in (1536, 3584, 4096):
        slots_B(win, 8, c0, 512)
    slots_B(win, 8, 4616, D)
    slots_B(win, 8, 5640, D)
    slots_B(DA["w_a_2"][0], 4, 0, D)
    slots_B(DA["w_b_2"][0], 4, 0, D)
    slots_B(DA["w_out_2"][0], 8, 0, D)

    BK = [[4, 5], [6, 7]]
    LOWB = [[0, 1], [2, 3]]

    split_to(3)
    thg = []
    for i, nm in enumerate(("mem_q_norm_g", "mem_k_norm_g")):
        for l in range(2):
            thg.append(load(hg[:, 2 * i + l, :], rows128(A[nm][l])))
    thg.append(load(hg[:, 4, :], rows128(A["k_norm_g"])))
    thg.append(load(hg[:, 5, :], rows128(A["b_q_norm_g"][0])))

    gphase = ExitStack()

    def ffn_mem(tag):
        c = ExitStack()
        gh = sb(f"gh{tag}", [128, 22, S], F32R, c)
        gl = sb(f"gl{tag}", [128, 22, S], F32R, c)
        sg = sb(f"sg{tag}", [128, 2, 512], F32, c)
        pr = sb(f"pr{tag}", [128, 2, 512], F32, c)
        return c, (gh, gl, sg, pr)

    def run_ffn(which, l, x, tx):
        c, g = ffn_mem(f"{which}{l}")
        r = ffn(0, DA[which + "_w_gate"][l], DA[which + "_w_up"][l], DA[which + "_w_down"][l], x, tx, g)
        c.close()
        return r

    X0, X1 = (xh[0], xl[0]), (xh[1], xl[1])

    g, tg, gi = load_gain(A["ffn1_norm_g"][0])
    rs = stats(hx, h_ready)
    tx = normed(hx, h_ready, g, tg, gi, X0, LOWB, rs)
    x0_last = run_ffn("ffn1", 0, X0, tx)
    dump("h1", hx[:], *h_ready)

    g, tg, gi = load_gain(A["mix_norm_g"][0])
    rs = stats(hx, h_ready)
    tx = normed(hx, h_ready, g, tg, gi, X0, LOWB, rs, [x0_last])

    mx = ExitStack()
    hc = sb("hc", [128, 6, 30 + S], F32, mx)
    cv = sb("cv", [128, 6, S], F32, mx)
    rows = sb("rows", [34, 768], F32, mx)
    taps = sb("taps", [128, 6, 34], F32, mx)
    sg = sb("sgm", [128, 2, 512], F32, mx)
    qm = sb("qm", [128, 2, 256], F32, mx)
    sq = sb("sqm", [128, 2, 256], F32, mx)
    qTm = sb("qTm", [128, 2, S], F32, mx)
    att = sb("attm", [128, 2, 256], F32, mx)
    stat = sb("statm", [128, 4, S], F32, mx)
    pbuf = sb("pbm", [128, 3, 512], F32, mx)
    ptbuf = sb("ptm", [128, 2, 512], F32, mx)
    xs = (sb("xsh", [128, 8, S], F32R, mx), sb("xsl", [128, 8, S], F32R, mx))
    ffn_last = pe_done[-1]
    P.wait("sp", ffn_last)
    mem = sb("memt", [128, 2, D], F32, mx)
    t_mem = load(mem[:], A["mem"][0].rearrange("(t p) d -> p t d", p=128))
    tr_ = [load(rows[0:31, :], A["a_dw_kernel"][0].rearrange("k a c -> k (a c)")),
           load(rows[31:32, :], A["a_dw_bias"]), load(rows[32:33, :], A["a_ln_g"]), load(rows[33:34, :], A["a_ln_b"])]
    tz = V(lambda: dve.memset(hc[:, :, 0:30], 0.0), ffn_last)
    take(4)
    P.wait("pe", t_ident, *tr_)
    for c in range(6):
        f = lambda c=c: pe.transpose(bank[4][:, c * 34:(c + 1) * 34], rows[:, c * 128:(c + 1) * 128], ident[0:34, 0:34])
        if c < 5:
            P.quiet("pe", f)
        else:
            t = T(f)
    t_taps = V(lambda: dve.tensor_copy(taps[:].rearrange("p a b -> p (a b)"), bank[4][:, 0:204]), t)
    free[4] = [t_taps]

    tc = []
    sgf = [None, None]
    hcs = []
    for p in range(3):
        ba, bg = (0, 1) if p % 2 == 0 else (2, 3)
        lin_A(X0, ain, p * 256, ba, tx)
        t1 = pe_done[-1]
        lin_A(X0, ain, 768 + p * 256, bg, tx)
        t2 = pe_done[-1]
        ts = C(lambda p=p, bg=bg: act.activation(sg[:, p % 2, :], bank[bg][:], ACT.Sigmoid), t2, sgf[p % 2])
        free[bg] = [ts]
        tm = V(lambda p=p, ba=ba: dve.tensor_tensor(
            hc[:, 2 * p:2 * p + 2, 30:30 + S], sg[:, p % 2, :].rearrange("p (a b) -> p a b", a=2),
            bank[ba][:].rearrange("p (a b) -> p a b", a=2), ALU.mult), ts, t1)
        free[ba] = [tm]
        sgf[p % 2] = tm
        hcs.append(tm)
    tq = run(lin_B(X0, ain, 8, 1536, 256, [[5], [6]], tx))
    x0_last = tq
    tqs = []
    for tt in range(2):
        t = C(lambda tt=tt: act.copy(qm[:, tt, :], bank[5 + tt][:, 0:256]), tq)
        free[5 + tt] = [t]
        tqs.append(t)

    def conv_tile(c, ready):
        for k in range(31):
            if k == 0:
                t = V(lambda: dve.tensor_scalar(cv[:, c, :], hc[:, c, 0:S], taps[:, c, 0:1], taps[:, c, 31:32],
                                                ALU.mult, ALU.add), ready, t_taps, tz)
            else:
                t = V(lambda k=k: dve.scalar_tensor_tensor(out=cv[:, c, :], in0=hc[:, c, k:k + S],
                                                           scalar=taps[:, c, k:k + 1], in1=cv[:, c, :],
                                                           op0=ALU.mult, op1=ALU.add), t)
            yield t

    def conv_all():
        for c in range(6):
            for t in conv_tile(c, hcs[c // 2]):
                yield t
            tcv.append(t)

    tcv = []
    cg = conv_all()

    def some(gen, n):
        for _ in range(n):
            next(gen, None)

    rsm = stats(mem, [t_mem, t_mem])
    tmk, tmv = [], []
    for l in range(2):
        g, tg, gi = load_gain(A["mem_norm_g"][l])
        dst = X1 if l == 0 else X0
        tx = normed(mem, [t_mem, t_mem], g, tg, gi, dst, LOWB, rsm, [x0_last] if l else [])
        some(cg, 30)
        bk = [[4], [5]] if l == 0 else [[6], [7]]
        gg = lin_B(dst, DA["w_mem_kv"][l], 8, 0, 512, bk, tx)
        for t in gg:
            some(cg, 8)
        tl = []
        for tt in range(2):
            b = bk[tt][0]
            t = C(lambda tt=tt, b=b, l=l: act.copy(mkv[l][:, tt, :], bank[b][:]), t)
            free[b] = [t]
            tl.append(t)
            t = head_rms(mkv[l][:, tt, 0:256], 4, 32 + 64 * tt, hg[:, 2 + l, :], thg[2 + l], mkv[l][:, tt, 0:256],
                         [t], sq[:, tt, :])
            tmk.append(plain_T(lambda j, tt=tt, l=l: mkv[l][:, tt, j * 128:(j + 1) * 128], 2,
                               kTm[l][:, :, tt * 128:(tt + 1) * 128], [t], tt))
        tmv.append(tl)
        x1_last = pe_done[-1]
        if l == 1:
            x0_last = pe_done[-1]

    def mem_jobs(l, qT, ready, oc0):
        jobs = []
        for tt in range(2):
            for c in range(2):
                heads = []
                for h in range(2):
                    heads.append((lambda tt, c=c, h=h: qT[h * 64:(h + 1) * 64, c, tt * 128:(tt + 1) * 128],
                                  lambda kw, c=c, h=h: kTm[l][h * 64:(h + 1) * 64, c, :],
                                  lambda k, c=c, h=h: mkv[l][:, k, 256 + (2 * c + h) * 64:256 + (2 * c + h + 1) * 64]))
                jobs.append((tt, False, heads, oc0 + c * 128, ready + tmk + tmv[l]))
        return jobs

    tqT = []
    for tt in range(2):
        t = head_rms(qm[:, tt, :], 4, 32 + 64 * tt, hg[:, 0, :], thg[0], qm[:, tt, :], [tqs[tt]], sq[:, tt, :])
        tqT.append(plain_T(lambda j, tt=tt: qm[:, tt, j * 128:(j + 1) * 128], 2,
                           qTm[:, :, tt * 128:(tt + 1) * 128], [t], tt))
        some(cg, 20)
    for t in attend(mem_jobs(0, qTm, tqT, 0), pbuf, ptbuf, att, 160):
        some(cg, 10)
    tatt = t
    txs = []
    for tt in range(2):
        txs += to_T(lambda c, tt=tt: att[:, tt, c * 128:(c + 1) * 128], 2, xs, 6, [tatt], [tt], tt)
    some(cg, 500)

    cvf = cv[:].rearrange("p a b -> p (a b)")

    def over_channels(src, b):
        take(b)
        for c in range(6):
            MM(bank[b][:, 0:S], ln1[:], src[:, c, :], c == 0, c == 5, t_ln1, tcv[c])
    take(2)
    for c in range(6):
        t = MMi(bank[2][:, 0:S], ln1[:], cv[:, c, :], c == 0, c == 5, t_ln1, tcv[c])
    tm = C(lambda: act.copy(stat[:, 0, :], bank[2][:, 0:S]), t)
    free[2] = [tm]
    t = V(lambda: dve.tensor_tensor(cv[:], cv[:], wide(stat[:, 0, :], 1, 6), ALU.subtract), tm, tcv[-1])
    hcv = hc[:, :, 0:S]
    ts = C(lambda: act.activation(hcv, cv[:], ACT.Square), t)
    take(3)
    for c in range(6):
        t2 = MMi(bank[3][:, 0:S], ln1[:], hcv[:, c, :], c == 0, c == 5, ts)
    t2 = V(lambda: dve.tensor_scalar(stat[:, 1, :], bank[3][:, 0:S], EPS, None, ALU.add), t2)
    free[3] = [t2]
    t3 = C(lambda: act.activation(stat[:, 2, :], stat[:, 1, :], ACT.Sqrt), t2)
    t3 = V(lambda: dve.reciprocal(stat[:, 3, :], stat[:, 2, :]), t3)
    t3 = V(lambda: dve.tensor_tensor(stat[:, 2, :], stat[:, 3, :], stat[:, 3, :], ALU.mult), t3)
    t3 = V(lambda: dve.tensor_tensor(stat[:, 2, :], stat[:, 2, :], stat[:, 1, :], ALU.mult), t3)
    t3 = V(lambda: dve.tensor_scalar(stat[:, 2, :], stat[:, 2, :], -0.5, 1.5, ALU.mult, ALU.add), t3)
    t3 = V(lambda: dve.tensor_tensor(stat[:, 3, :], stat[:, 3, :], stat[:, 2, :], ALU.mult), t3)
    t3 = V(lambda: dve.tensor_tensor(cv[:], cv[:], wide(stat[:, 3, :], 1, 6), ALU.mult), t3)
    for c in range(6):
        t4 = C(lambda c=c: act.activation(cv[:, c, :], cv[:, c, :], ACT.Silu, bias=taps[:, c, 33:34],
                                          scale=taps[:, c, 32:33]), t3, t_taps)
        t5 = C(lambda c=c: act.copy(xs[0][:, c, :], cv[:, c, :]), t4)
        t6 = V(lambda c=c: dve.tensor_tensor(xs[1][:, c, :], cv[:, c, :], xs[0][:, c, :].bitcast(F32), ALU.subtract), t5)
        txs += [t5, t6]
    dump("prim", cv[:], t4)
    dump("mo", att[:], tatt)
    t = run(lin_B(xs, DA["w_o"][0], 8, 0, D, BK, txs))
    xs_last = t
    add_to_h(BK, 1.0, t)
    for e in ("dve", "act", "sp"):
        P.wait(e, xs_last)
    mx.close()
    dump("h2", hx[:], *h_ready)
    P.wait("act", *dumps)
    P.wait("dve", *dumps)

    g, tg, gi = load_gain(A["ffn2_norm_g"][0])
    rs = stats(hx, h_ready)
    tx = normed(hx, h_ready, g, tg, gi, X0, LOWB, rs, [x0_last])
    x0_last = run_ffn("ffn2", 0, X0, tx)
    dump("h3", hx[:], *h_ready)

    kv = ExitStack()
    kT = sb("kT", [128, 6, S], F32, kv)
    vn = sb("vn", [128, 2, 768], F32, kv)
    cs = sb("cs", [128, 2, 2, 8], F32, kv)
    tk = ExitStack()
    kn = sb("kn", [128, 2, 768], F32, tk)

    g, tg, gi = load_gain(A["kv_norm_g"])
    g2, tg2, gi2 = load_gain(A["ffn1_norm_g"][1])
    rs = stats(hx, h_ready)
    tx = normed(hx, h_ready, g, tg, gi, X1, LOWB, rs, [x1_last])
    tkv = []
    gk = lin_B(X1, DA["w_kv"], 8, 0, 512, [[4], [5]], tx)
    t = run(gk)
    for tt in range(2):
        tkv.append(C(lambda tt=tt: act.copy(kn[:, tt, 0:512], bank[4 + tt][:]), t))
        free[4 + tt] = [tkv[-1]]
    t = run(lin_B(X1, DA["w_kv"], 8, 512, 512, [[6], [7]], tx))
    for tt in range(2):
        tkv.append(V(lambda tt=tt: dve.tensor_copy(kn[:, tt, 512:768], bank[6 + tt][:, 0:256]), t))
        u = V(lambda tt=tt: dve.tensor_copy(vn[:, tt, 0:256], bank[6 + tt][:, 256:512]), t)
        free[6 + tt] = [tkv[-1], u]
    tx0 = normed(hx, h_ready, g2, tg2, gi2, X0, LOWB, rs, [x0_last])
    t = run(lin_B(X1, DA["w_kv"], 8, 1024, 512, [[4], [5]], tx))
    x1_last = t
    for tt in range(2):
        u = V(lambda tt=tt: dve.tensor_copy(vn[:, tt, 256:768], bank[4 + tt][:]), t)
        free[4 + tt] = [u]
    t_vn = u

    posi = sb("posi", [128, 2, 1], I32, tk)
    posf = sb("posf", [128, 2], F32, tk)
    freq = sb("freq", [128, 8], F32, tk)
    ang = sb("ang", [128, 2, 2, 8], F32, tk)
    rd = sb("rd", [128, 2, 2, 8], F32, tk)
    t = load(posi[:], A["positions"][0].rearrange("(t p o) -> p t o", p=128, o=1), slow=True)
    t = V(lambda: dve.tensor_copy(posf[:], posi[:, :, 0]), t)
    import numpy as np
    fr = 1.0 / (np.float32(500000.0) ** (np.arange(0, 16, 2, dtype=np.float32) / np.float32(16)))
    fr = fr.astype(np.float32)
    for i in range(8):
        tf = V(lambda i=i: dve.memset(freq[:, i:i + 1], float(fr[i])))
    for tt in range(2):
        t = V(lambda tt=tt: dve.tensor_scalar(ang[:, tt, 1, :], freq[:], posf[:, tt:tt + 1], None, ALU.mult), t, tf)
    c1, rest = 6.28125, 2 * np.pi - 6.28125
    c2 = float(np.float32(round(rest * 2 ** 19) / 2 ** 19))
    c3 = float(np.float32(rest - c2))
    magic = 12582912.0
    a1 = ang[:, :, 1, :]
    k1 = rd[:, :, 1, :]
    t = V(lambda: dve.tensor_scalar(k1, a1, float(1 / (2 * np.pi)), magic, ALU.mult, ALU.add), t)
    t = V(lambda: dve.tensor_scalar(k1, k1, -magic, None, ALU.add), t)
    for c in (c1, c2, c3):
        t = V(lambda c=c: dve.scalar_tensor_tensor(out=a1, in0=k1, scalar=-c, in1=a1, op0=ALU.mult, op1=ALU.add), t)
    a0 = ang[:, :, 0, :]
    k0 = rd[:, :, 0, :]
    t = V(lambda: dve.tensor_scalar(a0, a1, float(np.pi / 2), None, ALU.add), t)
    t = V(lambda: dve.tensor_scalar(k0, a0, float(np.pi), None, ALU.is_gt), t)
    t = V(lambda: dve.scalar_tensor_tensor(out=a0, in0=k0, scalar=-float(2 * np.pi), in1=a0, op0=ALU.mult, op1=ALU.add), t)
    t = V(lambda: dve.tensor_scalar(ang[:], ang[:], 3.1415925, -3.1415925, ALU.min, ALU.max), t)
    t_cs = C(lambda: act.activation(cs[:], ang[:], ACT.Sin), t)

    def rope(x, tt, nh, tmp, t):
        v = x.rearrange("p (h d) -> p h d", d=64)
        x1, x2 = v[:, :, 0:8], v[:, :, 8:16]
        co = wide(cs[:, tt, 0, :], 1, nh)
        si = wide(cs[:, tt, 1, :], 1, nh)
        m = [tmp[:, i, :].rearrange("p (h d) -> p h d", d=8) for i in range(4)]
        u = []
        for o, a, b in ((m[0], x1, co), (m[1], x2, si), (m[2], x2, co), (m[3], x1, si)):
            u = V(lambda o=o, a=a, b=b: dve.tensor_tensor(o, a, b, ALU.mult), t, t_cs)
        V(lambda: dve.tensor_tensor(x1, m[0], m[1], ALU.subtract), u)
        return V(lambda: dve.tensor_tensor(x2, m[2], m[3], ALU.add), u)

    rtmp = sb("rtmp", [128, 2, 4, 96], F32, tk)
    tkT = []
    sqk = sb("sqk", [128, 2, 768], F32, tk)
    for tt in range(2):
        t = head_rms(kn[:, tt, :], 12, 32 + 64 * tt, hg[:, 4, :], thg[4], kn[:, tt, :], tkv, sqk[:, tt, :])
        t = rope(kn[:, tt, :], tt, 12, rtmp[:, tt], t)
        tkT.append(plain_T(lambda j, tt=tt: kn[:, tt, j * 128:(j + 1) * 128], 4,
                           kT[:, 0:4, tt * 128:(tt + 1) * 128], [t], 4))
        tkT.append(plain_T(lambda j, tt=tt: kn[:, tt, (4 + j) * 128:(5 + j) * 128], 2,
                           kT[:, 4:6, tt * 128:(tt + 1) * 128], [t], 5))
    tk.close()
    P.wait("act", t)
    dump("kn", kn[:], t)
    dump("vn", vn[:], t_vn)

    x0_last = run_ffn("ffn1", 1, X0, tx0)
    dump("h4", hx[:], *h_ready)
    ffn_last = pe_done[-1]

    g, tg, gi = load_gain(A["mix_norm_g"][1])
    rs = stats(hx, h_ready)
    tx = normed(hx, h_ready, g, tg, gi, X0, LOWB, rs, [x0_last])
    t = run(lin_B(X0, DA["b_w_in"][0], 8, 0, D, BK, tx))
    x0_last = t
    mx = ExitStack()
    qn = sb("qn", [128, 2, D], F32, mx)
    rtmp = sb("rtmp1", [128, 2, 4, 96], F32, mx)
    sq = sb("sqq", [128, 2, D], F32, mx)
    qT = sb("qT", [128, 8, S], F32, mx)
    att = sb("att1", [128, 2, D], F32, mx)
    pbuf = sb("pb1", [128, 3, 512], F32, mx)
    ptbuf = sb("pt1", [128, 2, 512], F32, mx)
    for tt in range(2):
        u = C(lambda tt=tt: act.copy(qn[:, tt, 0:512], bank[BK[tt][0]][:]), t)
        w = V(lambda tt=tt: dve.tensor_copy(qn[:, tt, 512:1024], bank[BK[tt][1]][:]), t)
        free[BK[tt][0]], free[BK[tt][1]] = [u], [w]
        v1 = head_rms(qn[:, tt, 0:768], 12, 32 + 64 * tt, hg[:, 5, :], thg[5], qn[:, tt, 0:768], [u, w], sq[:, tt, 0:768])
        v1 = rope(qn[:, tt, 0:768], tt, 12, rtmp[:, tt], v1)
        v2 = head_rms(qn[:, tt, 768:], 4, 44 + 64 * tt, hg[:, 1, :], thg[1], qn[:, tt, 768:], [w], sq[:, tt, 768:])
        for j0 in (0, 4):
            tqT_ = plain_T(lambda j, tt=tt, j0=j0: qn[:, tt, (j0 + j) * 128:(j0 + j + 1) * 128], 4,
                           qT[:, j0:j0 + 4, tt * 128:(tt + 1) * 128], [v1, v2], tt * 2 + j0 // 4, "act")
    dump("qn", qn[:], v1, v2)
    jobs = []
    for tt in range(2):
        for c in range(6):
            heads = [(lambda tt, c=c, h=h: qT[h * 64:(h + 1) * 64, c, tt * 128:(tt + 1) * 128],
                      lambda kw, c=c, h=h: kT[h * 64:(h + 1) * 64, c, 0:kw],
                      lambda k, c=c, h=h: vn[:, k, (2 * c + h) * 64:(2 * c + h + 1) * 64]) for h in range(2)]
            jobs.append((tt, True, heads, c * 128, [tqT_, t_vn] + tkT))
        jobs += [j for j in mem_jobs(1, qT[:, 6:8, :], [tqT_], 768) if j[0] == tt]
    tatt = run(attend(jobs, pbuf, ptbuf, att, 160))
    dump("att", att[:], tatt)
    txs = []
    for tt in range(2):
        txs += to_T(lambda c, tt=tt: att[:, tt, c * 128:(c + 1) * 128], 8, X1, 0, [tatt, x1_last], LOWB[tt], tt)
    t = run(lin_B(X1, DA["w_o"][1], 8, 0, D, BK, txs))
    x1_last = t
    add_to_h(BK, 1.0, t)
    mx.close()
    kv.close()
    for e in ("act", "dve", "pool"):
        P.wait(e, t)
    P.wait("act", *dumps)
    P.wait("dve", *dumps)
    dump("h5", hx[:], *h_ready)

    g, tg, gi = load_gain(A["ffn2_norm_g"][1])
    rs = stats(hx, h_ready)
    tx = normed(hx, h_ready, g, tg, gi, X0, LOWB, rs, [x0_last])
    x0_last = run_ffn("ffn2", 1, X0, tx)
    dump("h6", hx[:], *h_ready)

    ffn_last = pe_done[-1]
    for e in ("act", "dve", "pool", "sp"):
        P.wait(e, ffn_last)
    g, tg, gi = load_gain(A["norm_pre_2"][0])
    rs = stats(hx, h_ready)
    tx = normed(hx, h_ready, g, tg, gi, X0, LOWB, rs, [x0_last])

    mx = ExitStack()
    va = sb("va", [128, 2, 512], F32, mx)
    vb = sb("vb", [128, 2, 512], F32, mx)
    zob = sb("zob", [128, 3, 2, 512], F32, mx)
    gab = xg
    qk = sb("qk", [128, 8, 3 + S], F32, mx)
    qkc = sb("qkc", [128, 8, S], F32, mx)
    aT = sb("aT", [128, 8, S], F32, mx)
    ctap = sb("ctap", [128, 8, 4], F32, mx)
    lamr = sb("lamr", [128, 4, 64], F32, mx)
    lam = sb("lam", [128, 8], F32, mx)
    gt = sb("gt", [128, 2, 8], F32, mx)
    gates = sb("gates", [128, 2, 64], F32, mx)
    bif = sb("bif", [128, 8], F32, mx)
    kbn = sb("kbn", [128, 1], F32, mx)
    oa = sb("oa", [128, 2, 512], F32, mx)
    ob = sb("ob", [128, 2, 512], F32, mx)
    pbuf = sb("pb2", [128, 3, 512], F32, mx)
    ptbuf = sb("pt2", [128, 2, 256], F32, mx)
    crow = pbuf[0:4, 0:2, :].rearrange("p a b -> p (a b)")
    nab = sb("nab", [128, 2, 512], F32, mx)

    t_crow = load(crow, A["conv_qk_2"][0])
    t_lam = load(lamr[:].rearrange("p a d -> p (a d)"),
                 rows128(A["lambda_qk_2"].rearrange("a b d -> (a b d)")))
    t_bif = load(bif[:], rows128(A["b_if_2"][0]))
    t_na = load(nab[:, 0, :], rows128(A["norm_a_2"][0]))
    t_nb = load(nab[:, 1, :], rows128(A["norm_b_2"][0]))
    tz = V(lambda: dve.memset(qk[:, :, 0:3], 0.0))
    take(4)
    P.wait("pe", t_crow)
    for c in range(8):
        t = T(lambda c=c: pe.transpose(bank[4][:, c * 4:(c + 1) * 4], crow[:, c * 128:(c + 1) * 128], ident[0:4, 0:4]))
    t_ctap = V(lambda: dve.tensor_copy(ctap[:].rearrange("p a b -> p (a b)"), bank[4][:, 0:32]), t)
    free[4] = [t_ctap]
    pf0 = t
    l12 = lamr[:, 0:3:2, :]
    t = V(lambda: dve.tensor_tensor(l12, l12, lamr[:, 1:4:2, :], ALU.mult), t_lam)
    t = V(lambda: dve.reduce_sum(lam[:, 0:2], l12, AX), t)
    t = C(lambda: act.activation(lam[:, 2:4], lam[:, 0:2], ACT.Exp), t)
    t = V(lambda: dve.tensor_tensor(lam[:, 4:5], lam[:, 3:4], lam[:, 2:3], ALU.subtract), t)
    lam_init = 0.8 - 0.6
    t_lamn = V(lambda: dve.tensor_scalar(lam[:, 5:6], lam[:, 4:5], -lam_init, None, ALU.add), t)

    tqk = []
    for c in range(4):
        b = c
        lin_A(X0, win, 2048 + c * 256, b, tx)
        t = C(lambda c=c, b=b: act.copy(qk[:, 2 * c:2 * c + 2, 3:3 + S],
                                        bank[b][:].rearrange("p (a n) -> p a n", a=2)), pe_done[-1])
        free[b] = [t]
        tqk.append(t)

    def conv4():
        for c in range(8):
            for k in range(4):
                if k == 0:
                    t = V(lambda c=c: dve.tensor_scalar(qkc[:, c, :], qk[:, c, 0:S], ctap[:, c, 0:1], None, ALU.mult),
                          tqk[c // 2], t_ctap, tz)
                else:
                    t = V(lambda c=c, k=k: dve.scalar_tensor_tensor(
                        out=qkc[:, c, :], in0=qk[:, c, k:k + S], scalar=ctap[:, c, k:k + 1], in1=qkc[:, c, :],
                        op0=ALU.mult, op1=ALU.add), t)
                yield t
            tcv4.append(t)
    tcv4 = []
    cg = conv4()

    take(4)
    take(5)
    s = next_slot((0, 8, 4608, 8))
    P.wait("pe", s.th, s.tl)
    for tt in range(2):
        for k in range(8):
            l = [X0[i][:, k, tt * 128:(tt + 1) * 128] for i in range(2)]
            o = bank[4 + tt][:, 0:8]
            MM(o, l[0], s.hi[:, k, :], k == 0, False)
            MM(o, l[1], s.hi[:, k, :], False, False)
            t = T(lambda o=o, l=l, k=k, s=s: pe.matmul(o, l[0], s.lo[:, k, :], start=False, stop=k == 7,
                                                       skip_group_check=True), sem="w" if tt == 1 and k == 7 else None)
        u = V(lambda tt=tt: dve.tensor_tensor(gt[:, tt, :], bank[4 + tt][:, 0:8], bif[:], ALU.add), t, t_bif)
        free[4 + tt] = [u]
    pe_done.append(t)
    t_gt = u

    taT = []
    for c in range(4):
        b = c
        lin_A(X0, win, c * 256, b, tx)
        t = C(lambda c=c, b=b: act.copy(aT[:, 2 * c:2 * c + 2, :],
                                        bank[b][:].rearrange("p (a n) -> p a n", a=2)), pe_done[-1])
        free[b] = [t]
        taT.append(t)
        some(cg, 8)
    some(cg, 100)
    tcc = []
    for h in range(2):
        tcc.append(C(lambda h=h: act.activation(qkc[:, 4 * h:4 * h + 4, :], qkc[:, 4 * h:4 * h + 4, :], ACT.Silu),
                     tcv4[4 * h + 3]))
    V(lambda: dve.tensor_scalar(qkc[:, 4:8, :], qkc[:, 4:8, :], 128.0 ** -0.5, None, ALU.mult), tcc[1])
    tcc.append(("dve_done", P.counts["dve_done"]))

    fg = gt[:, :, 4:8]
    e1 = gates[:, :, 0:4]
    e2 = gates[:, :, 4:8]
    lf = gates[:, :, 8:12]
    Fc = gates[:, :, 12:16]
    w_ = gates[:, :, 16:20]
    t = V(lambda: dve.tensor_scalar(e1, fg, -1.0, None, ALU.mult), t_gt)
    t = V(lambda: dve.tensor_tensor(e1, e1, fg, ALU.min), t)
    t = C(lambda: act.activation(e2, e1, ACT.Exp), t)
    t = C(lambda: act.activation(e2, e2, ACT.Ln, bias=1.0), t)
    u = V(lambda: dve.tensor_scalar(lf, fg, 0.0, None, ALU.min), t_gt)
    t = V(lambda: dve.tensor_tensor(lf, lf, e2, ALU.subtract), t, u)
    take(4)
    MM(bank[4][:, 0:4], upper[:], gates[:, 0, 8:12], True, True, t, t_upper)
    MM(bank[4][:, 4:8], ones[:], gates[:, 0, 8:12], True, False)
    t = MMi(bank[4][:, 4:8], upper[:], gates[:, 1, 8:12], False, True)
    t = V(lambda: dve.tensor_copy(Fc, bank[4][:, 0:8].rearrange("p (a b) -> p a b", a=2)), t)
    free[4] = [t]
    t_w = V(lambda: dve.tensor_tensor(w_, gt[:, :, 0:4], Fc, ALU.subtract), t)
    t_F = t
    dump("F", gates[:], t_w)

    t = run(lin_B(X0, win, 8, 3072, 512, [[5], [6]], tx))
    for tt in range(2):
        u = V(lambda tt=tt: dve.tensor_copy(vb[:, tt, :], bank[5 + tt][:]), t)
        free[5 + tt] = [u]
    t_vb = u
    t = run(lin_B(X0, win, 8, 1024, 512, [[4], [7]], tx))
    for tt, b in enumerate((4, 7)):
        u = V(lambda tt=tt, b=b: dve.tensor_copy(va[:, tt, :], bank[b][:]), t)
        free[b] = [u]
    t_va = u

    def rest():
        for i, c0 in enumerate((1536, 3584, 4096)):
            g_ = lin_B(X0, win, 8, c0, 512, [[6], [7]], tx)
            for t in g_:
                yield
            for tt in range(2):
                u = V(lambda i=i, tt=tt: dve.tensor_copy(zob[:, i, tt, :], bank[6 + tt][:]), t)
                free[6 + tt] = [u]
            tzo.append(u)
    tzo = []
    rg = rest()

    st = [dict() for _ in range(8)]
    pf, ptf = [pf0] * 3, [None] * 2
    toa = []

    def d_scores(i):
        tt, h = i // 4, i % 4
        kw = 128 * (tt + 1)
        b = 2 * (i % 2)
        take(b)
        take(b + 1)
        P.wait("pe", t_alib, t_identb, *taT)
        ps = psum[:, b:b + 2, 0:kw]
        for c in range(2):
            MM(ps[:, c, :], aT[c * 64:(c + 1) * 64, h, tt * 128:(tt + 1) * 128],
               aT[c * 64:(c + 1) * 64, 4 + h, 0:kw], True, False)
        for c in range(2):
            t = MMi(ps[:, c, :], identb[:], alib[:, tt, h, 0:kw], False, True)
        col0 = 160 + 12 * (i % 3)
        mx_, nb, sm, rc = (small[:, col0 + 2 * q:col0 + 2 * q + 2] for q in range(4))
        t = V(lambda: dve.reduce_max(mx_, ps, AX), t, st[i - 3]["fin"] if i >= 3 else None)
        t = V(lambda: dve.tensor_scalar(nb, mx_, -0.125, None, ALU.mult), t)
        p = pbuf[:, i % 3, 0:2 * kw].rearrange("p (c k) -> p c k", c=2)
        for c in range(2):
            te = C(lambda c=c: act.activation(p[:, c, :], ps[:, c, :], ACT.Exp, bias=nb[:, c:c + 1], scale=0.125,
                                              accum_out=sm[:, c:c + 1]), t, pf[i % 3])
        free[b] = free[b + 1] = [te]
        t = V(lambda: dve.reciprocal(rc, sm), te)
        t = V(lambda: dve.tensor_scalar(rc[:, 1:2], rc[:, 1:2], lam[:, 5:6], None, ALU.mult), t, t_lamn)
        t = V(lambda: dve.tensor_scalar(p[:, 1, :], p[:, 1, :], rc[:, 1:2], None, ALU.mult), t)
        t = V(lambda: dve.scalar_tensor_tensor(out=p[:, 0, :], in0=p[:, 0, :], scalar=rc[:, 0:1], in1=p[:, 1, :],
                                               op0=ALU.mult, op1=ALU.add), t)
        st[i].update(p=p[:, 0, :], tp=t, kw=kw)

    def pv_turn(st, i):
        s = st[i]
        nk = s["kw"] // 128
        s["pt"] = None
        take(4)
        P.wait("pe", s["tp"])
        for k in range(nk):
            t = T(lambda k=k: pe.transpose(bank[4][:, k * 128:(k + 1) * 128], s["p"][:, k * 128:(k + 1) * 128], ident[:]))
        pf[i % 3] = t
        s["pt"] = C(lambda: act.copy(ptbuf[:, i % 2, 0:nk * 128], bank[4][:, 0:nk * 128]), t, ptf[i % 2])
        free[4] = [s["pt"]]

    def pv_values(st, i, v, tv, b):
        tt, h = i // 4, i % 4
        s = st[i]
        nk = s["kw"] // 128
        take(b)
        P.wait("pe", s["pt"], tv)
        for k in range(nk):
            t = T(lambda k=k: pe.matmul(bank[b][:, 0:128], ptbuf[:, i % 2, k * 128:(k + 1) * 128],
                                        v[:, k, h * 128:(h + 1) * 128], start=k == 0, stop=k == nk - 1,
                                        skip_group_check=True))
        ptf[i % 2] = t
        return t

    def diff():
        for i in range(10):
            if i < 8:
                d_scores(i)
            if 0 <= i - 1 < 8:
                pv_turn(st, i - 1)
            if 0 <= i - 2 < 8:
                j = i - 2
                b = 5
                t = pv_values(st, j, va, t_va, b)
                u = V(lambda j=j, b=b: dve.tensor_copy(oa[:, j // 4, (j % 4) * 128:(j % 4 + 1) * 128], bank[b][:, 0:128]), t)
                free[b] = [u]
                st[j]["fin"] = u
                toa.append(u)
            yield
    dg = diff()
    for _ in dg:
        next(rg, None)
    dump("oa", oa[:], toa[-1])

    st2 = [dict() for _ in range(8)]
    tob = []
    wd = sb("wd", [128, 2, 128], F32, mx)
    wdf = [None, None]

    def m_scores(i):
        tt, h = i // 4, i % 4
        kw = 128 * (tt + 1)
        b = i % 3
        td = []
        for k in range(tt + 1):
            td.append(V(lambda k=k: dve.tensor_scalar(wd[:, k, :], ident[:], gates[:, k, 16 + h:17 + h], None, ALU.mult),
                        t_w, wdf[k], t_ident))
        take(b)
        P.wait("pe", *tcc)
        MM(bank[b][:, 0:kw], qkc[:, h, tt * 128:(tt + 1) * 128], qkc[:, 4 + h, 0:kw], True, False)
        for k in range(tt + 1):
            t = MMi(bank[b][:, kw + k * 128:kw + (k + 1) * 128], ones[:], wd[:, k, :], False, False, td[k], t_ones)
            wdf[k] = t
        t = MMi(bank[b][:, 2 * kw - 128:2 * kw], identb[:], maskb[:], False, True)
        wr = bank[b][:, kw:2 * kw]
        col0 = 160 + 12 * (i % 3)
        M, nM, e, den, r = (small[:, col0 + q:col0 + q + 1] for q in range(5))
        t = V(lambda: dve.reduce_max(M, wr, AX), t, st2[i - 3]["fin"] if i >= 3 else None)
        t = V(lambda: dve.tensor_scalar(nM, M, 0.0, -1.0, ALU.max, ALU.mult), t)
        p = pbuf[:, i % 3, 0:2 * kw].rearrange("p (c k) -> p c k", c=2)
        te = C(lambda: act.activation(p[:, 1, :], wr, ACT.Exp, bias=nM), t, pf[i % 3])
        tF = V(lambda: dve.tensor_tensor(e, nM, gates[:, tt, 12 + h:13 + h], ALU.subtract), t)
        tF = C(lambda: act.activation(e, e, ACT.Exp), tF)
        t = V(lambda: dve.tensor_tensor(p[:, 0, :], bank[b][:, 0:kw], p[:, 1, :], ALU.mult), te, pf[i % 3])
        free[b] = [te, t]
        st2[i].update(p=p[:, 0, :], tp=t, kw=kw)
        t = V(lambda: dve.reduce_sum(den, p[:, 0, :], AX), t)
        t = V(lambda: dve.tensor_scalar(M, den, -1.0, None, ALU.mult), t)
        t = V(lambda: dve.tensor_tensor(den, den, M, ALU.max), t)
        t = V(lambda: dve.tensor_tensor(den, den, e, ALU.max), t, tF)
        t = V(lambda: dve.reciprocal(r, den), t)
        st2[i].update(r=r, tr=t)

    def mlstm():
        for i in range(10):
            if i < 8:
                m_scores(i)
            if 0 <= i - 1 < 8:
                pv_turn(st2, i - 1)
            if 0 <= i - 2 < 8:
                j = i - 2
                b = 5
                t = pv_values(st2, j, vb, t_vb, b)
                u = V(lambda j=j, b=b: dve.tensor_scalar(ob[:, j // 4, (j % 4) * 128:(j % 4 + 1) * 128],
                                                         bank[b][:, 0:128], st2[j]["r"], None, ALU.mult), t, st2[j]["tr"])
                free[b] = [u]
                st2[j]["fin"] = u
                tob.append(u)
            yield
    for _ in mlstm():
        next(rg, None)
    for _ in rg:
        pass
    dump("ob", ob[:], tob[-1])
    x0_read = []

    sc = pbuf[:].rearrange("p a b -> p (a b)")
    dst = [X1, X1]
    tga = run(lin_B(X0, win, 8, 4616, D, BK, tx))
    sig = []
    for tt in range(2):
        for j in range(2):
            b = BK[tt][j]
            t = C(lambda tt=tt, j=j, b=b: act.activation(gab[:, tt, j * 512:(j + 1) * 512], bank[b][:], ACT.Sigmoid), tga, xg_free[tt])
            free[b] = [t]
            sig.append(t)
    tsg = C(lambda: act.activation(zob[:, 1].rearrange("p a b -> p (a b)"), zob[:, 1].rearrange("p a b -> p (a b)"),
                                   ACT.Sigmoid), tzo[1])
    tsa = C(lambda: act.activation(zob[:, 0].rearrange("p a b -> p (a b)"), zob[:, 0].rearrange("p a b -> p (a b)"),
                                   ACT.Silu), tzo[0])
    tsb = C(lambda: act.activation(zob[:, 2].rearrange("p a b -> p (a b)"), zob[:, 2].rearrange("p a b -> p (a b)"),
                                   ACT.Silu), tzo[2])
    sqs = aT[:].rearrange("p a b -> p (a b)")

    def head128(x, z, ng, tng, mul, ready, tz_, c0):
        v = x.rearrange("p (g d) -> p g d", d=128)
        q = sqs[:, 0:1024].rearrange("p (g d) -> p g d", d=128)
        ss, r_ = small[:, c0:c0 + 8], small[:, c0 + 8:c0 + 16]
        t = V(lambda: dve.tensor_tensor(q, v, v, ALU.mult), *ready)
        t = V(lambda: dve.reduce_sum(ss, q, AX), t)
        t = rstd_of(ss, r_, 128, t, 8)
        if mul != 1.0:
            t = V(lambda: dve.tensor_scalar(r_, r_, mul, None, ALU.mult), t)
        t = V(lambda: dve.tensor_tensor(v, v, wide(r_, 2, 128), ALU.mult), t)
        v2 = x.rearrange("p (t n) -> p t n", t=2)
        t = V(lambda: dve.tensor_tensor(v2, v2, wide(ng, 1, 2), ALU.mult), t, tng)
        return V(lambda: dve.tensor_tensor(x, x, z, ALU.mult), t, tz_)

    flat = lambda a: a.rearrange("p a b -> p (a b)")
    toaf = head128(flat(oa[:]), flat(zob[:, 0]), nab[:, 0, :], t_na, 1.0 - lam_init, toa, tsa, 200)
    t = V(lambda: dve.tensor_tensor(flat(ob[:]), flat(ob[:]), flat(zob[:, 1]), ALU.mult), tsg, *tob)
    tobf = head128(flat(ob[:]), flat(zob[:, 2]), nab[:, 1, :], t_nb, 1.0, [t], tsb, 216)
    dump("ya", oa[:], toaf)
    dump("yb", ob[:], tobf)
    tgb = run(lin_B(X0, win, 8, 5640, D, BK, tx))
    gbb = zob[:].rearrange("p a t n -> p (a t n)")[:, 0:2048].rearrange("p (t n) -> p t n", t=2)
    sigb = []
    for tt in range(2):
        for j in range(2):
            b = BK[tt][j]
            t = C(lambda tt=tt, j=j, b=b: act.activation(gbb[:, tt, j * 512:(j + 1) * 512], bank[b][:], ACT.Sigmoid),
                  tgb, toaf, tobf)
            free[b] = [t]
            sigb.append(t)
    tya, tyb = [], []
    for tt in range(2):
        tya += to_T(lambda c, tt=tt: oa[:, tt, c * 128:(c + 1) * 128], 4, X1, 0, [toaf, x1_last], [2 * tt], tt)
    for tt in range(2):
        tyb += to_T(lambda c, tt=tt: ob[:, tt, c * 128:(c + 1) * 128], 4, X1, 4, [tobf], [2 * tt + 1], tt)
    t = run(lin_B(X1, DA["w_a_2"][0], 4, 0, D, LOWB, tya))
    mg = []
    for tt in range(2):
        for j in range(2):
            b = LOWB[tt][j]
            o = gab[:, tt, j * 512:(j + 1) * 512]
            u = V(lambda o=o, b=b: dve.tensor_tensor(o, o, bank[b][:], ALU.mult), t, *sig)
            free[b] = [u]
            mg.append(u)
    YB = (xh[1][:, 4:8, :], xl[1][:, 4:8, :])
    t = run(lin_B(YB, DA["w_b_2"][0], 4, 0, D, BK, tyb))
    for tt in range(2):
        for j in range(2):
            b = BK[tt][j]
            o = gbb[:, tt, j * 512:(j + 1) * 512]
            u = V(lambda o=o, b=b: dve.tensor_tensor(o, o, bank[b][:], ALU.mult), t, *sigb)
            free[b] = [u]
        u = V(lambda tt=tt: dve.tensor_tensor(gab[:, tt, :], gab[:, tt, :], gbb[:, tt, :], ALU.add), u, *mg)
        mg.append(u)
    x0_last = tgb
    txs = []
    for tt in range(2):
        txs += to_T(lambda c, tt=tt: gab[:, tt, c * 128:(c + 1) * 128], 8, X0, 0, [mg[4 + tt]], LOWB[tt], tt)
    g, tg, gi = load_gain(A["norm_post_2"][0])
    t = run(lin_B(X0, DA["w_out_2"][0], 8, 0, D, BK, txs))
    xg_free[0] = xg_free[1] = t
    outs = []
    for tt in range(2):
        u = []
        for j in range(2):
            u.append(C(lambda tt=tt, j=j: act.copy(gbb[:, tt, j * 512:(j + 1) * 512], bank[BK[tt][j]][:]), t, mg[-1]))
        c0 = 2 * (col() % 16)
        r_ = sumsq(gbb[:, tt, :], c0, u[-1], tt)
        v = V(lambda tt=tt, c0=c0: dve.scalar_tensor_tensor(
            out=xg[:, tt, :], in0=gbb[:, tt, :], scalar=small[:, c0 + 1:c0 + 2], in1=g, op0=ALU.mult, op1=ALU.mult), r_, tg)
        v = V(lambda tt=tt: dve.tensor_tensor(xg[:, tt, :], xg[:, tt, :], hx[:, tt, :], ALU.add), v, h_ready[tt])
        outs.append(load(out[0, tt * 128:(tt + 1) * 128, :], xg[:, tt, :], v))
    mx.close()
    P.wait("sp", *outs, *dumps)
    assert state["used"] == len(plan)


_INS = ['x', 'mem', 'positions', 'ffn1_norm_g', 'ffn1_w_gate', 'ffn1_w_up', 'ffn1_w_down', 'mix_norm_g',
        'mem_norm_g', 'w_mem_kv', 'mem_q_norm_g', 'mem_k_norm_g', 'w_o', 'ffn2_norm_g', 'ffn2_w_gate',
        'ffn2_w_up', 'ffn2_w_down', 'a_w_in', 'a_dw_kernel', 'a_dw_bias', 'a_ln_g', 'a_ln_b', 'kv_norm_g',
        'w_kv', 'k_norm_g', 'b_w_in', 'b_q_norm_g', 'norm_pre_2', 'norm_post_2', 'w_in_2', 'b_if_2',
        'conv_qk_2', 'lambda_qk_2', 'norm_a_2', 'norm_b_2', 'w_a_2', 'w_b_2', 'w_out_2']


def kernel(**inputs):
    import numpy as _np
    import concourse.bacc as _bacc
    from concourse import mybir as _mybir
    from concourse.bass_utils import run_bass_kernel_spmd as _run

    nc = _bacc.Bacc("TRN2", target_bir_lowering=False, num_devices=1)
    arrays, args = {}, {}
    for name in _INS:
        a = _np.ascontiguousarray(inputs[name])
        arrays[f"in_{name}"] = a
        args[name] = nc.dram_tensor(f"in_{name}", a.shape, _mybir.dt.from_np(a.dtype), kind="ExternalInput").ap()
    out = nc.dram_tensor("out_0", (1, S, D), _mybir.dt.float32, kind="ExternalOutput").ap()
    program(nc, args, out)
    r = _run(nc, [arrays], core_ids=[0])
    return r.results[0]["out_0"]
```

```python
from contextlib import ExitStack

import concourse.bass as bass
import numpy as np
from concourse import mybir

F32 = mybir.dt.float32
F32R = mybir.dt.float32r
BF16 = mybir.dt.bfloat16
I32 = mybir.dt.int32
ALU = mybir.AluOpType
ACT = mybir.ActivationFunctionType
AX = mybir.AxisListType.X

D = 1024
S = 256
FF = 2816
NEG = -1.0e30
EPS = 1e-6
NDG = 16
CONV_PE = (1, 3)
CONV_DVE = (0, 2, 4, 5)
SLOT = 1024
RAW, SPLIT, AHEAD = 7, 5, 4


def wide(ap, axis, n):
    v = ap.unsqueeze(axis)
    shape = list(v.shape)
    shape[axis] = n
    return v.broadcast_to(shape)


def rows128(row):
    return row.partition_broadcast(128)


class Program:

    def __init__(self, nc, ctx):
        self.nc, self.ctx = nc, ctx
        self.engines = {"pe": nc.tensor, "act": nc.scalar, "dve": nc.vector, "pool": nc.gpsimd, "sp": nc.sync}
        self.sems, self.counts = {}, {}
        self.seen = {e: {} for e in self.engines}

    def sem(self, name):
        if name not in self.sems:
            self.sems[name] = self.ctx.enter_context(self.nc.semaphore(name))
            self.counts[name] = 0
        return self.sems[name]

    def op(self, eng, fn, *waits, sem=None, by=1):
        self.wait(eng, *waits)
        name = f"{eng}_{sem}" if sem else f"{eng}_done"
        s = self.sem(name)
        self.counts[name] += by
        fn().then_inc(s, by)
        return (name, self.counts[name])

    def quiet(self, eng, fn, *waits):
        self.wait(eng, *waits)
        fn()

    def wait(self, eng, *waits):
        for w in waits:
            if w is None:
                continue
            name, n = w
            if self.seen[eng].get(name, 0) >= n:
                continue
            self.seen[eng][name] = n
            s = self.sems[name]
            self.engines[eng].wait_ge(s, n)


def program(nc, A, out, dbg=None):
    with ExitStack() as ctx:
        build(nc, ctx, A, out, dbg or {})


def build(nc, ctx, A, out, dbg):
    P = Program(nc, ctx)
    pe, act, dve, pool = nc.tensor, nc.scalar, nc.vector, nc.gpsimd

    def sb(name, shape, dt=F32, c=ctx):
        return c.enter_context(nc.sbuf_tensor(name, shape, dt))

    psum = ctx.enter_context(nc.psum_tensor("psum", [128, 8, 512], F32))
    bank = [psum[:, i, :] for i in range(8)]
    free = [[] for _ in range(8)]

    def V(fn, *w, sem=None):
        return P.op("dve", fn, *w, sem=sem)

    def C(fn, *w, sem=None):
        return P.op("act", fn, *w, sem=sem)

    def G(fn, *w, sem=None):
        return P.op("pool", fn, *w, sem=sem)

    def T(fn, *w, sem=None):
        return P.op("pe", fn, *w, sem=sem)

    def MM(o, l, r, start, stop, *w):
        P.quiet("pe", lambda: pe.matmul(o, l, r, start=start, stop=stop, skip_group_check=True), *w)

    def MMi(o, l, r, start, stop, *w):
        return T(lambda: pe.matmul(o, l, r, start=start, stop=stop, skip_group_check=True), *w)

    def take(b):
        P.wait("pe", *free[b])
        free[b] = []

    raw = sb("raw", [128, RAW, SLOT])
    whi = sb("whi", [128, SPLIT, SLOT], F32R)
    wlo = sb("wlo", [128, SPLIT, SLOT], F32R)
    hT = sb("hT", [128, 8, S])
    acc = sb("acc", [128, 512])
    sqb = sb("sqb", [128, 2, 512])
    rowr = sb("rowr", [128, 2, S])
    diag = sb("diag", [128, 2, 128])
    gcol = sb("gcol", [128, 8, 8])
    xh = [sb(f"xh{i}", [128, 8, S], F32R) for i in range(2)]
    xl = [sb(f"xl{i}", [128, 8, S], F32R) for i in range(2)]
    ident = sb("ident", [128, 128])
    ones = sb("ones", [128, 128])
    ln1 = sb("ln1", [128, 128])
    upper = sb("upper", [128, 128])
    identb = sb("identb", [128, 128], BF16)
    maskb = sb("maskb", [128, 128], BF16)
    alib = sb("alib", [128, 2, 4, S], BF16)
    mhalf = sb("mhalf", [128, 16])
    hg = sb("hg", [128, 6, 64])
    small = sb("small", [128, 320])
    kTm = [sb(f"kTm{i}", [128, 2, S]) for i in range(2)]
    mkv = [sb(f"mkv{i}", [128, 2, 512]) for i in range(2)]

    plan = []

    def slots_A(w, K, c0, n=256):
        for k in range(0, K, 4):
            plan.append((w, k, min(4, K - k), c0, n))

    def slots_B(w, K, c0, n):
        kk = SLOT // n
        for k in range(0, K, kk):
            plan.append((w, k, kk, c0, n))

    state = {"dma": 0, "split": 0, "used": 0}
    lo_done, hi_done, pe_done = [], [], []
    hooks = {}

    def at_slot(ahead, f):
        hooks.setdefault(state["used"] + ahead, []).append(f)

    def view(t, j, nk, n):
        return t[:, j, 0:nk * n].rearrange("p (k n) -> p k n", k=nk)

    def split_to(i):
        while state["split"] <= min(i, len(plan) - 1):
            j = state["split"]
            w, k0, nk, c0, n = plan[j]
            if j >= RAW:
                P.wait("sp", lo_done[j - RAW])
            src = w[k0 * 128:(k0 + nk) * 128, c0:c0 + n].rearrange("(k p) n -> p k n", p=128)
            dst = view(raw, j % RAW, nk, n)
            t = P.op("sp", lambda d=dst, s=src: nc.sync.dma_start(d, s), sem=f"w{j % RAW}", by=16)
            r = raw[:, j % RAW, 0:nk * n]
            h = whi[:, j % SPLIT, 0:nk * n]
            lo = wlo[:, j % SPLIT, 0:nk * n]
            before = pe_done[j - SPLIT] if j >= SPLIT else None
            th = C(lambda h=h, r=r: act.copy(h, r), t, before, sem="hi")
            tl = V(lambda h=h, r=r, lo=lo: dve.tensor_tensor(lo, r, h.bitcast(F32), ALU.subtract), th, before, sem="lo")
            hi_done.append(th)
            lo_done.append(tl)
            state["split"] += 1

    class Slot:
        pass

    def next_slot(key):
        i = state["used"]
        for f in hooks.pop(i, []):
            f()
        assert plan[i][1:] == key, (plan[i], key)
        split_to(i + AHEAD)
        s = Slot()
        s.hi = view(whi, i % SPLIT, key[1], key[3])
        s.lo = view(wlo, i % SPLIT, key[1], key[3])
        s.th, s.tl = hi_done[i], lo_done[i]
        state["used"] += 1
        return s

    def lin_A(x, w, K, c0, b):
        take(b)
        for k0 in range(0, K, 4):
            m = min(4, K - k0)
            s = next_slot((k0, m, c0, 256))
            for k in range(m):
                kc = k0 + k
                for j in range(2):
                    o = bank[b][:, j * 256:(j + 1) * 256]
                    hi = s.hi[:, k, j * 128:(j + 1) * 128]
                    lo = s.lo[:, k, j * 128:(j + 1) * 128]
                    last = kc == K - 1 and j == 1
                    MM(o, hi, x[0][:, kc, :], kc == 0 and j == 0, False, s.th, x[2][kc][0])
                    MM(o, hi, x[1][:, kc, :], False, False, x[2][kc][1])
                    P.wait("pe", s.tl)
                    if k == m - 1 and j == 1:
                        t = T(lambda: pe.matmul(o, lo, x[0][:, kc, :], start=False, stop=last,
                                                skip_group_check=True), sem="w")
                    else:
                        MM(o, lo, x[0][:, kc, :], False, last)
            pe_done.append(t)
        return t

    def lin_B(x, w, K, c0, n, banks):
        kk = SLOT // n if n >= 64 else K
        for tt in range(2):
            for b in banks[tt]:
                take(b)
        for k0 in range(0, K, kk):
            s = next_slot((k0, kk, c0, n))
            P.wait("pe", s.th)
            for k in range(kk):
                kc = k0 + k
                P.wait("pe", x[2][kc][0], x[2][kc][1])
                for tt in range(2):
                    jobs = []
                    for xi, wi in ((0, 0), (1, 0), (0, 1)):
                        for j, b in enumerate(banks[tt]):
                            jobs.append((xi, wi, j, b))
                    for i, (xi, wi, j, b) in enumerate(jobs):
                        w0, w1 = j * 512, min(n, (j + 1) * 512)
                        o = bank[b][:, 0:w1 - w0]
                        l = x[xi][:, kc, tt * 128:(tt + 1) * 128]
                        r = (s.lo if wi else s.hi)[:, k, w0:w1]
                        st = kc == 0 and xi == 0 and wi == 0
                        sp_ = kc == K - 1 and wi == 1
                        if wi:
                            P.wait("pe", s.tl)
                        if k == kk - 1 and tt == 1 and i == len(jobs) - 1:
                            t = T(lambda o=o, l=l, r=r, sp_=sp_: pe.matmul(
                                o, l, r, start=False, stop=sp_, skip_group_check=True), sem="w")
                        else:
                            MM(o, l, r, st, sp_)
            pe_done.append(t)
            yield t

    def run(g):
        t = None
        for t in g:
            pass
        return t

    def load(dst, src, *w, slow=False):
        n = state.setdefault("loads", 0)
        state["loads"] += 1
        return P.op("sp", lambda: nc.sync.dma_start(dst, src, allow_slow_non_contiguous=slow), *w, sem=f"l{n}", by=16)

    t = G(lambda: pool.memset(ident[:], 0.0))
    t_ident = G(lambda: pool.affine_select(out=ident[:], in_=ident[:], compare_op=ALU.not_equal, fill=1.0,
                                           base=0, pattern=[[-1, 128]], channel_multiplier=1), t)
    t = G(lambda: pool.memset(ones[:], 1.0))
    t_ones = t
    t_ln1 = G(lambda: pool.memset(ln1[:], 1.0 / 768))
    t_upper = G(lambda: pool.affine_select(out=upper[:], in_=ones[:], compare_op=ALU.is_ge, fill=0.0,
                                           base=0, pattern=[[1, 128]], channel_multiplier=-1), t)
    t_identb = G(lambda: pool.tensor_copy(identb[:], ident[:]), t_ident)
    t = G(lambda: pool.memset(maskb[:], 0.0))
    t_mask = G(lambda: pool.affine_select(out=maskb[:], in_=maskb[:], compare_op=ALU.is_ge, fill=NEG,
                                          base=0, pattern=[[-1, 128]], channel_multiplier=1), t)
    t_half = G(lambda: pool.memset(mhalf[:], -0.5))
    t = None
    for tt in range(2):
        ti = G(lambda tt=tt: pool.iota(kTm[0][:, 0, :], pattern=[[1, S]], base=-128 * tt, channel_multiplier=-1,
                                       allow_small_or_imprecise_dtypes=True), t)
        for h in range(4):
            c = 8.0 * 2.0 ** (-2 * (h + 1))
            t = G(lambda tt=tt, h=h, c=c: pool.tensor_scalar(alib[:, tt, h, :], kTm[0][:, 0, :], c, None, ALU.mult), ti)
    t_alib = G(lambda: pool.affine_select(out=alib[:, 0], in_=alib[:, 0], compare_op=ALU.is_ge, fill=NEG, base=0,
                                          pattern=[[0, 4], [-1, S]], channel_multiplier=1), t)
    t_alib = G(lambda: pool.affine_select(out=alib[:, 1], in_=alib[:, 1], compare_op=ALU.is_ge, fill=NEG, base=128,
                                          pattern=[[0, 4], [-1, S]], channel_multiplier=1), t)

    h_done = [None] * 4
    row_free = [None, None]

    def rstd_of(ss, rs, n, t, width=1):
        t = G(lambda: pool.tensor_scalar(rs, ss, 1.0 / n, EPS, ALU.mult, ALU.add), t)
        return G(lambda: pool.tensor_tensor(rs, rs, mhalf[:, 0:width], ALU.pow), t)


    class Norm:
        pass

    def prep(p, targets):
        pair = hT[:, 2 * p:2 * p + 2, :]
        flat_ = pair.rearrange("p a b -> p (a b)")
        if p == 0:
            st_["acc"] = C(lambda: act.activation(acc[:], flat_, ACT.Square), h_done[p], st_.get("accfree"))
        for gi, x, xfree in targets:
            for c in (2 * p, 2 * p + 1):
                g = gcol[:, c, gi:gi + 1]
                th = C(lambda: act.activation(x[0][:, c, :], hT[:, c, :], ACT.Copy, scale=g), h_done[p], t_gcol, xfree)
                tl = V(lambda: dve.scalar_tensor_tensor(out=x[1][:, c, :], in0=hT[:, c, :], scalar=g,
                                                        in1=x[0][:, c, :].bitcast(F32), op0=ALU.mult,
                                                        op1=ALU.subtract), th, xfree)
                x[2][c] = [th, tl]
        if p > 0:
            t = C(lambda: act.activation(sqb[:, p % 2, :], flat_, ACT.Square), h_done[p], st_.get(("sqb", p % 2)))
            st_["acc"] = V(lambda: dve.tensor_tensor(acc[:], acc[:], sqb[:, p % 2, :], ALU.add), t, st_["acc"])
            st_["sqb", p % 2] = st_["acc"]

    st_ = {}

    def norm(b, ahead=(2, 3)):
        N = Norm()
        i = st_["n"] = st_.get("n", 0) + 1
        c0 = 4 * (i % 4)
        v = small[:, c0:c0 + 2]
        r = small[:, c0 + 2:c0 + 4]
        N.col = [r[:, 0:1], r[:, 1:2]]
        N.row = rowr[:, i % 2, :]
        N.i = i % 2
        t_acc = st_["acc"]

        def one():
            take(b)
            P.wait("pe", t_acc, t_ones)
            for tt in range(2):
                for j in range(2):
                    t = MMi(bank[b][:, 4 * tt:4 * tt + 4], acc[:, j * 256 + tt * 128:j * 256 + (tt + 1) * 128],
                            ones[:, 0:4], j == 0, j == 1)
            st_["accfree"] = t
            src = bank[b][:, 0:8:4]
            t = V(lambda: dve.tensor_scalar(v, src, 1.0 / D, EPS, ALU.mult, ALU.add), t)
            N.t_col = G(lambda: pool.tensor_tensor(r, v, mhalf[:, 0:2], ALU.pow), t)
            td = [V(lambda: dve.tensor_scalar(diag[:, tt, :], ident[:], N.col[tt], None, ALU.mult),
                    N.t_col, t_ident, st_.get("dgfree")) for tt in range(2)]
            N.td = td

        def two():
            for tt in range(2):
                t = MMi(bank[b][:, 128 + tt * 128:256 + tt * 128], ones[:], diag[:, tt, :], True, True, N.td[tt])
            st_["dgfree"] = t
            N.t_row = C(lambda: act.copy(N.row, bank[b][:, 128:384]), t, row_free[N.i])
            free[b] = [N.t_row]

        at_slot(ahead[0], one)
        at_slot(ahead[1], two)
        return N

    def to_T(src_of, n_chunks, dst, d0, ready, banks, tt, skip=0):
        res = []
        for i, c in enumerate(range(0, n_chunks, 4)):
            m = min(4, n_chunks - c)
            b = banks[i % len(banks)]
            take(b)
            P.wait("pe", t_ident, *ready)
            for j in range(m):
                f = lambda b=b, j=j, c=c: pe.transpose(bank[b][:, j * 128:(j + 1) * 128], src_of(c + j), ident[:])
                if j == m - 1:
                    t = T(f)
                else:
                    P.quiet("pe", f)
            src = bank[b][:, 0:m * 128].rearrange("p (k n) -> p k n", k=m)
            oh = dst[0][:, d0 + c:d0 + c + m, tt * 128:(tt + 1) * 128]
            ol = dst[1][:, d0 + c:d0 + c + m, tt * 128:(tt + 1) * 128]
            th = C(lambda oh=oh, src=src: act.copy(oh, src), t)
            tl = V(lambda oh=oh, ol=ol, src=src: dve.tensor_tensor(ol, src, oh.bitcast(F32), ALU.subtract), th)
            free[b] = [th, tl]
            for k in range(m):
                dst[2][d0 + c + k] = [th, tl]
            res += [th, tl]
        last_T[0] = t
        return res

    last_T = [None]

    def from_rows(src, ready, g, tg, dst, banks, rs, xg, xfree):
        r = [None, None]
        for tt in range(2):
            c, t = rs[tt]
            r[tt] = V(lambda: dve.scalar_tensor_tensor(out=xg[:, tt, :], in0=src[:, tt, :], scalar=c, in1=g,
                                                       op0=ALU.mult, op1=ALU.mult), t, tg, ready, xfree)
        P.wait("act", xfree)
        for tt in range(2):
            to_T(lambda c: xg[:, tt, c * 128:(c + 1) * 128], 8, dst, 0, [r[tt]], banks[tt], tt)
        return last_T[0]

    def row_stats(src, ready, junk, jfree, c0):
        r = []
        for tt in range(2):
            s = small[:, c0 + 2 * tt:c0 + 2 * tt + 1]
            o = small[:, c0 + 2 * tt + 1:c0 + 2 * tt + 2]
            t = C(lambda: act.activation(junk[:, tt, :], src[:, tt, :], ACT.Square, accum_out=s), ready, jfree)
            r.append((o, rstd_of(s, o, D, t)))
        return r

    def add_h(p, b, t, scale, N, targets, tmp, tmpfree):
        pair = hT[:, 2 * p:2 * p + 2, :].rearrange("p a b -> p (a b)")
        if N is None:
            t = V(lambda: dve.tensor_tensor(pair, bank[b][:], pair, ALU.add), t, h_done[p])
            free[b] = [t]
        else:
            o = tmp.rearrange("p (a b) -> p a b", a=2)
            src = bank[b][:].rearrange("p (a b) -> p a b", a=2)
            t = V(lambda: dve.scalar_tensor_tensor(out=o, in0=src, scalar=scale, in1=wide(N.row, 1, 2),
                                                   op0=ALU.mult, op1=ALU.mult), t, N.t_row)
            free[b] = [t]
            row_free[N.i] = t
            t = V(lambda: dve.tensor_tensor(pair, tmp, pair, ALU.add), t, h_done[p])
        h_done[p] = t
        prep(p, targets)

    def ffn(wg, wu, wd, x, N, gT, targets):
        gh, gl, gr, pr = gT
        gt_ = [None] * 22
        sgf = [[None], [None]]
        for p in range(FF // 256):
            bg, bu = (0, 1) if p % 2 == 0 else (2, 3)
            t1 = lin_A(x, wg, 8, p * 256, bg)
            t2 = lin_A(x, wu, 8, p * 256, bu)
            r, s, q = gr[:, p % 2, :], gr[:, p % 2, :], pr[:, p % 2, :]
            tr = V(lambda: dve.tensor_tensor(r.rearrange("p (a b) -> p a b", a=2),
                                             bank[bg][:].rearrange("p (a b) -> p a b", a=2), wide(N.row, 1, 2),
                                             ALU.mult), t1, N.t_row, *sgf[p % 2])
            free[bg] = [tr]
            ts = C(lambda: act.activation(s, r, ACT.Silu), tr, *sgf[p % 2])
            tm = V(lambda: dve.tensor_tensor(q, s, bank[bu][:], ALU.mult), ts, t2, *sgf[p % 2])
            free[bu] = [tm]
            oh = gh[:, 2 * p:2 * p + 2, :].rearrange("p a b -> p (a b)")
            ol = gl[:, 2 * p:2 * p + 2, :].rearrange("p a b -> p (a b)")
            th = C(lambda: act.copy(oh, q), tm)
            tl = V(lambda: dve.tensor_tensor(ol, q, oh.bitcast(F32), ALU.subtract), th)
            sgf[p % 2] = [ts, th, tl]
            gt_[2 * p] = gt_[2 * p + 1] = [th, tl]
        x_last = pe_done[-1]
        targets = [(gi, xx, x_last if f is None else f) for gi, xx, f in targets]
        for p in range(4):
            t = lin_A((gh, gl, gt_), wd, 22, p * 256, 4 + p)
            add_h(p, 4 + p, t, 0.5, N, targets, sqb_tmp(p), None)
        return x_last

    def sqb_tmp(p):
        return htmp[:, p % 2, :]

    def head_rms(src, nh, c0, g, tg, dst, ready, sq):
        ss = small[:, c0:c0 + nh]
        rs = small[:, c0 + 16:c0 + 16 + nh]
        v = src.rearrange("p (h d) -> p h d", d=64)
        o = dst.rearrange("p (h d) -> p h d", d=64)
        q = sq.rearrange("p (h d) -> p h d", d=64)
        t = V(lambda: dve.tensor_tensor(q, v, v, ALU.mult), *ready)
        t = V(lambda: dve.reduce_sum(ss, q, AX), t)
        t = rstd_of(ss, rs, 64, t, nh)
        t = V(lambda: dve.tensor_tensor(o, v, wide(rs, 2, 64), ALU.mult), t)
        return V(lambda: dve.tensor_tensor(o, o, wide(g, 1, nh), ALU.mult), t, tg)

    def padded_T(src_of, n, dst, c0, tt, ready, b):
        take(b)
        P.wait("pe", t_ident, *ready)
        for j in range(n):
            t = T(lambda: pe.transpose(bank[b][:, j * 128:(j + 1) * 128], src_of(j), ident[:]))
        for e in range(2):
            q = slice(64 * e, 64 * e + 64)
            src = bank[b][q, 0:n * 128].rearrange("p (k n) -> p k n", k=n)
            o = dst[q, 2 * c0 + e:2 * (c0 + n):2, tt * 128:(tt + 1) * 128]
            t = C(lambda: act.copy(o, src), t)
        free[b] = [t]
        return t

    def plain_T(src_of, n, dst_of, ready, b, eng="act"):
        take(b)
        P.wait("pe", t_ident, *ready)
        for j in range(n):
            f = lambda j=j: pe.transpose(bank[b][:, j * 128:(j + 1) * 128], src_of(j), ident[:])
            if j == n - 1:
                t = T(f)
            else:
                P.quiet("pe", f)
        src = bank[b][:, 0:n * 128].rearrange("p (k n) -> p k n", k=n)
        if eng == "act":
            t = C(lambda: act.copy(dst_of, src), t)
        else:
            t = V(lambda: dve.tensor_copy(dst_of, src), t)
        free[b] = [t]
        return t

    def attend(jobs, pbuf, ptbuf, att, sbase, banks, vbank):
        n = len(jobs)
        st = [dict() for _ in jobs]
        pf, ptf = [None] * 3, [None] * 2
        done = []

        def scores(i):
            tt, causal, heads, oc, ready = jobs[i]
            kw = 128 * (tt + 1) if causal else 256
            b = banks[i % 2]
            take(b)
            take(b + 1)
            P.wait("pe", *ready)
            ps = psum[:, b:b + 2, 0:kw]
            for h, (qT, kT, vv) in enumerate(heads):
                t = MMi(ps[:, h, :], qT(tt), kT(kw), True, not causal)
            if causal:
                for h in range(2):
                    t = MMi(ps[:, h, kw - 128:kw], identb[:], maskb[:], False, True, t_identb, t_mask)
            c = sbase + 8 * (i % 3)
            mx, nb, sm, rc = (small[:, c + 2 * q:c + 2 * q + 2] for q in range(4))
            t = V(lambda: dve.reduce_max(mx, ps, AX), t, st[i - 3]["fin"] if i >= 3 else None)
            t = V(lambda: dve.tensor_scalar(nb, mx, -0.125, None, ALU.mult), t)
            p = pbuf[:, i % 3, 0:2 * kw].rearrange("p (h k) -> p h k", h=2)
            P.wait("act", pf[i % 3])
            for h in range(2):
                te = C(lambda h=h: act.activation(p[:, h, :], ps[:, h, :], ACT.Exp, bias=nb[:, h:h + 1], scale=0.125,
                                                  accum_out=sm[:, h:h + 1]), t)
            free[b] = free[b + 1] = [te]
            st[i].update(p=p, kw=kw, sm=sm, rc=rc, te=te)

        def turn(i):
            s = st[i]
            nk = s["kw"] // 128
            b = banks[2 + i % 2]
            take(b)
            P.wait("pe", s["te"], t_ident)
            m = 2 * nk
            for j in range(m):
                f = lambda j=j: pe.transpose(bank[b][:, j * 128:(j + 1) * 128],
                                             s["p"][:, j // nk, (j % nk) * 128:(j % nk + 1) * 128], ident[:])
                if j == m - 1:
                    t = T(f)
                else:
                    P.quiet("pe", f)
            pf[i % 3] = t
            dst = ptbuf[:, i % 2, 0:m * 128]
            s["tr"] = V(lambda: dve.reciprocal(s["rc"], s["sm"]), s["te"])
            eng = V if i % 2 else C
            if i % 2:
                t = V(lambda: dve.tensor_copy(dst, bank[b][:, 0:m * 128]), t, ptf[i % 2])
            else:
                t = C(lambda: act.copy(dst, bank[b][:, 0:m * 128]), t, ptf[i % 2])
            free[b] = [t]
            s["pt"] = t

        def values(i):
            tt, causal, heads, oc, ready = jobs[i]
            s = st[i]
            nk = s["kw"] // 128
            b = vbank
            take(b)
            P.wait("pe", s["pt"])
            for h, (qT, kT, vv) in enumerate(heads):
                for k in range(nk):
                    l = ptbuf[:, i % 2, (h * nk + k) * 128:(h * nk + k + 1) * 128]
                    f = lambda l=l, h=h, k=k, vv=vv: pe.matmul(bank[b][:, h * 64:(h + 1) * 64], l, vv(k),
                                                               start=k == 0, stop=k == nk - 1,
                                                               skip_group_check=True)
                    if h == 1 and k == nk - 1:
                        t = T(f)
                    else:
                        P.quiet("pe", f)
            ptf[i % 2] = t
            o = att[:, tt, oc:oc + 128].rearrange("p (h d) -> p h d", h=2)
            src = bank[b][:, 0:128].rearrange("p (h d) -> p h d", h=2)
            t = V(lambda: dve.tensor_tensor(o, src, wide(s["rc"], 2, 64), ALU.mult), t, s["tr"])
            free[b] = [t]
            s["fin"] = t
            done.append(t)

        for i in range(n + 2):
            if i < n:
                scores(i)
            if 0 <= i - 1 < n:
                turn(i - 1)
            if 0 <= i - 2 < n:
                values(i - 2)
            yield done[-1] if done else None

    def dump(name, ap, *w):
        if name in dbg:
            t = load(dbg[name], ap, *w)
            dumps.append(t)
            for e in ("dve", "act", "pe", "pool"):
                P.wait(e, t)

    dumps = []
    DA = {k: A[k] for k in A}

    def plan_ffn(which, l):
        for p in range(FF // 256):
            slots_A(DA[which + "_w_gate"][l], 8, p * 256)
            slots_A(DA[which + "_w_up"][l], 8, p * 256)
        for p in range(4):
            slots_A(DA[which + "_w_down"][l], 22, p * 256)

    ain = DA["a_w_in"][0]
    win = DA["w_in_2"][0]
    plan_ffn("ffn1", 0)
    for p in range(3):
        slots_A(ain, 8, p * 256)
        slots_A(ain, 8, 768 + p * 256)
    slots_B(ain, 8, 1536, 256)
    for l in range(2):
        slots_B(DA["w_mem_kv"][l], 8, 0, 512)
    for p in range(4):
        slots_A(DA["w_o"][0], 8, p * 256)
    plan_ffn("ffn2", 0)
    for c in range(3):
        slots_B(DA["w_kv"], 8, c * 512, 512)
    plan_ffn("ffn1", 1)
    slots_B(DA["b_w_in"][0], 8, 0, D)
    for p in range(4):
        slots_A(DA["w_o"][1], 8, p * 256)
    plan_ffn("ffn2", 1)
    for c in range(4):
        slots_A(win, 8, 2048 + c * 256)
    plan.append((win, 0, 8, 4608, 8))
    for c in range(4):
        slots_A(win, 8, c * 256)
    slots_B(win, 8, 3072, 512)
    slots_B(win, 8, 1024, 512)
    for c0 in (1536, 3584, 4096):
        slots_B(win, 8, c0, 512)
    for c in range(8):
        slots_A(win, 8, 4616 + c * 256)
    for c in range(4):
        slots_A(DA["w_a_2"][0], 4, c * 256)
        slots_A(DA["w_b_2"][0], 4, c * 256)
    slots_B(DA["w_out_2"][0], 8, 0, D)

    LOWB = [[0, 1], [2, 3]]
    htmp = sb("htmp", [128, 2, 512])
    X0, X1 = (xh[0], xl[0], [[None, None]] * 8), (xh[1], xl[1], [[None, None]] * 8)
    X0, X1 = [(xh[i], xl[i], [[None, None] for _ in range(8)]) for i in range(2)]

    st0 = ExitStack()
    xn = sb("xn", [128, 2, D], F32, st0)
    grow = sb("grow", [8, D], F32, st0)
    t_x = [load(xn[:, tt, :], A["x"][0, tt * 128:(tt + 1) * 128, :]) for tt in range(2)]
    gains = [A["ffn1_norm_g"][0:1], A["mix_norm_g"][0:1], A["ffn2_norm_g"][0:1],
             A["kv_norm_g"].rearrange("(a d) -> a d", a=1), A["ffn1_norm_g"][1:2], A["mix_norm_g"][1:2],
             A["ffn2_norm_g"][1:2], A["norm_pre_2"][0:1]]
    t_gr = [load(grow[i:i + 1, :], g) for i, g in enumerate(gains)]
    thg = []
    for i, nm in enumerate(("mem_q_norm_g", "mem_k_norm_g")):
        for l in range(2):
            thg.append(load(hg[:, 2 * i + l, :], rows128(A[nm][l])))
    thg.append(load(hg[:, 4, :], rows128(A["k_norm_g"])))
    thg.append(load(hg[:, 5, :], rows128(A["b_q_norm_g"][0])))
    P.wait("pe", t_ident, *t_gr)
    for c in range(8):
        t = T(lambda: pe.transpose(bank[4][:, c * 8:(c + 1) * 8], grow[:, c * 128:(c + 1) * 128], ident[0:8, 0:8]))
    t_gcol = V(lambda: dve.tensor_copy(gcol[:].rearrange("p a b -> p (a b)"), bank[4][:, 0:64]), t)
    free[4] = [t_gcol]
    for p in range(4):
        P.wait("pe", *t_x)
        for j in range(2):
            for tt in range(2):
                c = 2 * p + j
                t = T(lambda: pe.transpose(bank[p][:, j * 256 + tt * 128:j * 256 + (tt + 1) * 128],
                                           xn[:, tt, c * 128:(c + 1) * 128], ident[:]))
        t = V(lambda: dve.tensor_copy(hT[:, 2 * p:2 * p + 2, :].rearrange("p a b -> p (a b)"), bank[p][:]), t)
        free[p] = [t]
        h_done[p] = t
        prep(p, [(0, X0, None)])
    N = norm(5)
    split_to(2)
    x_read = last_pe = ("pe_done", P.counts["pe_done"])
    st0.close()

    def run_ffn(which, l, x, N, targets):
        c = ExitStack()
        gh = sb(f"gh{which}{l}", [128, 22, S], F32R, c)
        gl = sb(f"gl{which}{l}", [128, 22, S], F32R, c)
        gr = sb(f"gr{which}{l}", [128, 2, 512], F32, c)
        pr = sb(f"pr{which}{l}", [128, 2, 512], F32, c)
        r = ffn(DA[which + "_w_gate"][l], DA[which + "_w_up"][l], DA[which + "_w_down"][l], x, N,
                (gh, gl, gr, pr), targets)
        c.close()
        return r

    P.wait("act", x_read)
    P.wait("dve", x_read)
    x0_last = run_ffn("ffn1", 0, X0, N, [(1, X0, None)])
    N = norm(4)
    dump("h1", hT[:], *h_done)

    mx = ExitStack()
    hc = sb("hc", [128, 6, 30 + S], F32, mx)
    cv = sb("cv", [128, 6, S], F32, mx)
    rows = sb("rows", [34, 768], F32, mx)
    taps = sb("taps", [128, 6, 34], F32, mx)
    sg = sb("sgm", [128, 2, 512], F32, mx)
    gr = sb("grm", [128, 2, 512], F32, mx)
    qm = sb("qm", [128, 2, 256], F32, mx)
    sq = sb("sqm", [128, 2, 256], F32, mx)
    qTm = sb("qTm", [128, 4, S], F32, mx)
    att = sb("attm", [128, 2, 256], F32, mx)
    stat = sg[:].rearrange("p a (b c) -> p (a b) c", b=2)
    scr = sb("scrm", [128, 5, 512], F32, mx)
    pbuf, ptbuf = scr[:, 0:3, :], scr[:, 3:5, :]
    xg = scr[:, 0:4, :].rearrange("p (t a) b -> p t (a b)", t=2)
    mem = sb("memt", [128, 2, D], F32, mx)
    gn = sb("gnm", [128, D], F32, mx)
    dgs = sb("dgs", [128, NDG, 128], F32, mx)
    ffn_last = pe_done[-1]
    for e in ("sp", "act", "dve", "pool"):
        P.wait(e, ffn_last)
    t_mem = load(mem[:], A["mem"][0].rearrange("(t p) d -> p t d", p=128))
    t_gn = load(gn[:], rows128(A["mem_norm_g"][0]))
    tr_ = [load(rows[0:31, :], A["a_dw_kernel"][0].rearrange("k a c -> k (a c)")),
           load(rows[31:32, :], A["a_dw_bias"]), load(rows[32:33, :], A["a_ln_g"]), load(rows[33:34, :], A["a_ln_b"])]
    tz = G(lambda: pool.memset(hc[:, :, 0:30], 0.0))
    tzq = G(lambda: pool.memset(qTm[:], 0.0))

    def load_taps():
        take(7)
        P.wait("pe", t_ident, *tr_)
        for c in range(6):
            t = T(lambda: pe.transpose(bank[7][:, c * 34:(c + 1) * 34], rows[:, c * 128:(c + 1) * 128],
                                       ident[0:34, 0:34]))
        st_["taps"] = V(lambda: dve.tensor_copy(taps[:].rearrange("p a b -> p (a b)"), bank[7][:, 0:204]), t)
        free[7] = [st_["taps"]]
    at_slot(3, load_taps)

    hcs = []
    dgt = []

    def diags(upto):
        while len(dgt) < min(upto, 31 * len(CONV_PE)):
            i = len(dgt)
            c, k = CONV_PE[i // 31], i % 31
            w = dgfree[i - NDG] if i >= NDG else None
            dgt.append(G(lambda: pool.tensor_scalar(dgs[:, i % NDG, :], ident[:], taps[:, c, k:k + 1], None, ALU.mult),
                         st_["taps"], w))
    dgfree = []

    def conv_dve(cs):
        for c2 in range(0, len(cs), 2):
            pair = cs[c2:c2 + 2]
            t = {}
            for k in range(31):
                for c in pair:
                    if k == 0:
                        t[c] = V(lambda: dve.tensor_scalar(cv[:, c, :], hc[:, c, 0:S], taps[:, c, 0:1],
                                                           taps[:, c, 31:32], ALU.mult, ALU.add),
                                 hcs[c // 2], st_["taps"], tz)
                    else:
                        t[c] = V(lambda: dve.scalar_tensor_tensor(out=cv[:, c, :], in0=hc[:, c, k:k + S],
                                                                  scalar=taps[:, c, k:k + 1], in1=cv[:, c, :],
                                                                  op0=ALU.mult, op1=ALU.add), t[c])
                    if k == 30:
                        tcv[c] = t[c]
                    yield

    def conv_pe(cs, b):
        for c in cs:
            take(b)
            P.wait("pe", hcs[c // 2], tz)
            for k in range(31):
                i = len(dgfree)
                t = MMi(bank[b][:, 0:S], dgs[:, i % NDG, :], hc[:, c, k:k + S], k == 0, k == 30, dgt[i])
                dgfree.append(t)
                diags(i + 1 + NDG)
                if k % 4 == 3:
                    yield
            tcv[c] = C(lambda: act.activation(cv[:, c, :], bank[b][:, 0:S], ACT.Identity, bias=taps[:, c, 31:32]), t)
            free[b] = [tcv[c]]
            yield

    def some(gen, n):
        for _ in range(n):
            next(gen, None)

    tcv = [None] * 6
    cd = conv_dve(CONV_DVE)
    sgf = [None, None]
    for p in range(3):
        ba, bg = (0, 1) if p % 2 == 0 else (2, 3)
        t1 = lin_A(X0, ain, 8, p * 256, ba)
        t2 = lin_A(X0, ain, 8, 768 + p * 256, bg)
        if p == 0:
            P.wait("pool", st_["taps"])
        r = gr[:, p % 2, :].rearrange("p (a b) -> p a b", a=2)
        s_ = sg[:, p % 2, :].rearrange("p (a b) -> p a b", a=2)
        b3 = lambda b: bank[b][:].rearrange("p (a b) -> p a b", a=2)
        tr = V(lambda: dve.tensor_tensor(r, b3(bg), wide(N.row, 1, 2), ALU.mult), t2, N.t_row, sgf[p % 2])
        free[bg] = [tr]
        ts = C(lambda: act.activation(s_, r, ACT.Sigmoid), tr, sgf[p % 2])
        ta = V(lambda: dve.tensor_tensor(r, b3(ba), wide(N.row, 1, 2), ALU.mult), ts, t1)
        free[ba] = [ta]
        row_free[N.i] = ta
        tm = V(lambda: dve.tensor_tensor(hc[:, 2 * p:2 * p + 2, 30:30 + S], s_, r, ALU.mult), ta, tz)
        sgf[p % 2] = tm
        hcs.append(tm)
        if p:
            some(cd, 10)
    diags(NDG)
    cp = conv_pe(CONV_PE, 7)
    tq = run(lin_B(X0, ain, 8, 1536, 256, [[5], [6]]))
    x0_last = tq
    tqs = []
    for tt in range(2):
        t = C(lambda: act.activation(qm[:, tt, :], bank[5 + tt][:, 0:256], ACT.Copy, scale=N.col[tt]), tq, N.t_col)
        free[5 + tt] = [t]
        tqs.append(t)
    some(cd, 8)

    rsm = row_stats(mem, t_mem, xg, None, 24)
    xg_free = rsm[1][1]
    x1_last = None
    tmk, tmv = [[], []], [[], []]
    mem_x = []

    def mem_norm(l, dst, xfree, xgf, tg):
        P.wait("dve", xfree)
        return from_rows(mem, t_mem, gn[:], tg, dst, LOWB, rsm, xg, xgf)

    def mem_kv(l, x, bk, each):
        for t in lin_B(x, DA["w_mem_kv"][l], 8, 0, 512, bk):
            each()
        for tt in range(2):
            b = bk[tt][0]
            t2 = C(lambda: act.copy(mkv[l][:, tt, :], bank[b][:]), t)
            free[b] = [t2]
            tmv[l].append(t2)
            t3 = head_rms(mkv[l][:, tt, 0:256], 4, 32 + 64 * tt, hg[:, 2 + l, :], thg[2 + l],
                          mkv[l][:, tt, 0:256], [t2], sq[:, tt, :])
            tmk[l].append(plain_T(lambda j: mkv[l][:, tt, j * 128:(j + 1) * 128], 2,
                                  kTm[l][:, :, tt * 128:(tt + 1) * 128], [t3], bk[tt][0]))

    t = mem_norm(0, X1, None, xg_free, t_gn)
    t_gn = load(gn[:], rows128(A["mem_norm_g"][1]), t)
    some(cd, 16)
    some(cp, 8)
    mem_kv(0, X1, [[4], [5]], lambda: (some(cd, 6), some(cp, 1)))
    x1_last = pe_done[-1]
    t = mem_norm(1, X0, x0_last, t, t_gn)
    some(cp, 8)

    def mem_jobs(l, qTp, ready, oc0):
        jobs = []
        for tt in range(2):
            for c in range(2):
                heads = []
                for h in range(2):
                    heads.append((lambda tt, c=c, h=h: qTp[:, 2 * c + h, tt * 128:(tt + 1) * 128],
                                  lambda kw, c=c: kTm[l][:, c, :],
                                  lambda k, c=c, h=h: mkv[l][:, k, 256 + (2 * c + h) * 64:256 + (2 * c + h + 1) * 64]))
                jobs.append((tt, False, heads, oc0 + c * 128, ready + tmk[l] + tmv[l]))
        return jobs

    tqT = []
    for tt in range(2):
        t = head_rms(qm[:, tt, :], 4, 32 + 64 * tt, hg[:, 0, :], thg[0], qm[:, tt, :], [tqs[tt]], sq[:, tt, :])
        tqT.append(padded_T(lambda j: qm[:, tt, j * 128:(j + 1) * 128], 2, qTm, 0, tt, [t, tzq], 6))
        some(cd, 10)
    for t in attend(mem_jobs(0, qTm, tqT, 0), pbuf, ptbuf, att, 160, [0, 2, 4, 6], 5):
        some(cd, 6)
        some(cp, 3)
    tatt = t
    some(cd, 500)
    some(cp, 500)
    XS = X1
    P.wait("act", x1_last)
    P.wait("dve", x1_last)
    for tt in range(2):
        to_T(lambda c: att[:, tt, c * 128:(c + 1) * 128], 2, XS, 6, [tatt], [tt], tt)

    take(2)
    for c in range(6):
        t = MMi(bank[2][:, 0:S], ln1[:], cv[:, c, :], c == 0, c == 5, t_ln1, tcv[c])
    gm = lin_B(X0, DA["w_mem_kv"][1], 8, 0, 512, [[4], [5]])
    next(gm)
    tm = C(lambda: act.copy(stat[:, 0, :], bank[2][:, 0:S]), t)
    free[2] = [tm]
    t = V(lambda: dve.tensor_tensor(cv[:], cv[:], wide(stat[:, 0, :], 1, 6), ALU.subtract), tm, *tcv)
    hcv = hc[:, :, 0:S]
    ts = C(lambda: act.activation(hcv, cv[:], ACT.Square), t)
    take(3)
    for c in range(6):
        t2 = MMi(bank[3][:, 0:S], ln1[:], hcv[:, c, :], c == 0, c == 5, ts)
    next(gm)
    t2 = V(lambda: dve.tensor_scalar(stat[:, 1, :], bank[3][:, 0:S], EPS, None, ALU.add), t2)
    free[3] = [t2]
    t3 = C(lambda: act.activation(stat[:, 2, :], stat[:, 1, :], ACT.Sqrt), t2)
    t3 = V(lambda: dve.reciprocal(stat[:, 3, :], stat[:, 2, :]), t3)
    t3 = V(lambda: dve.tensor_tensor(stat[:, 2, :], stat[:, 3, :], stat[:, 3, :], ALU.mult), t3)
    t3 = V(lambda: dve.tensor_tensor(stat[:, 2, :], stat[:, 2, :], stat[:, 1, :], ALU.mult), t3)
    t3 = V(lambda: dve.tensor_scalar(stat[:, 2, :], stat[:, 2, :], -0.5, 1.5, ALU.mult, ALU.add), t3)
    t3 = V(lambda: dve.tensor_tensor(stat[:, 3, :], stat[:, 3, :], stat[:, 2, :], ALU.mult), t3)
    for c in range(6):
        u3 = V(lambda: dve.tensor_tensor(cv[:, c, :], cv[:, c, :], stat[:, 3, :], ALU.mult), t3)
        t4 = C(lambda: act.activation(cv[:, c, :], cv[:, c, :], ACT.Silu, bias=taps[:, c, 33:34],
                                      scale=taps[:, c, 32:33]), u3)
        t5 = C(lambda: act.copy(XS[0][:, c, :], cv[:, c, :]), t4)
        t6 = V(lambda: dve.tensor_tensor(XS[1][:, c, :], cv[:, c, :], XS[0][:, c, :].bitcast(F32), ALU.subtract), t5)
        XS[2][c] = [t5, t6]
    for tg_ in gm:
        pass
    x0_last = pe_done[-1]
    dump("prim", cv[:], t4)
    dump("mo", att[:], tatt)
    for p in range(4):
        t = lin_A(XS, DA["w_o"][0], 8, p * 256, p)
        if p == 0:
            for tt in range(2):
                t2 = C(lambda: act.copy(mkv[1][:, tt, :], bank[4 + tt][:]), tg_)
                free[4 + tt] = [t2]
                tmv[1].append(t2)
                t3 = head_rms(mkv[1][:, tt, 0:256], 4, 32 + 64 * tt, hg[:, 3, :], thg[3],
                              mkv[1][:, tt, 0:256], [t2], sq[:, tt, :])
                tmk[1].append((tt, t3))
        if p == 1:
            tmk[1] = [plain_T(lambda j: mkv[1][:, tt, j * 128:(j + 1) * 128], 2,
                              kTm[1][:, :, tt * 128:(tt + 1) * 128], [t3], 6) for tt, t3 in tmk[1]]
        add_h(p, p, t, 1.0, None, [(2, X0, x0_last)], None, None)
    x1_last = pe_done[-1]
    N = norm(4)
    mx.close()
    dump("h2", hT[:], *h_done)
    for e in ("dve", "act", "sp"):
        P.wait(e, x1_last, ("act_done", P.counts["act_done"]) if e == "dve" else ("dve_done", P.counts["dve_done"]),
               *dumps)

    x0_last = run_ffn("ffn2", 0, X0, N, [(3, X1, x1_last), (4, X0, None)])
    N = norm(4)
    dump("h3", hT[:], *h_done)

    kv = ExitStack()
    kT = sb("kT", [128, 6, S], F32, kv)
    vn = sb("vn", [128, 2, 768], F32, kv)
    cs = sb("cs", [128, 2, 2, 8], F32, kv)
    tk = ExitStack()
    kn = sb("kn", [128, 2, 768], F32, tk)
    posi = sb("posi", [128, 2, 1], I32, tk)
    posf = sb("posf", [128, 2], F32, tk)
    freq = sb("freq", [128, 8], F32, tk)
    ang = sb("ang", [128, 2, 2, 8], F32, tk)
    rd = sb("rd", [128, 2, 2, 8], F32, tk)
    rtmp = sb("rtmp", [128, 2, 4, 96], F32, tk)
    sqk = sb("sqk", [128, 2, 768], F32, tk)
    ffn_last = pe_done[-1]
    for e in ("act", "dve", "pool", "sp"):
        P.wait(e, ffn_last)

    t = load(posi[:], A["positions"][0].rearrange("(t p o) -> p t o", p=128, o=1), slow=True)
    t = V(lambda: dve.tensor_copy(posf[:], posi[:, :, 0]), t)
    fr = (1.0 / (np.float32(500000.0) ** (np.arange(0, 16, 2, dtype=np.float32) / np.float32(16)))).astype(np.float32)
    for i in range(8):
        tf = G(lambda: pool.memset(freq[:, i:i + 1], float(fr[i])))
    for tt in range(2):
        t = V(lambda: dve.tensor_scalar(ang[:, tt, 1, :], freq[:], posf[:, tt:tt + 1], None, ALU.mult), t, tf)
    c1, left = 6.28125, 2 * np.pi - 6.28125
    c2 = float(np.float32(round(left * 2 ** 19) / 2 ** 19))
    c3 = float(np.float32(left - c2))
    magic = 12582912.0
    a1 = ang[:, :, 1, :]
    k1 = rd[:, :, 1, :]
    t = V(lambda: dve.tensor_scalar(k1, a1, float(1 / (2 * np.pi)), magic, ALU.mult, ALU.add), t)
    t = V(lambda: dve.tensor_scalar(k1, k1, -magic, None, ALU.add), t)
    for c in (c1, c2, c3):
        t = V(lambda: dve.scalar_tensor_tensor(out=a1, in0=k1, scalar=-c, in1=a1, op0=ALU.mult, op1=ALU.add), t)
    a0 = ang[:, :, 0, :]
    k0 = rd[:, :, 0, :]
    t = V(lambda: dve.tensor_scalar(a0, a1, float(np.pi / 2), None, ALU.add), t)
    t = V(lambda: dve.tensor_scalar(k0, a0, float(np.pi), None, ALU.is_gt), t)
    t = V(lambda: dve.scalar_tensor_tensor(out=a0, in0=k0, scalar=-float(2 * np.pi), in1=a0, op0=ALU.mult,
                                           op1=ALU.add), t)
    t = V(lambda: dve.tensor_scalar(ang[:], ang[:], 3.1415925, -3.1415925, ALU.min, ALU.max), t)
    t_cs = C(lambda: act.activation(cs[:], ang[:], ACT.Sin), t)

    def rope(x, tt, nh, tmp, t):
        v = x.rearrange("p (h d) -> p h d", d=64)
        x1, x2 = v[:, :, 0:8], v[:, :, 8:16]
        co = wide(cs[:, tt, 0, :], 1, nh)
        si = wide(cs[:, tt, 1, :], 1, nh)
        m = [tmp[:, i, :].rearrange("p (h d) -> p h d", d=8) for i in range(4)]
        for o, a, b in ((m[0], x1, co), (m[1], x2, si), (m[2], x2, co), (m[3], x1, si)):
            u = V(lambda: dve.tensor_tensor(o, a, b, ALU.mult), t, t_cs)
        V(lambda: dve.tensor_tensor(x1, m[0], m[1], ALU.subtract), u)
        return V(lambda: dve.tensor_tensor(x2, m[2], m[3], ALU.add), u)

    tkv = []
    t = run(lin_B(X1, DA["w_kv"], 8, 0, 512, [[5], [6]]))
    for tt in range(2):
        tkv.append(C(lambda: act.activation(kn[:, tt, 0:512], bank[5 + tt][:], ACT.Copy, scale=N.col[tt]), t, N.t_col))
        free[5 + tt] = [tkv[-1]]
    t = run(lin_B(X1, DA["w_kv"], 8, 512, 512, [[7], [4]]))
    for tt, b in enumerate((7, 4)):
        tkv.append(V(lambda: dve.tensor_scalar(kn[:, tt, 512:768], bank[b][:, 0:256], N.col[tt], None, ALU.mult),
                     t, N.t_col))
        u = V(lambda: dve.tensor_scalar(vn[:, tt, 0:256], bank[b][:, 256:512], N.col[tt], None, ALU.mult), t)
        free[b] = [tkv[-1], u]
    t = run(lin_B(X1, DA["w_kv"], 8, 1024, 512, [[5], [6]]))
    x1_last = t
    for tt in range(2):
        t_vn = V(lambda: dve.tensor_scalar(vn[:, tt, 256:768], bank[5 + tt][:], N.col[tt], None, ALU.mult), t)
        free[5 + tt] = [t_vn]
    tkT = []
    tkr = []
    for tt in range(2):
        t = head_rms(kn[:, tt, :], 12, 32 + 64 * tt, hg[:, 4, :], thg[4], kn[:, tt, :], tkv, sqk[:, tt, :])
        tkr.append(rope(kn[:, tt, :], tt, 12, rtmp[:, tt], t))

    def k_turn():
        for tt in range(2):
            tkT.append(plain_T(lambda j: kn[:, tt, j * 128:(j + 1) * 128], 4,
                               kT[:, 0:4, tt * 128:(tt + 1) * 128], [tkr[tt]], 4))
            tkT.append(plain_T(lambda j: kn[:, tt, (4 + j) * 128:(5 + j) * 128], 2,
                               kT[:, 4:6, tt * 128:(tt + 1) * 128], [tkr[tt]], 5))
        for e in ("dve", "act", "sp"):
            P.wait(e, tkT[-1], tkr[-1], *dumps)
    k_turn()
    dump("kn", kn[:], tkr[-1])
    dump("vn", vn[:], t_vn)
    P.wait("dve", *dumps)
    P.wait("act", *dumps)
    tk.close()

    x0_last = run_ffn("ffn1", 1, X0, N, [(5, X0, None)])
    N = norm(7, (1, 2))
    dump("h4", hT[:], *h_done)
    mx = ExitStack()
    qn = sb("qn", [128, 2, D], F32, mx)
    rtmp = sb("rtmp1", [128, 2, 4, 96], F32, mx)
    sq = sb("sqq", [128, 2, D], F32, mx)
    qT = sb("qT", [128, 16, S], F32, mx)
    att = sb("att1", [128, 2, D], F32, mx)
    pbuf = sb("pb1", [128, 3, 512], F32, mx)
    ptbuf = sb("pt1", [128, 2, 512], F32, mx)
    ffn_last = pe_done[-1]
    for e in ("act", "dve", "pool", "sp"):
        P.wait(e, ffn_last)
    tzq = G(lambda: pool.memset(qT[:], 0.0))
    BQ = [[0, 1], [2, 3]]
    t = run(lin_B(X0, DA["b_w_in"][0], 8, 0, D, BQ))
    x0_last = t
    tqT = []
    rp = []
    for tt in range(2):
        u = C(lambda: act.activation(qn[:, tt, 0:512], bank[BQ[tt][0]][:], ACT.Copy, scale=N.col[tt]), t, N.t_col)
        w = V(lambda: dve.tensor_scalar(qn[:, tt, 512:1024], bank[BQ[tt][1]][:], N.col[tt], None, ALU.mult), t, N.t_col)
        free[BQ[tt][0]], free[BQ[tt][1]] = [u], [w]
        rp.append((u, w))
    for tt in range(2):
        u, w = rp[tt]
        v1 = head_rms(qn[:, tt, 0:768], 12, 32 + 64 * tt, hg[:, 5, :], thg[5], qn[:, tt, 0:768], [u, w], sq[:, tt, 0:768])
        v1 = rope(qn[:, tt, 0:768], tt, 12, rtmp[:, tt], v1)
        v2 = head_rms(qn[:, tt, 768:], 4, 44 + 64 * tt, hg[:, 1, :], thg[1], qn[:, tt, 768:], [w], sq[:, tt, 768:])
        tqT.append([padded_T(lambda j: qn[:, tt, (j0 + j) * 128:(j0 + j + 1) * 128], 4, qT, j0, tt,
                             [v1, v2, tzq], 4 + tt * 2 + j0 // 4) for j0 in (0, 4)][-1])
    dump("qn", qn[:], v1, v2)
    jobs = []
    for tt in range(2):
        for c in range(6):
            heads = [(lambda tt, c=c, h=h: qT[:, 2 * c + h, tt * 128:(tt + 1) * 128],
                      lambda kw, c=c: kT[:, c, 0:kw],
                      lambda k, c=c, h=h: vn[:, k, (2 * c + h) * 64:(2 * c + h + 1) * 64]) for h in range(2)]
            jobs.append((tt, True, heads, c * 128, [tqT[tt], t_vn] + tkT))
        jobs += [j for j in mem_jobs(1, qT[:, 12:16, :], [tqT[tt]], 768) if j[0] == tt]
    P.wait("act", x1_last)
    P.wait("dve", x1_last)
    ga_ = attend(jobs, pbuf, ptbuf, att, 160, [0, 2, 4, 6], 5)
    for n_, tatt in enumerate(ga_):
        if n_ == 11:
            to_T(lambda c: att[:, 0, c * 128:(c + 1) * 128], 8, X1, 0, [tatt], [7], 0)
    dump("att", att[:], tatt)
    to_T(lambda c: att[:, 1, c * 128:(c + 1) * 128], 8, X1, 0, [tatt], [0, 1], 1)
    for p in range(4):
        t = lin_A(X1, DA["w_o"][1], 8, p * 256, [2, 3, 4, 5][p])
        add_h(p, [2, 3, 4, 5][p], t, 1.0, None, [(6, X0, x0_last)], None, None)
    x1_last = pe_done[-1]
    N = norm(6)
    mx.close()
    kv.close()
    for e in ("act", "dve", "pool", "sp"):
        P.wait(e, t, *dumps)
    dump("h5", hT[:], *h_done)

    x0_last = run_ffn("ffn2", 1, X0, N, [(7, X0, None)])
    N = norm(4)
    dump("h6", hT[:], *h_done)

    mx = ExitStack()
    va = sb("va", [128, 2, 512], F32, mx)
    vb = sb("vb", [128, 2, 512], F32, mx)
    zob = sb("zob", [128, 3, 2, 512], F32, mx)
    qk = sb("qk", [128, 8, 3 + S], F32, mx)
    qkc = sb("qkc", [128, 8, S], F32, mx)
    aq = sb("aq", [128, 8, S], F32, mx)
    ak = sb("ak", [128, 4, S], F32, mx)
    ctap = sb("ctap", [128, 8, 4], F32, mx)
    lam = sb("lam", [128, 8], F32, mx)
    gt = sb("gt", [128, 2, 8], F32, mx)
    gates = sb("gates", [128, 2, 64], F32, mx)
    bif = sb("bif", [128, 8], F32, mx)
    oa = sb("oa", [128, 2, 512], F32, mx)
    ob = sb("ob", [128, 2, 512], F32, mx)
    pbuf = sb("pb2", [128, 3, 512], F32, mx)
    ptbuf = sb("pt2", [128, 2, 256], F32, mx)
    crow = pbuf[0:4, 0:2, :].rearrange("p a b -> p (a b)")
    lamr = ptbuf[:, 0, :].rearrange("p (a d) -> p a d", a=4)
    ga_t = qk[:].rearrange("p a b -> p (a b)")[:, 0:2048].rearrange("p (a b) -> p a b", b=S)
    gb_t = aq
    nab = va
    wd = diag
    ffn_last = pe_done[-1]
    for e in ("act", "dve", "pool", "sp"):
        P.wait(e, ffn_last)

    t_crow = load(crow, A["conv_qk_2"][0])
    t_lam = load(ptbuf[:, 0, :],
                 rows128(A["lambda_qk_2"].rearrange("a b d -> (a b d)")))
    t_bif = load(bif[:], rows128(A["b_if_2"][0]))
    tz = G(lambda: pool.memset(qk[:, :, 0:3], 0.0))
    tzq = G(lambda: pool.memset(aq[:], 0.0))

    def load_ctap():
        take(5)
        P.wait("pe", t_crow)
        for c in range(8):
            t = T(lambda: pe.transpose(bank[5][:, c * 4:(c + 1) * 4], crow[:, c * 128:(c + 1) * 128], ident[0:4, 0:4]))
        st_["ctap"] = V(lambda: dve.tensor_copy(ctap[:].rearrange("p a b -> p (a b)"), bank[5][:, 0:32]), t)
        free[5] = [st_["ctap"]]
        st_["pf0"] = t
    at_slot(3, load_ctap)

    tcv4 = [None] * 8

    def conv4():
        for c2 in range(0, 8, 2):
            t = {}
            for k in range(4):
                for c in (c2, c2 + 1):
                    if k == 0:
                        t[c] = V(lambda: dve.tensor_scalar(qkc[:, c, :], qk[:, c, 0:S], ctap[:, c, 0:1], None,
                                                           ALU.mult), tqk[c // 2], st_["ctap"], tz)
                    else:
                        t[c] = V(lambda: dve.scalar_tensor_tensor(
                            out=qkc[:, c, :], in0=qk[:, c, k:k + S], scalar=ctap[:, c, k:k + 1], in1=qkc[:, c, :],
                            op0=ALU.mult, op1=ALU.add), t[c])
                    tcv4[c] = t[c]
                    yield

    def scaled(o, b, t, q=slice(0, 128)):
        return V(lambda: dve.tensor_tensor(o, bank[b][q, :].rearrange("p (a n) -> p a n", a=2),
                                           wide(N.row[q], 1, 2), ALU.mult), t, N.t_row)

    tqk = []
    cg = conv4()
    tl_ = []
    for c in range(5):
        if c < 4:
            tl_.append(lin_A(X0, win, 8, 2048 + c * 256, c))
        if c > 0:
            t = scaled(qk[:, 2 * c - 2:2 * c, 3:3 + S], c - 1, tl_[c - 1])
            free[c - 1] = [t]
            tqk.append(t)
            some(cg, 8)

    l12 = lamr[:, 0:3:2, :]
    t = V(lambda: dve.tensor_tensor(l12, l12, lamr[:, 1:4:2, :], ALU.mult), t_lam)
    t = V(lambda: dve.reduce_sum(lam[:, 0:2], l12, AX), t)
    t = C(lambda: act.activation(lam[:, 2:4], lam[:, 0:2], ACT.Exp), t)
    t = V(lambda: dve.tensor_tensor(lam[:, 4:5], lam[:, 3:4], lam[:, 2:3], ALU.subtract), t)
    lam_init = 0.8 - 0.6
    t_lamn = V(lambda: dve.tensor_scalar(lam[:, 5:6], lam[:, 4:5], -lam_init, None, ALU.add), t)

    take(6)
    take(5)
    s = next_slot((0, 8, 4608, 8))
    P.wait("pe", s.th, s.tl)
    for tt in range(2):
        b = 5 + tt
        for k in range(8):
            l = [X0[i][:, k, tt * 128:(tt + 1) * 128] for i in range(2)]
            o = bank[b][:, 0:8]
            MM(o, l[0], s.hi[:, k, :], k == 0, False)
            MM(o, l[1], s.hi[:, k, :], False, False)
            t = T(lambda: pe.matmul(o, l[0], s.lo[:, k, :], start=False, stop=k == 7, skip_group_check=True), sem="w")
        u = V(lambda: dve.scalar_tensor_tensor(out=gt[:, tt, :], in0=bank[b][:, 0:8], scalar=N.col[tt], in1=bif[:],
                                               op0=ALU.mult, op1=ALU.add), t, t_bif, N.t_col)
        free[b] = [u]
    pe_done.append(t)
    t_gt = u

    taT = []
    for c in range(4):
        b = c
        t = lin_A(X0, win, 8, c * 256, b)
        if c < 2:
            for e in range(2):
                q = slice(64 * e, 64 * e + 64)
                u = scaled(aq[q, 4 * c + e:4 * c + e + 3:2, :], b, t, q)
                P.wait("dve", tzq)
        else:
            u = scaled(ak[:, 2 * c - 4:2 * c - 2, :], b, t)
        free[b] = [u]
        taT.append(u)
    some(cg, 100)
    tcc = []
    for h in range(2):
        tcc.append(C(lambda: act.activation(qkc[:, 4 * h:4 * h + 4, :], qkc[:, 4 * h:4 * h + 4, :], ACT.Silu),
                     tcv4[4 * h + 3], tcv4[4 * h + 2]))
    tcc.append(V(lambda: dve.tensor_scalar(qkc[:, 4:8, :], qkc[:, 4:8, :], 128.0 ** -0.5, None, ALU.mult), tcc[1]))

    fg = gt[:, :, 4:8]
    e1 = gates[:, :, 0:4]
    e2 = gates[:, :, 4:8]
    lf = gates[:, :, 8:12]
    Fc = gates[:, :, 12:16]
    w_ = gates[:, :, 16:20]
    t = V(lambda: dve.tensor_scalar(e1, fg, -1.0, None, ALU.mult), t_gt)
    t = V(lambda: dve.tensor_tensor(e1, e1, fg, ALU.min), t)
    t = C(lambda: act.activation(e2, e1, ACT.Exp), t)
    t = C(lambda: act.activation(e2, e2, ACT.Ln, bias=1.0), t)
    u = V(lambda: dve.tensor_scalar(lf, fg, 0.0, None, ALU.min), t_gt)
    t_lf = V(lambda: dve.tensor_tensor(lf, lf, e2, ALU.subtract), t, u)

    gv = lin_B(X0, win, 8, 3072, 512, [[5], [6]])
    next(gv)
    take(4)
    MM(bank[4][:, 0:4], upper[:], gates[:, 0, 8:12], True, True, t_lf, t_upper)
    MM(bank[4][:, 4:8], ones[:], gates[:, 0, 8:12], True, False)
    t = MMi(bank[4][:, 4:8], upper[:], gates[:, 1, 8:12], False, True)
    t = V(lambda: dve.tensor_copy(Fc, bank[4][:, 0:8].rearrange("p (a b) -> p a b", a=2)), t)
    free[4] = [t]
    t_w = V(lambda: dve.tensor_tensor(w_, gt[:, :, 0:4], Fc, ALU.subtract), t)
    dump("F", gates[:], t_w)
    for t in gv:
        pass
    for tt in range(2):
        u = V(lambda: dve.tensor_scalar(vb[:, tt, :], bank[5 + tt][:], N.col[tt], None, ALU.mult), t, N.t_col)
        free[5 + tt] = [u]
    t_vb = u
    t = run(lin_B(X0, win, 8, 1024, 512, [[4], [7]]))
    for tt, b in enumerate((4, 7)):
        u = V(lambda: dve.tensor_scalar(va[:, tt, :], bank[b][:], N.col[tt], None, ALU.mult), t, N.t_col)
        free[b] = [u]
    t_va = u

    tzo = []
    tgab = []

    def rest():
        for i, c0 in enumerate((1536, 3584, 4096)):
            for t in lin_B(X0, win, 8, c0, 512, [[6], [7]]):
                yield
            for tt in range(2):
                u = V(lambda: dve.tensor_scalar(zob[:, i, tt, :], bank[6 + tt][:], N.col[tt], None, ALU.mult), t)
                free[6 + tt] = [u]
            tzo.append(u)
        for c in range(8):
            b = 6 + c % 2
            t = lin_A(X0, win, 8, 4616 + c * 256, b)
            g_ = ga_t if c < 4 else gb_t
            u = scaled(g_[:, 2 * (c % 4):2 * (c % 4) + 2, :], b, t)
            free[b] = [u]
            tgab.append(u)
            yield
    rg = rest()

    st = [dict() for _ in range(8)]
    pf, ptf = [st_["pf0"]] * 3, [None] * 2
    toa = []

    def d_scores(i):
        tt, h = i // 4, i % 4
        kw = 128 * (tt + 1)
        b = 2 * (i % 2)
        take(b)
        take(b + 1)
        P.wait("pe", t_alib, t_identb, *taT)
        ps = psum[:, b:b + 2, 0:kw]
        for c in range(2):
            MM(ps[:, c, :], aq[:, 2 * h + c, tt * 128:(tt + 1) * 128], ak[:, h, 0:kw], True, False)
            t = MMi(ps[:, c, :], identb[:], alib[:, tt, h, 0:kw], False, True)
        col0 = 160 + 12 * (i % 3)
        mx_, nb, sm, rc = (small[:, col0 + 2 * q:col0 + 2 * q + 2] for q in range(4))
        t = V(lambda: dve.reduce_max(mx_, ps, AX), t, st[i - 3]["fin"] if i >= 3 else None)
        t = V(lambda: dve.tensor_scalar(nb, mx_, -0.125, None, ALU.mult), t)
        p = pbuf[:, i % 3, 0:2 * kw].rearrange("p (c k) -> p c k", c=2)
        for c in range(2):
            te = C(lambda: act.activation(p[:, c, :], ps[:, c, :], ACT.Exp, bias=nb[:, c:c + 1], scale=0.125,
                                          accum_out=sm[:, c:c + 1]), t, pf[i % 3])
        free[b] = free[b + 1] = [te]
        t = V(lambda: dve.reciprocal(rc, sm), te)
        t = V(lambda: dve.tensor_scalar(rc[:, 1:2], rc[:, 1:2], lam[:, 5:6], None, ALU.mult), t, t_lamn)
        t = V(lambda: dve.tensor_scalar(p[:, 1, :], p[:, 1, :], rc[:, 1:2], None, ALU.mult), t)
        t = V(lambda: dve.scalar_tensor_tensor(out=p[:, 0, :], in0=p[:, 0, :], scalar=rc[:, 0:1], in1=p[:, 1, :],
                                               op0=ALU.mult, op1=ALU.add), t)
        st[i].update(p=p[:, 0, :], tp=t, kw=kw)

    def pv_turn(st, i):
        s = st[i]
        nk = s["kw"] // 128
        take(4)
        P.wait("pe", s["tp"])
        for k in range(nk):
            t = T(lambda: pe.transpose(bank[4][:, k * 128:(k + 1) * 128], s["p"][:, k * 128:(k + 1) * 128], ident[:]))
        pf[i % 3] = t
        s["pt"] = C(lambda: act.copy(ptbuf[:, i % 2, 0:nk * 128], bank[4][:, 0:nk * 128]), t, ptf[i % 2])
        free[4] = [s["pt"]]

    def pv_values(st, i, v, tv, b):
        h = i % 4
        s = st[i]
        nk = s["kw"] // 128
        take(b)
        P.wait("pe", s["pt"], tv)
        for k in range(nk):
            t = T(lambda: pe.matmul(bank[b][:, 0:128], ptbuf[:, i % 2, k * 128:(k + 1) * 128],
                                    v[:, k, h * 128:(h + 1) * 128], start=k == 0, stop=k == nk - 1,
                                    skip_group_check=True))
        ptf[i % 2] = t
        return t

    def diff():
        for i in range(10):
            if i < 8:
                d_scores(i)
            if 0 <= i - 1 < 8:
                pv_turn(st, i - 1)
            if 0 <= i - 2 < 8:
                j = i - 2
                t = pv_values(st, j, va, t_va, 5)
                u = V(lambda: dve.tensor_copy(oa[:, j // 4, (j % 4) * 128:(j % 4 + 1) * 128], bank[5][:, 0:128]), t)
                free[5] = [u]
                st[j]["fin"] = u
                toa.append(u)
            yield
    for _ in diff():
        next(rg, None)
    dump("oa", oa[:], toa[-1])
    t_na = load(nab[:, 0, :], rows128(A["norm_a_2"][0]), toa[-1])
    t_nb = load(nab[:, 1, :], rows128(A["norm_b_2"][0]), toa[-1])

    st2 = [dict() for _ in range(8)]
    tob = []
    wdf = [None, None]

    def m_scores(i):
        tt, h = i // 4, i % 4
        kw = 128 * (tt + 1)
        b = i % 3
        td = []
        for k in range(tt + 1):
            td.append(V(lambda: dve.tensor_scalar(wd[:, k, :], ident[:], gates[:, k, 16 + h:17 + h], None, ALU.mult),
                        t_w, wdf[k], t_ident))
        take(b)
        P.wait("pe", *tcc)
        MM(bank[b][:, 0:kw], qkc[:, h, tt * 128:(tt + 1) * 128], qkc[:, 4 + h, 0:kw], True, False)
        for k in range(tt + 1):
            t = MMi(bank[b][:, kw + k * 128:kw + (k + 1) * 128], ones[:], wd[:, k, :], False, False, td[k], t_ones)
            wdf[k] = t
        t = MMi(bank[b][:, 2 * kw - 128:2 * kw], identb[:], maskb[:], False, True)
        wr = bank[b][:, kw:2 * kw]
        col0 = 160 + 12 * (i % 3)
        M, nM, e, den, r = (small[:, col0 + q:col0 + q + 1] for q in range(5))
        t = V(lambda: dve.reduce_max(M, wr, AX), t, st2[i - 3]["fin"] if i >= 3 else None)
        t = V(lambda: dve.tensor_scalar(nM, M, 0.0, -1.0, ALU.max, ALU.mult), t)
        p = pbuf[:, i % 3, 0:2 * kw].rearrange("p (c k) -> p c k", c=2)
        te = C(lambda: act.activation(p[:, 1, :], wr, ACT.Exp, bias=nM), t, pf[i % 3])
        tF = V(lambda: dve.tensor_tensor(e, nM, gates[:, tt, 12 + h:13 + h], ALU.subtract), t)
        tF = C(lambda: act.activation(e, e, ACT.Exp), tF)
        t = V(lambda: dve.tensor_tensor(p[:, 0, :], bank[b][:, 0:kw], p[:, 1, :], ALU.mult), te, pf[i % 3])
        free[b] = [te, t]
        st2[i].update(p=p[:, 0, :], tp=t, kw=kw)
        t = V(lambda: dve.reduce_sum(den, p[:, 0, :], AX), t)
        t = V(lambda: dve.tensor_scalar(M, den, -1.0, None, ALU.mult), t)
        t = V(lambda: dve.tensor_tensor(den, den, M, ALU.max), t)
        t = V(lambda: dve.tensor_tensor(den, den, e, ALU.max), t, tF)
        t = V(lambda: dve.reciprocal(r, den), t)
        st2[i].update(r=r, tr=t)

    def mlstm():
        for i in range(10):
            if i < 8:
                m_scores(i)
            if 0 <= i - 1 < 8:
                pv_turn(st2, i - 1)
            if 0 <= i - 2 < 8:
                j = i - 2
                t = pv_values(st2, j, vb, t_vb, 5)
                u = V(lambda: dve.tensor_scalar(ob[:, j // 4, (j % 4) * 128:(j % 4 + 1) * 128],
                                                bank[5][:, 0:128], st2[j]["r"], None, ALU.mult), t, st2[j]["tr"])
                free[5] = [u]
                st2[j]["fin"] = u
                tob.append(u)
            yield
    for _ in mlstm():
        next(rg, None)
    dump("ob", ob[:], tob[-1])
    for _ in rg:
        pass

    f1 = lambda i: zob[:, i].rearrange("p a b -> p (a b)")
    tsg = C(lambda: act.activation(f1(1), f1(1), ACT.Sigmoid), tzo[1])
    tsa = C(lambda: act.activation(f1(0), f1(0), ACT.Silu), tzo[0])
    tsb = C(lambda: act.activation(f1(2), f1(2), ACT.Silu), tzo[2])
    tgs = []
    for c in range(4):
        v = (ga_t if c < 2 else gb_t)[:, 4 * (c % 2):4 * (c % 2) + 4, :]
        tgs.append(C(lambda: act.activation(v, v, ACT.Sigmoid), tgab[2 * c + 1], tgab[2 * c]))
    sqs = qkc[:].rearrange("p a b -> p (a b)")

    def head128(x, z, ng, tng, mul, ready, tz_, c0):
        v = x.rearrange("p (g d) -> p g d", d=128)
        q = sqs[:, 0:1024].rearrange("p (g d) -> p g d", d=128)
        ss, r_ = small[:, c0:c0 + 8], small[:, c0 + 8:c0 + 16]
        t = V(lambda: dve.tensor_tensor(q, v, v, ALU.mult), *ready)
        t = V(lambda: dve.reduce_sum(ss, q, AX), t)
        t = rstd_of(ss, r_, 128, t, 8)
        if mul != 1.0:
            t = V(lambda: dve.tensor_scalar(r_, r_, mul, None, ALU.mult), t)
        t = V(lambda: dve.tensor_tensor(v, v, wide(r_, 2, 128), ALU.mult), t)
        v2 = x.rearrange("p (t n) -> p t n", t=2)
        t = V(lambda: dve.tensor_tensor(v2, v2, wide(ng, 1, 2), ALU.mult), t, tng)
        return V(lambda: dve.tensor_tensor(x, x, z, ALU.mult), t, tz_)

    flat = lambda a: a.rearrange("p a b -> p (a b)")
    toaf = head128(flat(oa[:]), f1(0), nab[:, 0, :], t_na, 1.0 - lam_init, toa, tsa, 200)
    t = V(lambda: dve.tensor_tensor(flat(ob[:]), flat(ob[:]), f1(1), ALU.mult), tsg, *tob)
    tobf = head128(flat(ob[:]), f1(2), nab[:, 1, :], t_nb, 1.0, [t], tsb, 216)
    dump("ya", oa[:], toaf)
    dump("yb", ob[:], tobf)
    P.wait("act", x1_last)
    P.wait("dve", x1_last)
    for tt in range(2):
        to_T(lambda c: oa[:, tt, c * 128:(c + 1) * 128], 4, X1, 0, [toaf], [2 * tt], tt)
    for tt in range(2):
        to_T(lambda c: ob[:, tt, c * 128:(c + 1) * 128], 4, X1, 4, [tobf], [2 * tt + 1], tt)
    YA = (xh[1], xl[1], X1[2])
    YB = (xh[1][:, 4:8, :], xl[1][:, 4:8, :], X1[2][4:8])
    x0_last = ("pe_w", P.counts["pe_w"])
    P.wait("act", x0_last)
    P.wait("dve", x0_last)
    P.wait("sp", tobf)
    gn = zob[:, 0].rearrange("p a b -> p (a b)")
    t_gn = load(gn, rows128(A["norm_post_2"][0]), toaf)
    xrow = zob[:, 1:3].rearrange("p i a b -> p i (a b)")
    tsq = []
    for c in range(4):
        ba, bb = (4, 5) if c % 2 == 0 else (6, 7)
        t1 = lin_A(YA, DA["w_a_2"][0], 4, c * 256, ba)
        t2 = lin_A(YB, DA["w_b_2"][0], 4, c * 256, bb)
        oa_ = ga_t[:, 2 * c:2 * c + 2, :].rearrange("p a b -> p (a b)")
        ob_ = gb_t[:, 2 * c:2 * c + 2, :].rearrange("p a b -> p (a b)")
        u1 = V(lambda: dve.tensor_tensor(oa_, oa_, bank[ba][:], ALU.mult), t1, *tgs)
        free[ba] = [u1]
        u2 = V(lambda: dve.tensor_tensor(ob_, ob_, bank[bb][:], ALU.mult), t2)
        free[bb] = [u2]
        u = V(lambda: dve.tensor_tensor(oa_, oa_, ob_, ALU.add), u1, u2)
        oh = X0[0][:, 2 * c:2 * c + 2, :].rearrange("p a b -> p (a b)")
        ol = X0[1][:, 2 * c:2 * c + 2, :].rearrange("p a b -> p (a b)")
        th = C(lambda: act.copy(oh, oa_), u)
        tl = V(lambda: dve.tensor_tensor(ol, oa_, oh.bitcast(F32), ALU.subtract), th)
        X0[2][2 * c] = X0[2][2 * c + 1] = [th, tl]
    thr = []
    for tt in range(2):
        for j in range(2):
            b = 4 + 2 * tt + j
            take(b)
            P.wait("pe", *h_done)
            for c in range(4):
                t = T(lambda: pe.transpose(bank[b][:, c * 128:(c + 1) * 128],
                                           hT[:, 4 * j + c, tt * 128:(tt + 1) * 128], ident[:]))
            t = V(lambda: dve.tensor_copy(xrow[:, tt, j * 512:(j + 1) * 512], bank[b][:]), t, tobf)
            free[b] = [t]
            thr.append(t)
    t = run(lin_B(X0, DA["w_out_2"][0], 8, 0, D, LOWB))
    sqf = aq[:].rearrange("p a b -> p (a b)").rearrange("p (a b) -> p a b", b=D)
    fin = qkc[:].rearrange("p a b -> p (a b)").rearrange("p (a b) -> p a b", b=D)
    outs = []
    for tt in range(2):
        ps = psum[:, 2 * tt:2 * tt + 2, :].rearrange("p a b -> p (a b)")
        ss, rr = small[:, 240 + 2 * tt:241 + 2 * tt], small[:, 241 + 2 * tt:242 + 2 * tt]
        u = C(lambda: act.activation(sqf[:, tt, :], ps, ACT.Square, accum_out=ss), t)
        r_ = rstd_of(ss, rr, D, u)
        for j in range(2):
            q = slice(j * 512, (j + 1) * 512)
            v = V(lambda: dve.scalar_tensor_tensor(out=fin[:, tt, q], in0=ps[:, q], scalar=rr, in1=gn[:, q],
                                                   op0=ALU.mult, op1=ALU.mult), r_, t_gn)
            v = V(lambda: dve.tensor_tensor(fin[:, tt, q], fin[:, tt, q], xrow[:, tt, q], ALU.add), v)
            outs.append(load(out[0, tt * 128:(tt + 1) * 128, q], fin[:, tt, q], v))
    mx.close()
    P.wait("sp", *outs, *dumps)
    assert state["used"] == len(plan) and not hooks


_INS = ['x', 'mem', 'positions', 'ffn1_norm_g', 'ffn1_w_gate', 'ffn1_w_up', 'ffn1_w_down', 'mix_norm_g',
        'mem_norm_g', 'w_mem_kv', 'mem_q_norm_g', 'mem_k_norm_g', 'w_o', 'ffn2_norm_g', 'ffn2_w_gate',
        'ffn2_w_up', 'ffn2_w_down', 'a_w_in', 'a_dw_kernel', 'a_dw_bias', 'a_ln_g', 'a_ln_b', 'kv_norm_g',
        'w_kv', 'k_norm_g', 'b_w_in', 'b_q_norm_g', 'norm_pre_2', 'norm_post_2', 'w_in_2', 'b_if_2',
        'conv_qk_2', 'lambda_qk_2', 'norm_a_2', 'norm_b_2', 'w_a_2', 'w_b_2', 'w_out_2']


def kernel(**inputs):
    import numpy as _np
    import concourse.bacc as _bacc
    from concourse import mybir as _mybir
    from concourse.bass_utils import run_bass_kernel_spmd as _run

    nc = _bacc.Bacc("TRN2", target_bir_lowering=False, num_devices=1)
    arrays, args = {}, {}
    for name in _INS:
        a = _np.ascontiguousarray(inputs[name])
        arrays[f"in_{name}"] = a
        args[name] = nc.dram_tensor(f"in_{name}", a.shape, _mybir.dt.from_np(a.dtype), kind="ExternalInput").ap()
    out = nc.dram_tensor("out_0", (1, S, D), _mybir.dt.float32, kind="ExternalOutput").ap()
    program(nc, args, out)
    r = _run(nc, [arrays], core_ids=[0])
    return r.results[0]["out_0"]
```

```python
from contextlib import ExitStack

import concourse.bass as bass
import numpy as np
from concourse import mybir

F32 = mybir.dt.float32
F32R = mybir.dt.float32r
BF16 = mybir.dt.bfloat16
I32 = mybir.dt.int32
ALU = mybir.AluOpType
ACT = mybir.ActivationFunctionType
AX = mybir.AxisListType.X

D = 1024
S = 256
FF = 2816
NEG = -1.0e30
EPS = 1e-6
NDG = 16
CONV_PE = (3, 5)
CONV_DVE = (0, 1, 2, 4)
SLOT = 1024
RAW, SPLIT, AHEAD = 7, 5, 4


def wide(ap, axis, n):
    v = ap.unsqueeze(axis)
    shape = list(v.shape)
    shape[axis] = n
    return v.broadcast_to(shape)


def rows128(row):
    return row.partition_broadcast(128)


class Program:

    def __init__(self, nc, ctx):
        self.nc, self.ctx = nc, ctx
        self.engines = {"pe": nc.tensor, "act": nc.scalar, "dve": nc.vector, "pool": nc.gpsimd, "sp": nc.sync}
        self.sems, self.counts = {}, {}
        self.seen = {e: {} for e in self.engines}

    def sem(self, name):
        if name not in self.sems:
            self.sems[name] = self.ctx.enter_context(self.nc.semaphore(name))
            self.counts[name] = 0
        return self.sems[name]

    def op(self, eng, fn, *waits, sem=None, by=1):
        self.wait(eng, *waits)
        name = f"{eng}_{sem}" if sem else f"{eng}_done"
        s = self.sem(name)
        self.counts[name] += by
        fn().then_inc(s, by)
        return (name, self.counts[name])

    def quiet(self, eng, fn, *waits):
        self.wait(eng, *waits)
        fn()

    def wait(self, eng, *waits):
        for w in waits:
            if w is None:
                continue
            name, n = w
            if self.seen[eng].get(name, 0) >= n:
                continue
            self.seen[eng][name] = n
            s = self.sems[name]
            self.engines[eng].wait_ge(s, n)


def program(nc, A, out, dbg=None):
    with ExitStack() as ctx:
        build(nc, ctx, A, out, dbg or {})


def build(nc, ctx, A, out, dbg):
    P = Program(nc, ctx)
    pe, act, dve, pool = nc.tensor, nc.scalar, nc.vector, nc.gpsimd

    def sb(name, shape, dt=F32, c=ctx):
        return c.enter_context(nc.sbuf_tensor(name, shape, dt))

    psum = ctx.enter_context(nc.psum_tensor("psum", [128, 8, 512], F32))
    bank = [psum[:, i, :] for i in range(8)]
    free = [[] for _ in range(8)]

    def V(fn, *w, sem=None):
        return P.op("dve", fn, *w, sem=sem)

    def C(fn, *w, sem=None):
        return P.op("act", fn, *w, sem=sem)

    def G(fn, *w, sem=None):
        return P.op("pool", fn, *w, sem=sem)

    def T(fn, *w, sem=None):
        return P.op("pe", fn, *w, sem=sem)

    def MM(o, l, r, start, stop, *w):
        P.quiet("pe", lambda: pe.matmul(o, l, r, start=start, stop=stop, skip_group_check=True), *w)

    def MMi(o, l, r, start, stop, *w):
        return T(lambda: pe.matmul(o, l, r, start=start, stop=stop, skip_group_check=True), *w)

    def take(b):
        P.wait("pe", *free[b])
        free[b] = []

    raw = sb("raw", [128, RAW, SLOT])
    whi = sb("whi", [128, SPLIT, SLOT], F32R)
    wlo = sb("wlo", [128, SPLIT, SLOT], F32R)
    hT = sb("hT", [128, 8, S])
    acc = sb("acc", [128, 512])
    sqb = sb("sqb", [128, 2, 512])
    rowr = sb("rowr", [128, 2, S])
    diag = sb("diag", [128, 2, 128])
    gcol = sb("gcol", [128, 8, 8])
    xh = [sb(f"xh{i}", [128, 8, S], F32R) for i in range(2)]
    xl = [sb(f"xl{i}", [128, 8, S], F32R) for i in range(2)]
    ident = sb("ident", [128, 128])
    ones = sb("ones", [128, 128])
    ln1 = sb("ln1", [128, 128])
    upper = sb("upper", [128, 128])
    identb = sb("identb", [128, 128], BF16)
    maskb = sb("maskb", [128, 128], BF16)
    alib = sb("alib", [128, 2, 4, S], BF16)
    mhalf = sb("mhalf", [128, 16])
    hg = sb("hg", [128, 6, 64])
    small = sb("small", [128, 320])
    kTm = [sb(f"kTm{i}", [128, 2, S]) for i in range(2)]
    mkv2 = sb("mkv2", [128, 2, 2, 512])
    mkv = [mkv2[:, 0], mkv2[:, 1]]

    plan = []

    def slots_A(w, K, c0, n=256):
        for k in range(0, K, 4):
            plan.append((w, k, min(4, K - k), c0, n))

    def slots_B(w, K, c0, n):
        kk = SLOT // n
        for k in range(0, K, kk):
            plan.append((w, k, kk, c0, n))

    state = {"dma": 0, "split": 0, "used": 0, "cap": 10 ** 6}
    lo_done, hi_done, pe_done = [], [], []
    hooks = {}

    def at_slot(ahead, f):
        hooks.setdefault(state["used"] + ahead, []).append(f)

    def view(t, j, nk, n):
        return t[:, j, 0:nk * n].rearrange("p (k n) -> p k n", k=nk)

    loaded = []

    def load_weights(i):
        while state["dma"] <= min(i, len(plan) - 1):
            j = state["dma"]
            w, k0, nk, c0, n = plan[j]
            if j >= RAW:
                P.wait("sp", lo_done[j - RAW])
            src = w[k0 * 128:(k0 + nk) * 128, c0:c0 + n].rearrange("(k p) n -> p k n", p=128)
            dst = view(raw, j % RAW, nk, n)
            loaded.append(P.op("sp", lambda: nc.sync.dma_start(dst, src), sem=f"w{j % RAW}", by=16))
            state["dma"] += 1

    def split_to(i):
        while state["split"] <= min(i, len(plan) - 1):
            j = state["split"]
            load_weights(j)
            w, k0, nk, c0, n = plan[j]
            r = raw[:, j % RAW, 0:nk * n]
            h = whi[:, j % SPLIT, 0:nk * n]
            lo = wlo[:, j % SPLIT, 0:nk * n]
            before = pe_done[j - SPLIT] if j >= SPLIT else None
            th = C(lambda: act.copy(h, r), loaded[j], before, sem="hi")
            tl = V(lambda: dve.tensor_tensor(lo, r, h.bitcast(F32), ALU.subtract), th, before, sem="lo")
            hi_done.append(th)
            lo_done.append(tl)
            state["split"] += 1
            load_weights(j + RAW)

    class Slot:
        pass

    def hold(n):
        state["cap"] = state["used"] + n - 1

    def let_go():
        state["cap"] = 10 ** 6

    def next_slot(key):
        i = state["used"]
        for f in hooks.pop(i, []):
            f()
        assert plan[i][1:] == key, (plan[i], key)
        split_to(min(i + AHEAD, state["cap"]))
        s = Slot()
        s.hi = view(whi, i % SPLIT, key[1], key[3])
        s.lo = view(wlo, i % SPLIT, key[1], key[3])
        s.th, s.tl = hi_done[i], lo_done[i]
        state["used"] += 1
        return s

    def lin_A(x, w, K, c0, b):
        return run(lin_A_steps(x, w, K, c0, b))

    def lin_A_steps(x, w, K, c0, b):
        take(b)
        for k0 in range(0, K, 4):
            m = min(4, K - k0)
            s = next_slot((k0, m, c0, 256))
            for k in range(m):
                kc = k0 + k
                for j in range(2):
                    o = bank[b][:, j * 256:(j + 1) * 256]
                    hi = s.hi[:, k, j * 128:(j + 1) * 128]
                    lo = s.lo[:, k, j * 128:(j + 1) * 128]
                    last = kc == K - 1 and j == 1
                    MM(o, hi, x[0][:, kc, :], kc == 0 and j == 0, False, s.th, x[2][kc][0])
                    MM(o, hi, x[1][:, kc, :], False, False, x[2][kc][1])
                    P.wait("pe", s.tl)
                    if k == m - 1 and j == 1:
                        t = T(lambda: pe.matmul(o, lo, x[0][:, kc, :], start=False, stop=last,
                                                skip_group_check=True), sem="w")
                    else:
                        MM(o, lo, x[0][:, kc, :], False, last)
            pe_done.append(t)
            yield t

    tail_done = [[None, None], [None, None]]

    def lin_B(x, w, K, c0, n, banks, tail=0):
        kk = SLOT // n if n >= 64 else K
        for tt in range(2):
            for b in banks[tt]:
                take(b)
        for k0 in range(0, K - tail, kk):
            s = next_slot((k0, kk, c0, n))
            P.wait("pe", s.th)
            for k in range(kk):
                kc = k0 + k
                P.wait("pe", x[2][kc][0], x[2][kc][1])
                for tt in range(2):
                    jobs = []
                    for xi, wi in ((0, 0), (1, 0), (0, 1)):
                        for j, b in enumerate(banks[tt]):
                            jobs.append((xi, wi, j, b))
                    for i, (xi, wi, j, b) in enumerate(jobs):
                        w0, w1 = j * 512, min(n, (j + 1) * 512)
                        o = bank[b][:, 0:w1 - w0]
                        l = x[xi][:, kc, tt * 128:(tt + 1) * 128]
                        r = (s.lo if wi else s.hi)[:, k, w0:w1]
                        st = kc == 0 and xi == 0 and wi == 0
                        sp_ = kc == K - 1 and wi == 1
                        if wi:
                            P.wait("pe", s.tl)
                        if k == kk - 1 and tt == 1 and i == len(jobs) - 1:
                            t = T(lambda o=o, l=l, r=r, sp_=sp_: pe.matmul(
                                o, l, r, start=False, stop=sp_, skip_group_check=True), sem="w")
                        else:
                            MM(o, l, r, st, sp_)
            pe_done.append(t)
            yield t
        ss = [next_slot((k, 1, c0, n)) for k in range(K - tail, K)]
        for tt in range(2 if tail else 0):
            for j, b in enumerate(banks[tt]):
                w0, w1 = j * 512, (j + 1) * 512
                for k, s in zip(range(K - tail, K), ss):
                    l = [x[i][:, k, tt * 128:(tt + 1) * 128] for i in range(2)]
                    MM(bank[b][:], l[0], s.hi[:, 0, w0:w1], False, False, s.th, x[2][k][0])
                    MM(bank[b][:], l[1], s.hi[:, 0, w0:w1], False, False, x[2][k][1])
                    t = MMi(bank[b][:], l[0], s.lo[:, 0, w0:w1], False, k == K - 1, s.tl)
                tail_done[tt][j] = t

    def run(g):
        t = None
        for t in g:
            pass
        return t

    def load(dst, src, *w, slow=False, eng="sp"):
        n = state.setdefault("loads", 0)
        state["loads"] += 1
        q = nc.sync if eng == "sp" else nc.scalar
        return P.op(eng, lambda: q.dma_start(dst, src, allow_slow_non_contiguous=slow), *w, sem=f"l{n}", by=16)

    t = G(lambda: pool.memset(ident[:], 0.0))
    t_ident = G(lambda: pool.affine_select(out=ident[:], in_=ident[:], compare_op=ALU.not_equal, fill=1.0,
                                           base=0, pattern=[[-1, 128]], channel_multiplier=1), t)
    t = G(lambda: pool.memset(ones[:], 1.0))
    t_ones = t
    t_ln1 = G(lambda: pool.memset(ln1[:], 1.0 / 768))
    t_upper = G(lambda: pool.affine_select(out=upper[:], in_=ones[:], compare_op=ALU.is_ge, fill=0.0,
                                           base=0, pattern=[[1, 128]], channel_multiplier=-1), t)
    t_identb = G(lambda: pool.tensor_copy(identb[:], ident[:]), t_ident)
    t = G(lambda: pool.memset(maskb[:], 0.0))
    t_mask = G(lambda: pool.affine_select(out=maskb[:], in_=maskb[:], compare_op=ALU.is_ge, fill=NEG,
                                          base=0, pattern=[[-1, 128]], channel_multiplier=1), t)
    t_half = G(lambda: pool.memset(mhalf[:], -0.5))
    t = None
    for tt in range(2):
        ti = G(lambda tt=tt: pool.iota(kTm[0][:, 0, :], pattern=[[1, S]], base=-128 * tt, channel_multiplier=-1,
                                       allow_small_or_imprecise_dtypes=True), t)
        for h in range(4):
            c = 8.0 * 2.0 ** (-2 * (h + 1))
            t = G(lambda tt=tt, h=h, c=c: pool.tensor_scalar(alib[:, tt, h, :], kTm[0][:, 0, :], c, None, ALU.mult), ti)
    t_alib = G(lambda: pool.affine_select(out=alib[:, 0], in_=alib[:, 0], compare_op=ALU.is_ge, fill=NEG, base=0,
                                          pattern=[[0, 4], [-1, S]], channel_multiplier=1), t)
    t_alib = G(lambda: pool.affine_select(out=alib[:, 1], in_=alib[:, 1], compare_op=ALU.is_ge, fill=NEG, base=128,
                                          pattern=[[0, 4], [-1, S]], channel_multiplier=1), t)

    h_done = [None] * 4
    row_free = [None, None]

    def rstd_of(ss, rs, n, t, width=1):
        t = G(lambda: pool.tensor_scalar(rs, ss, 1.0 / n, EPS, ALU.mult, ALU.add), t)
        return G(lambda: pool.tensor_tensor(rs, rs, mhalf[:, 0:width], ALU.pow), t)


    class Norm:
        pass

    def squares(p):
        flat_ = hT[:, 2 * p:2 * p + 2, :].rearrange("p a b -> p (a b)")
        if p == 0:
            st_["acc"] = C(lambda: act.activation(acc[:], flat_, ACT.Square), h_done[p], st_.get("accfree"))
        else:
            t = C(lambda: act.activation(sqb[:, p % 2, :], flat_, ACT.Square), h_done[p], st_.get(("sqb", p % 2)))
            st_["acc"] = V(lambda: dve.tensor_tensor(acc[:], acc[:], sqb[:, p % 2, :], ALU.add), t, st_["acc"])
            st_["sqb", p % 2] = st_["acc"]

    def prep(p, targets, sq=True):
        if sq and p == 0:
            squares(p)
        for gi, x, xfree in targets:
            for c in (2 * p, 2 * p + 1):
                g = gcol[:, c, gi:gi + 1]
                th = C(lambda: act.activation(x[0][:, c, :], hT[:, c, :], ACT.Copy, scale=g), h_done[p], t_gcol, xfree)
                tl = V(lambda: dve.scalar_tensor_tensor(out=x[1][:, c, :], in0=hT[:, c, :], scalar=g,
                                                        in1=x[0][:, c, :].bitcast(F32), op0=ALU.mult,
                                                        op1=ALU.subtract), th, xfree)
                x[2][c] = [th, tl]
        if sq and p > 0:
            squares(p)

    st_ = {}

    def norm(b, ahead=(2, 3)):
        N = Norm()
        i = st_["n"] = st_.get("n", 0) + 1
        c0 = 4 * (i % 4)
        v = small[:, c0:c0 + 2]
        r = small[:, c0 + 2:c0 + 4]
        N.col = [r[:, 0:1], r[:, 1:2]]
        N.row = rowr[:, i % 2, :]
        N.i = i % 2
        t_acc = st_["acc"]

        def one():
            take(b)
            P.wait("pe", t_acc, t_ones)
            for tt in range(2):
                for j in range(2):
                    t = MMi(bank[b][:, 4 * tt:4 * tt + 4], acc[:, j * 256 + tt * 128:j * 256 + (tt + 1) * 128],
                            ones[:, 0:4], j == 0, j == 1)
            st_["accfree"] = t
            src = bank[b][:, 0:8:4]
            t = V(lambda: dve.tensor_scalar(v, src, 1.0 / D, EPS, ALU.mult, ALU.add), t)
            N.t_col = G(lambda: pool.tensor_tensor(r, v, mhalf[:, 0:2], ALU.pow), t)
            td = [V(lambda: dve.tensor_scalar(diag[:, tt, :], ident[:], N.col[tt], None, ALU.mult),
                    N.t_col, t_ident, st_.get("dgfree")) for tt in range(2)]
            N.td = td

        def two():
            for tt in range(2):
                t = MMi(bank[b][:, 128 + tt * 128:256 + tt * 128], ones[:], diag[:, tt, :], True, True, N.td[tt])
            st_["dgfree"] = t
            N.t_row = C(lambda: act.copy(N.row, bank[b][:, 128:384]), t, row_free[N.i])
            free[b] = [N.t_row]

        at_slot(ahead[0], one)
        at_slot(ahead[1], two)
        return N

    def to_T(src_of, n_chunks, dst, d0, ready, banks, tt, skip=0):
        res = []
        for i, c in enumerate(range(0, n_chunks, 4)):
            m = min(4, n_chunks - c)
            b = banks[i % len(banks)]
            take(b)
            P.wait("pe", t_ident, *ready)
            for j in range(m):
                f = lambda b=b, j=j, c=c: pe.transpose(bank[b][:, j * 128:(j + 1) * 128], src_of(c + j), ident[:])
                if j == m - 1:
                    t = T(f)
                else:
                    P.quiet("pe", f)
            src = bank[b][:, 0:m * 128].rearrange("p (k n) -> p k n", k=m)
            oh = dst[0][:, d0 + c:d0 + c + m, tt * 128:(tt + 1) * 128]
            ol = dst[1][:, d0 + c:d0 + c + m, tt * 128:(tt + 1) * 128]
            th = C(lambda oh=oh, src=src: act.copy(oh, src), t)
            tl = V(lambda oh=oh, ol=ol, src=src: dve.tensor_tensor(ol, src, oh.bitcast(F32), ALU.subtract), th)
            free[b] = [th, tl]
            for k in range(m):
                dst[2][d0 + c + k] = [th, tl]
            res += [th, tl]
        last_T[0] = t
        return res

    last_T = [None]

    def rows_normed(src, ready, g, tg, rs, xg, xfree):
        r = [None, None]
        for tt in range(2):
            c, t = rs[tt]
            r[tt] = V(lambda: dve.scalar_tensor_tensor(out=xg[:, tt, :], in0=src[:, tt, :], scalar=c, in1=g,
                                                       op0=ALU.mult, op1=ALU.mult), t, tg, ready, xfree)
        return r

    def from_rows(src, ready, g, tg, dst, banks, rs, xg, xfree):
        r = rows_normed(src, ready, g, tg, rs, xg, xfree)
        for tt in range(2):
            to_T(lambda c: xg[:, tt, c * 128:(c + 1) * 128], 8, dst, 0, [r[tt]], banks[tt], tt)
        return last_T[0]

    def row_stats(src, ready, junk, jfree, c0):
        r = []
        for tt in range(2):
            s = small[:, c0 + 2 * tt:c0 + 2 * tt + 1]
            o = small[:, c0 + 2 * tt + 1:c0 + 2 * tt + 2]
            t = C(lambda: act.activation(junk[:, tt, :], src[:, tt, :], ACT.Square, accum_out=s), ready, jfree)
            r.append((o, rstd_of(s, o, D, t)))
        return r

    def add_h(p, b, t, scale, N, targets, tmp, tmpfree):
        pair = hT[:, 2 * p:2 * p + 2, :].rearrange("p a b -> p (a b)")
        if N is None:
            t = V(lambda: dve.tensor_tensor(pair, bank[b][:], pair, ALU.add), t, h_done[p])
            free[b] = [t]
        else:
            o = tmp.rearrange("p (a b) -> p a b", a=2)
            src = bank[b][:].rearrange("p (a b) -> p a b", a=2)
            t = V(lambda: dve.scalar_tensor_tensor(out=o, in0=src, scalar=scale, in1=wide(N.row, 1, 2),
                                                   op0=ALU.mult, op1=ALU.mult), t, N.t_row)
            free[b] = [t]
            row_free[N.i] = t
            t = V(lambda: dve.tensor_tensor(pair, tmp, pair, ALU.add), t, h_done[p])
        h_done[p] = t
        prep(p, targets)

    def ffn(wg, wu, wd, x, N, gT, targets):
        gh, gl, gr, pr = gT
        gt_ = [None] * 22
        sgf = [[None], [None]]
        for p in range(FF // 256):
            bg, bu = (0, 1) if p % 2 == 0 else (2, 3)
            t1 = lin_A(x, wg, 8, p * 256, bg)
            t2 = lin_A(x, wu, 8, p * 256, bu)
            r, s, q = gr[:, p % 2, :], gr[:, p % 2, :], pr[:, p % 2, :]
            tr = V(lambda: dve.tensor_tensor(r.rearrange("p (a b) -> p a b", a=2),
                                             bank[bg][:].rearrange("p (a b) -> p a b", a=2), wide(N.row, 1, 2),
                                             ALU.mult), t1, N.t_row, *sgf[p % 2])
            free[bg] = [tr]
            ts = C(lambda: act.activation(s, r, ACT.Silu), tr, *sgf[p % 2])
            tm = V(lambda: dve.tensor_tensor(q, s, bank[bu][:], ALU.mult), ts, t2, *sgf[p % 2])
            free[bu] = [tm]
            oh = gh[:, 2 * p:2 * p + 2, :].rearrange("p a b -> p (a b)")
            ol = gl[:, 2 * p:2 * p + 2, :].rearrange("p a b -> p (a b)")
            th = C(lambda: act.copy(oh, q), tm)
            tl = V(lambda: dve.tensor_tensor(ol, q, oh.bitcast(F32), ALU.subtract), th)
            sgf[p % 2] = [ts, th, tl]
            gt_[2 * p] = gt_[2 * p + 1] = [th, tl]
        x_last = pe_done[-1]
        targets = [(gi, xx, x_last if f is None else f) for gi, xx, f in targets]
        for p in range(4):
            t = lin_A((gh, gl, gt_), wd, 22, p * 256, 4 + p)
            add_h(p, 4 + p, t, 0.5, N, targets, sqb_tmp(p), None)
        return x_last

    def sqb_tmp(p):
        return htmp[:, p % 2, :]

    def head_rms(src, nh, c0, g, tg, dst, ready, sq, mid=lambda: None):
        ss = small[:, c0:c0 + nh]
        rs = small[:, c0 + 16:c0 + 16 + nh]
        v = src.rearrange("p (h d) -> p h d", d=64)
        o = dst.rearrange("p (h d) -> p h d", d=64)
        q = sq.rearrange("p (h d) -> p h d", d=64)
        t = V(lambda: dve.tensor_tensor(q, v, v, ALU.mult), *ready)
        t = V(lambda: dve.reduce_sum(ss, q, AX), t)
        t = rstd_of(ss, rs, 64, t, nh)
        mid()
        t = V(lambda: dve.tensor_tensor(o, v, wide(rs, 2, 64), ALU.mult), t)
        return V(lambda: dve.tensor_tensor(o, o, wide(g, 1, nh), ALU.mult), t, tg)

    def heads_rms(jobs):
        rows = []
        for src, nh, c0, g, tg, dst, ready, sq in jobs:
            ss, rs = small[:, c0:c0 + nh], small[:, c0 + 16:c0 + 16 + nh]
            v, o, q = (a.rearrange("p (h d) -> p h d", d=64) for a in (src, dst, sq))
            t = C(lambda: act.activation(q, v, ACT.Square), *ready)
            t = V(lambda: dve.reduce_sum(ss, q, AX), t)
            rows.append((nh, g, tg, v, o, rs, rstd_of(ss, rs, 64, t, nh)))
            yield
        for nh, g, tg, v, o, rs, t in rows:
            t = V(lambda: dve.tensor_tensor(o, v, wide(rs, 2, 64), ALU.mult), t)
            yield V(lambda: dve.tensor_tensor(o, o, wide(g, 1, nh), ALU.mult), t, tg)

    def padded_T(src_of, n, dst, c0, tt, ready, b):
        take(b)
        P.wait("pe", t_ident, *ready)
        for j in range(n):
            t = T(lambda: pe.transpose(bank[b][:, j * 128:(j + 1) * 128], src_of(j), ident[:]))
        for e in range(2):
            q = slice(64 * e, 64 * e + 64)
            src = bank[b][q, 0:n * 128].rearrange("p (k n) -> p k n", k=n)
            o = dst[q, 2 * c0 + e:2 * (c0 + n):2, tt * 128:(tt + 1) * 128]
            t = C(lambda: act.copy(o, src), t)
        free[b] = [t]
        return t

    def plain_T(src_of, n, dst_of, ready, b, eng="act"):
        take(b)
        P.wait("pe", t_ident, *ready)
        for j in range(n):
            f = lambda j=j: pe.transpose(bank[b][:, j * 128:(j + 1) * 128], src_of(j), ident[:])
            if j == n - 1:
                t = T(f)
            else:
                P.quiet("pe", f)
        src = bank[b][:, 0:n * 128].rearrange("p (k n) -> p k n", k=n)
        if eng == "act":
            t = C(lambda: act.copy(dst_of, src), t)
        else:
            t = V(lambda: dve.tensor_copy(dst_of, src), t)
        free[b] = [t]
        return t

    def attend(jobs, pbuf, ptbuf, att, sbase, banks, vbank):
        n = len(jobs)
        st = [dict() for _ in jobs]
        pf, ptf = [None] * 3, [None] * 2
        done = []

        def scores(i):
            tt, causal, heads, oc, ready = jobs[i]
            kw = 128 * (tt + 1) if causal else 256
            b = banks[i % 2]
            take(b)
            take(b + 1)
            P.wait("pe", *ready)
            ps = psum[:, b:b + 2, 0:kw]
            for h, (qT, kT, vv) in enumerate(heads):
                t = MMi(ps[:, h, :], qT(tt), kT(kw), True, not causal)
            if causal:
                for h in range(2):
                    t = MMi(ps[:, h, kw - 128:kw], identb[:], maskb[:], False, True, t_identb, t_mask)
            c = sbase + 8 * (i % 3)
            mx, nb, sm, rc = (small[:, c + 2 * q:c + 2 * q + 2] for q in range(4))
            t = V(lambda: dve.reduce_max(mx, ps, AX), t, st[i - 3]["fin"] if i >= 3 else None)
            t = V(lambda: dve.tensor_scalar(nb, mx, -0.125, None, ALU.mult), t)
            p = pbuf[:, i % 3, 0:2 * kw].rearrange("p (h k) -> p h k", h=2)
            P.wait("act", pf[i % 3])
            for h in range(2):
                te = C(lambda h=h: act.activation(p[:, h, :], ps[:, h, :], ACT.Exp, bias=nb[:, h:h + 1], scale=0.125,
                                                  accum_out=sm[:, h:h + 1]), t)
            free[b] = free[b + 1] = [te]
            st[i].update(p=p, kw=kw, sm=sm, rc=rc, te=te)

        def turn(i):
            s = st[i]
            nk = s["kw"] // 128
            b = banks[2 + i % 2]
            take(b)
            P.wait("pe", s["te"], t_ident)
            m = 2 * nk
            for j in range(m):
                f = lambda j=j: pe.transpose(bank[b][:, j * 128:(j + 1) * 128],
                                             s["p"][:, j // nk, (j % nk) * 128:(j % nk + 1) * 128], ident[:])
                if j == m - 1:
                    t = T(f)
                else:
                    P.quiet("pe", f)
            pf[i % 3] = t
            dst = ptbuf[:, i % 2, 0:m * 128]
            s["tr"] = V(lambda: dve.reciprocal(s["rc"], s["sm"]), s["te"])
            eng = V if i % 2 else C
            if i % 2:
                t = V(lambda: dve.tensor_copy(dst, bank[b][:, 0:m * 128]), t, ptf[i % 2])
            else:
                t = C(lambda: act.copy(dst, bank[b][:, 0:m * 128]), t, ptf[i % 2])
            free[b] = [t]
            s["pt"] = t

        def values(i):
            tt, causal, heads, oc, ready = jobs[i]
            s = st[i]
            nk = s["kw"] // 128
            b = vbank
            take(b)
            P.wait("pe", s["pt"])
            for h, (qT, kT, vv) in enumerate(heads):
                for k in range(nk):
                    l = ptbuf[:, i % 2, (h * nk + k) * 128:(h * nk + k + 1) * 128]
                    f = lambda l=l, h=h, k=k, vv=vv: pe.matmul(bank[b][:, h * 64:(h + 1) * 64], l, vv(k),
                                                               start=k == 0, stop=k == nk - 1,
                                                               skip_group_check=True)
                    if h == 1 and k == nk - 1:
                        t = T(f)
                    else:
                        P.quiet("pe", f)
            ptf[i % 2] = t
            o = att[:, tt, oc:oc + 128].rearrange("p (h d) -> p h d", h=2)
            src = bank[b][:, 0:128].rearrange("p (h d) -> p h d", h=2)
            t = V(lambda: dve.tensor_tensor(o, src, wide(s["rc"], 2, 64), ALU.mult), t, s["tr"])
            free[b] = [t]
            s["fin"] = t
            done.append(t)

        for i in range(n + 2):
            if i < n:
                scores(i)
            if 0 <= i - 1 < n:
                turn(i - 1)
            if 0 <= i - 2 < n:
                values(i - 2)
            yield done[-1] if done else None

    def dump(name, ap, *w):
        if name in dbg:
            t = load(dbg[name], ap, *w)
            dumps.append(t)
            for e in ("dve", "act", "pe", "pool"):
                P.wait(e, t)

    dumps = []
    DA = {k: A[k] for k in A}

    def plan_ffn(which, l):
        for p in range(FF // 256):
            slots_A(DA[which + "_w_gate"][l], 8, p * 256)
            slots_A(DA[which + "_w_up"][l], 8, p * 256)
        for p in range(4):
            slots_A(DA[which + "_w_down"][l], 22, p * 256)

    ain = DA["a_w_in"][0]
    win = DA["w_in_2"][0]
    plan_ffn("ffn1", 0)
    for p in range(3):
        slots_A(ain, 8, p * 256)
        slots_A(ain, 8, 768 + p * 256)
    slots_B(ain, 8, 1536, 256)
    for l in range(2):
        slots_B(DA["w_mem_kv"][l], 8, 0, 512)
    for p in range(4):
        slots_A(DA["w_o"][0], 8, p * 256)
    plan_ffn("ffn2", 0)
    plan_ffn("ffn1", 1)
    slots_B(DA["w_kv"], 8, 0, 768)
    slots_B(DA["b_w_in"][0], 8, 0, D)
    slots_B(DA["w_kv"], 8, 768, 768)
    for p in range(4):
        slots_A(DA["w_o"][1], 8, p * 256)
    plan_ffn("ffn2", 1)
    for c in range(4):
        slots_A(win, 8, 2048 + c * 256)
    plan.append((win, 0, 8, 4608, 8))
    for c in range(4):
        slots_A(win, 8, c * 256)
    slots_B(win, 8, 3072, 512)
    slots_B(win, 8, 1024, 512)
    for c0 in (1536, 3584, 4096):
        slots_B(win, 8, c0, 512)
    for c in range(8):
        slots_A(win, 8, 4616 + c * 256)
    for nm in ("w_a_2", "w_b_2"):
        for c in range(4):
            slots_A(DA[nm][0], 4, c * 256)
    slots_B(DA["w_out_2"][0], 8, 0, D)

    LOWB = [[0, 1], [2, 3]]
    htmp = sb("htmp", [128, 2, 512])
    X0, X1 = (xh[0], xl[0], [[None, None]] * 8), (xh[1], xl[1], [[None, None]] * 8)
    X0, X1 = [(xh[i], xl[i], [[None, None] for _ in range(8)]) for i in range(2)]

    mm = ExitStack()
    mem = sb("memt", [128, 2, D], F32, mm)
    gn = sb("gnm", [128, D], F32, mm)
    st0 = ExitStack()
    xn = sb("xn", [128, 2, D], F32, st0)
    xg0 = mkv2[:].rearrange("p l t n -> p l (t n)")
    grow = gn[0:8, :]
    gains = [A["ffn1_norm_g"][0:1], A["mix_norm_g"][0:1], A["ffn2_norm_g"][0:1],
             A["kv_norm_g"].rearrange("(a d) -> a d", a=1), A["ffn1_norm_g"][1:2], A["mix_norm_g"][1:2],
             A["ffn2_norm_g"][1:2], A["norm_pre_2"][0:1]]
    t_g0 = load(grow[0:1, :], gains[0])
    t_x = [load(xn[:, tt, :], A["x"][0, tt * 128:(tt + 1) * 128, :]) for tt in range(2)]
    load_weights(3)
    t_gr = [load(grow[i:i + 1, :], gains[i]) for i in range(1, 8)]
    load_weights(5)
    thg = []

    def first_loads():
        for i, nm in enumerate(("mem_q_norm_g", "mem_k_norm_g")):
            for l in range(2):
                thg.append(load(hg[:, 2 * i + l, :], rows128(A[nm][l]), eng="act"))
        thg.append(load(hg[:, 4, :], rows128(A["k_norm_g"]), eng="act"))
        thg.append(load(hg[:, 5, :], rows128(A["b_q_norm_g"][0]), eng="act"))
        t_mem.append(load(mem[:], A["mem"][0].rearrange("(t p) d -> p t d", p=128), eng="act"))

    t_mem, t_gn0 = [], []
    P.wait("pe", t_ident, t_g0)
    for c in range(8):
        t = T(lambda: pe.transpose(bank[4][:, c:c + 1], grow[0:1, c * 128:(c + 1) * 128], ident[0:1, 0:1]))
    t_gcol = V(lambda: dve.tensor_copy(gcol[:, :, 0], bank[4][:, 0:8]), t)
    free[4] = [t_gcol]
    for p in range(4):
        for tt in range(2):
            P.wait("pe", t_x[tt])
            for j in range(2):
                c = 2 * p + j
                t = T(lambda: pe.transpose(bank[p][:, j * 256 + tt * 128:j * 256 + (tt + 1) * 128],
                                           xn[:, tt, c * 128:(c + 1) * 128], ident[:]))
        pair = hT[:, 2 * p:2 * p + 2, :].rearrange("p a b -> p (a b)")
        if p % 2 == 0:
            t = V(lambda: dve.tensor_copy(pair, bank[p][:]), t)
        else:
            t = C(lambda: act.copy(pair, bank[p][:]), t)
        free[p] = [t]
        h_done[p] = t
    prep(0, [(0, X0, None)], False)
    split_to(0)
    prep(1, [(0, X0, None)], False)
    split_to(1)
    for p in range(2, 4):
        prep(p, [(0, X0, None)], False)
    for p in range(4):
        squares(p)
    N = norm(5)

    def other_gains():
        take(4)
        P.wait("pe", *t_gr)
        for c in range(8):
            t = T(lambda: pe.transpose(bank[4][:, c * 8:(c + 1) * 8], grow[:, c * 128:(c + 1) * 128],
                                       ident[0:8, 0:8]))
        u = V(lambda: dve.tensor_copy(gcol[:].rearrange("p a b -> p (a b)"), bank[4][:, 0:64]), t)
        free[4] = [u]
        P.wait("act", u)
        t_gn0.append(load(gn[:], rows128(A["mem_norm_g"][0]), t, eng="act"))

    at_slot(5, first_loads)
    at_slot(6, other_gains)
    st0.close()
    for e in ("act", "dve"):
        P.wait(e, h_done[3], h_done[2], ("pe_done", P.counts["pe_done"]))

    def run_ffn(which, l, x, N, targets):
        c = ExitStack()
        gh = sb(f"gh{which}{l}", [128, 22, S], F32R, c)
        gl = sb(f"gl{which}{l}", [128, 22, S], F32R, c)
        gr = sb(f"gr{which}{l}", [128, 2, 512], F32, c)
        pr = sb(f"pr{which}{l}", [128, 2, 512], F32, c)
        r = ffn(DA[which + "_w_gate"][l], DA[which + "_w_up"][l], DA[which + "_w_down"][l], x, N,
                (gh, gl, gr, pr), targets)
        c.close()
        return r

    rsm = []

    def mem_stats():
        rsm.extend(row_stats(mem, t_mem[0], xg0, None, 24))

    mem_x = []

    def mem_first():
        mem_x.extend(rows_normed(mem, t_mem[0], gn[:], t_gn0[0], rsm, xg0, None))

    def mem_turn(tt):
        to_T(lambda c: xg0[:, tt, c * 128:(c + 1) * 128], 8, X1, 0, [mem_x[tt]], [[4, 5], [6, 7]][tt], tt)
        if tt == 1:
            rsm.append(load(gn[:], rows128(A["mem_norm_g"][1]), last_T[0]))

    at_slot(18, lambda: mem_turn(0))
    at_slot(20, lambda: mem_turn(1))
    at_slot(12, mem_stats)
    at_slot(16, mem_first)
    x0_last = run_ffn("ffn1", 0, X0, N, [(1, X0, None)])
    N = norm(4)
    dump("h1", hT[:], *h_done)

    mx = ExitStack()
    hc = sb("hc", [128, 6, 30 + S], F32, mx)
    cv = sb("cv", [128, 6, S], F32, mx)
    rows = sb("rows", [34, 768], F32, mx)
    taps = sb("taps", [128, 6, 34], F32, mx)
    sg = sb("sgm", [128, 2, 512], F32, mx)
    gr = sb("grm", [128, 2, 512], F32, mx)
    qm = sb("qm", [128, 2, 256], F32, mx)
    sq = sb("sqm", [128, 2, 256], F32, mx)
    qTm = sb("qTm", [128, 4, S], F32, mx)
    att = sb("attm", [128, 2, 256], F32, mx)
    scr = sb("scrm", [128, 5, 512], F32, mx)
    pbuf, ptbuf = scr[:, 0:3, :], scr[:, 3:5, :]
    xg = scr[:, 0:4, :].rearrange("p (t a) b -> p t (a b)", t=2)
    dgs = sb("dgs", [128, NDG, 128], F32, mx)
    ffn_last = pe_done[-1]
    for e in ("act", "dve", "pool"):
        P.wait(e, ffn_last)
    tr_ = [load(rows[0:31, :], A["a_dw_kernel"][0].rearrange("k a c -> k (a c)"), eng="act"),
           load(rows[31:32, :], A["a_dw_bias"], eng="act"), load(rows[32:33, :], A["a_ln_g"], eng="act"),
           load(rows[33:34, :], A["a_ln_b"], eng="act")]
    tz = G(lambda: pool.memset(hc[:, :, 0:30], 0.0))
    tzq = G(lambda: pool.memset(qTm[:], 0.0))

    def load_taps():
        take(7)
        P.wait("pe", t_ident, *tr_)
        for c in range(6):
            t = T(lambda: pe.transpose(bank[7][:, c * 34:(c + 1) * 34], rows[:, c * 128:(c + 1) * 128],
                                       ident[0:34, 0:34]))
        st_["taps"] = V(lambda: dve.tensor_copy(taps[:].rearrange("p a b -> p (a b)"), bank[7][:, 0:204]), t)
        free[7] = [st_["taps"]]
    at_slot(3, load_taps)

    hcs = []
    dgt = []

    def diags(upto):
        while len(dgt) < min(upto, 31 * len(CONV_PE)):
            i = len(dgt)
            c, k = CONV_PE[i // 31], i % 31
            w = dgfree[i - NDG] if i >= NDG else None
            dgt.append(C(lambda: act.activation(dgs[:, i % NDG, :], ident[:], ACT.Copy, scale=taps[:, c, k:k + 1]),
                         st_["taps"], w))
    dgfree = []

    def conv_dve(cs):
        for c2 in range(0, len(cs), 2):
            pair = cs[c2:c2 + 2]
            t = {}
            for k in range(31):
                for c in pair:
                    if k == 0:
                        t[c] = V(lambda: dve.tensor_scalar(cv[:, c, :], hc[:, c, 0:S], taps[:, c, 0:1],
                                                           taps[:, c, 31:32], ALU.mult, ALU.add),
                                 hcs[c // 2], st_["taps"], tz)
                    else:
                        t[c] = V(lambda: dve.scalar_tensor_tensor(out=cv[:, c, :], in0=hc[:, c, k:k + S],
                                                                  scalar=taps[:, c, k:k + 1], in1=cv[:, c, :],
                                                                  op0=ALU.mult, op1=ALU.add), t[c])
                    if k == 30:
                        tcv[c] = t[c]
                    yield

    def conv_pe(cs, b):
        for c in cs:
            take(b)
            P.wait("pe", hcs[c // 2], tz)
            for k in range(31):
                i = len(dgfree)
                t = MMi(bank[b][:, 0:S], dgs[:, i % NDG, :], hc[:, c, k:k + S], k == 0, k == 30, dgt[i])
                dgfree.append(t)
                diags(i + 1 + NDG)
                if k % 4 == 3:
                    yield
            tcv[c] = C(lambda: act.activation(cv[:, c, :], bank[b][:, 0:S], ACT.Identity, bias=taps[:, c, 31:32]), t)
            free[b] = [tcv[c]]
            yield

    def some(gen, n):
        for _ in range(n):
            next(gen, None)

    def both(n):
        for _ in range(n):
            some(cp, 1)
            some(cd, 4)

    tcv = [None] * 6
    cd = conv_dve(CONV_DVE)
    sgf = [None, None]
    for p in range(3):
        ba, bg = (0, 1) if p % 2 == 0 else (2, 3)
        t1 = lin_A(X0, ain, 8, p * 256, ba)
        t2 = lin_A(X0, ain, 8, 768 + p * 256, bg)
        if p == 0:
            P.wait("pool", st_["taps"])
        r = gr[:, p % 2, :].rearrange("p (a b) -> p a b", a=2)
        s_ = sg[:, p % 2, :].rearrange("p (a b) -> p a b", a=2)
        b3 = lambda b: bank[b][:].rearrange("p (a b) -> p a b", a=2)
        tr = V(lambda: dve.tensor_tensor(r, b3(bg), wide(N.row, 1, 2), ALU.mult), t2, N.t_row, sgf[p % 2])
        free[bg] = [tr]
        ts = C(lambda: act.activation(s_, r, ACT.Sigmoid), tr, sgf[p % 2])
        ta = V(lambda: dve.tensor_tensor(r, b3(ba), wide(N.row, 1, 2), ALU.mult), ts, t1)
        free[ba] = [ta]
        row_free[N.i] = ta
        tm = V(lambda: dve.tensor_tensor(hc[:, 2 * p:2 * p + 2, 30:30 + S], s_, r, ALU.mult), ta, tz)
        sgf[p % 2] = tm
        hcs.append(tm)
        diags((6, 11, NDG)[p])
        if p:
            some(cd, 10)
    cp = conv_pe(CONV_PE, 7)
    tq = run(lin_B(X0, ain, 8, 1536, 256, [[5], [6]]))
    x0_last = tq
    tqs = []
    for tt in range(2):
        t = C(lambda: act.activation(qm[:, tt, :], bank[5 + tt][:, 0:256], ACT.Copy, scale=N.col[tt]), tq, N.t_col)
        free[5 + tt] = [t]
        tqs.append(t)
    some(cd, 8)

    tmk, tmv = [[], []], [[], []]

    def mem_kv(l, x, bk, each, mid, between):
        for t in lin_B(x, DA["w_mem_kv"][l], 8, 0, 512, bk):
            each()
        for tt in range(2):
            b = bk[tt][0]
            t2 = C(lambda: act.copy(mkv[l][:, tt, :], bank[b][:]), t)
            free[b] = [t2]
            tmv[l].append(t2)
            tmk[l].append(head_rms(mkv[l][:, tt, 0:256], 4, 32 + 64 * tt, hg[:, 2 + l, :], thg[2 + l],
                                   mkv[l][:, tt, 0:256], [t2], sq[:, tt, :], mid))
        between()
        tmk[l] = [plain_T(lambda j: mkv[l][:, tt, j * 128:(j + 1) * 128], 2,
                          kTm[l][:, :, tt * 128:(tt + 1) * 128], [t3], bk[tt][0]) for tt, t3 in enumerate(tmk[l])]

    tqn = []

    def q_heads():
        for tt in range(2):
            yield
            tqn.append(head_rms(qm[:, tt, :], 4, 32 + 64 * tt, hg[:, 0, :], thg[0], qm[:, tt, :], [tqs[tt]],
                                sq[:, tt, :], lambda: some(cd, 3)))
            some(cd, 1)

    qh = q_heads()

    def kv0_step():
        some(cd, 2)
        next(qh, None)

    mem_kv(0, X1, [[4], [5]], kv0_step, lambda: some(cd, 3), lambda: some(cp, 8))
    x1_last = pe_done[-1]
    P.wait("dve", x0_last)
    from_rows(mem, t_mem[0], gn[:], rsm[2], X0, LOWB, rsm, xg, None)
    both(8)

    def mem_jobs(l, qTp, ready, oc0):
        jobs = []
        for tt in range(2):
            for c in range(2):
                heads = []
                for h in range(2):
                    heads.append((lambda tt, c=c, h=h: qTp[:, 2 * c + h, tt * 128:(tt + 1) * 128],
                                  lambda kw, c=c: kTm[l][:, c, :],
                                  lambda k, c=c, h=h: mkv[l][:, k, 256 + (2 * c + h) * 64:256 + (2 * c + h + 1) * 64]))
                jobs.append((tt, False, heads, oc0 + c * 128, ready + tmk[l] + tmv[l]))
        return jobs

    tqT = []
    for tt in range(2):
        tqT.append(padded_T(lambda j: qm[:, tt, j * 128:(j + 1) * 128], 2, qTm, 0, tt, [tqn[tt], tzq], 6))
    for t in attend(mem_jobs(0, qTm, tqT, 0), pbuf, ptbuf, att, 160, [0, 2, 4, 6], 5):
        some(cd, 6)
        some(cp, 3)
    tatt = t
    some(cd, 500)
    some(cp, 500)
    XS = X1
    P.wait("act", x1_last)
    P.wait("dve", x1_last)
    for tt in range(2):
        to_T(lambda c: att[:, tt, c * 128:(c + 1) * 128], 2, XS, 6, [tatt], [tt], tt)

    take(2)
    take(3)
    for c in range(6):
        t = MMi(bank[2][:, 0:S], ln1[:], cv[:, c, :], c == 0, c == 5, t_ln1, tcv[c])
    gm = lin_B(X0, DA["w_mem_kv"][1], 8, 0, 512, [[4], [5]])
    next(gm)
    hcv = hc[:, :, 0:S]
    for c in range(6):
        u = V(lambda: dve.tensor_tensor(cv[:, c, :], cv[:, c, :], bank[2][:, 0:S], ALU.subtract), t, tcv[c])
        ts = C(lambda: act.activation(hcv[:, c, :], cv[:, c, :], ACT.Square), u)
        for tt in range(2):
            t2 = MMi(bank[3][:, 4 * tt:4 * tt + 4], hcv[:, c, tt * 128:(tt + 1) * 128], ones[:, 0:4],
                     c == 0 and tt == 0, c == 5, ts)
    free[2] = [u]
    next(gm)
    var, rst = small[:, 24:26], small[:, 26:28]
    t2 = V(lambda: dve.tensor_scalar(var, bank[3][:, 0:8:4], 1.0 / 768, EPS, ALU.mult, ALU.add), t2)
    t2 = G(lambda: pool.tensor_tensor(rst, var, mhalf[:, 0:2], ALU.pow), t2)
    td = [V(lambda: dve.tensor_scalar(diag[:, tt, :], ident[:], rst[:, tt:tt + 1], None, ALU.mult), t2,
            st_["dgfree"]) for tt in range(2)]
    for tt in range(2):
        t3 = MMi(bank[3][:, 128 + tt * 128:256 + tt * 128], ones[:], diag[:, tt, :], True, True, td[tt])
    st_["dgfree"] = t3
    u3s = []
    for c in range(6):
        while len(u3s) < min(6, c + 3):
            e = len(u3s)
            u3s.append(V(lambda: dve.tensor_tensor(cv[:, e, :], cv[:, e, :], bank[3][:, 128:384], ALU.mult), t3))
        u3 = u3s[c]
        t4 = C(lambda: act.activation(cv[:, c, :], cv[:, c, :], ACT.Silu, bias=taps[:, c, 33:34],
                                      scale=taps[:, c, 32:33]), u3)
        t5 = C(lambda: act.copy(XS[0][:, c, :], cv[:, c, :]), t4)
        t6 = V(lambda: dve.tensor_tensor(XS[1][:, c, :], cv[:, c, :], XS[0][:, c, :].bitcast(F32), ALU.subtract), t5)
        XS[2][c] = [t5, t6]
    free[3] = [u3s[-1]]
    for tg_ in gm:
        pass
    x0_last = pe_done[-1]
    dump("prim", cv[:], t4)
    dump("mo", att[:], tatt)
    for p in range(4):
        t = lin_A(XS, DA["w_o"][0], 8, p * 256, p)
        if p == 0:
            for tt in range(2):
                t2 = C(lambda: act.copy(mkv[1][:, tt, :], bank[4 + tt][:]), tg_)
                free[4 + tt] = [t2]
                tmv[1].append(t2)
        add_h(p, p, t, 1.0, None, [(2, X0, x0_last)], None, None)
    x1_last = pe_done[-1]
    N = norm(4)
    mx.close()
    mm.close()
    dump("h2", hT[:], *h_done)
    for e in ("dve", "act"):
        P.wait(e, x1_last, ("act_done", P.counts["act_done"]) if e == "dve" else ("dve_done", P.counts["dve_done"]),
               *dumps)

    kg1 = heads_rms([(mkv[1][:, tt, 0:256], 4, 32 + 64 * tt, hg[:, 3, :], thg[3], mkv[1][:, tt, 0:256],
                      [tmv[1][tt]], htmp[:, tt, 0:256]) for tt in range(2)])

    def kv1_heads():
        t = next(kg1)
        if t:
            tmk[1].append(t)

    def kv1_turn():
        tmk[1] = [plain_T(lambda j: mkv[1][:, tt, j * 128:(j + 1) * 128], 2,
                          kTm[1][:, :, tt * 128:(tt + 1) * 128], [t3], 6 + tt) for tt, t3 in enumerate(tmk[1])]

    for i in range(4):
        at_slot(8 + 2 * i, kv1_heads)
    at_slot(20, kv1_turn)
    x0_last = run_ffn("ffn2", 0, X0, N, [(3, X1, x1_last), (4, X0, None)])
    N = norm(4)
    dump("h3", hT[:], *h_done)

    kv = ExitStack()
    kT = sb("kT", [128, 6, S], F32, kv)
    vn = sb("vn", [128, 2, 768], F32, kv)
    cs = sb("cs", [128, 2, 2, 8], F32, kv)
    posi = sb("posi", [128, 2, 1], I32, kv)
    posf = sb("posf", [128, 2], F32, kv)
    freq = sb("freq", [128, 8], F32, kv)
    ang = sb("ang", [128, 2, 2, 8], F32, kv)
    rd = sb("rd", [128, 2, 2, 8], F32, kv)
    ffn_last = pe_done[-1]
    for e in ("act", "dve", "pool"):
        P.wait(e, ffn_last)

    t_pos = load(posi[:], A["positions"][0].rearrange("(t p o) -> p t o", p=128, o=1), slow=True, eng="act")
    t_cs = []

    def rotary():
        t = V(lambda: dve.tensor_copy(posf[:], posi[:, :, 0]), t_pos)
        fr = (1.0 / (np.float32(500000.0) ** (np.arange(0, 16, 2, dtype=np.float32) / np.float32(16)))).astype(np.float32)
        for i in range(8):
            tf = G(lambda: pool.memset(freq[:, i:i + 1], float(fr[i])))
        for tt in range(2):
            t = V(lambda: dve.tensor_scalar(ang[:, tt, 1, :], freq[:], posf[:, tt:tt + 1], None, ALU.mult), t, tf)
        c1, left = 6.28125, 2 * np.pi - 6.28125
        c2 = float(np.float32(round(left * 2 ** 19) / 2 ** 19))
        c3 = float(np.float32(left - c2))
        magic = 12582912.0
        a1 = ang[:, :, 1, :]
        k1 = rd[:, :, 1, :]
        t = V(lambda: dve.tensor_scalar(k1, a1, float(1 / (2 * np.pi)), magic, ALU.mult, ALU.add), t)
        t = V(lambda: dve.tensor_scalar(k1, k1, -magic, None, ALU.add), t)
        for c in (c1, c2, c3):
            t = V(lambda: dve.scalar_tensor_tensor(out=a1, in0=k1, scalar=-c, in1=a1, op0=ALU.mult, op1=ALU.add), t)
        a0 = ang[:, :, 0, :]
        k0 = rd[:, :, 0, :]
        t = V(lambda: dve.tensor_scalar(a0, a1, float(np.pi / 2), None, ALU.add), t)
        t = V(lambda: dve.tensor_scalar(k0, a0, float(np.pi), None, ALU.is_gt), t)
        t = V(lambda: dve.scalar_tensor_tensor(out=a0, in0=k0, scalar=-float(2 * np.pi), in1=a0, op0=ALU.mult,
                                               op1=ALU.add), t)
        t = V(lambda: dve.tensor_scalar(ang[:], ang[:], 3.1415925, -3.1415925, ALU.min, ALU.max), t)
        t_cs.append(C(lambda: act.activation(cs[:], ang[:], ACT.Sin), t))

    at_slot(12, rotary)
    Nkv = N
    x0_last = run_ffn("ffn1", 1, X0, N, [(5, X0, None)])
    N = norm(7)
    dump("h4", hT[:], *h_done)
    def rope(x, tt, nh, tmp, t):
        v = x.rearrange("p (h d) -> p h d", d=64)
        x1, x2 = v[:, :, 0:8], v[:, :, 8:16]
        co = wide(cs[:, tt, 0, :], 1, nh)
        si = wide(cs[:, tt, 1, :], 1, nh)
        m = [tmp[:, i, :].rearrange("p (h d) -> p h d", d=8) for i in range(4)]
        for o, a, b in ((m[0], x1, co), (m[1], x2, si), (m[2], x2, co), (m[3], x1, si)):
            u = V(lambda: dve.tensor_tensor(o, a, b, ALU.mult), t, t_cs[0])
        V(lambda: dve.tensor_tensor(x1, m[0], m[1], ALU.subtract), u)
        return V(lambda: dve.tensor_tensor(x2, m[2], m[3], ALU.add), u)

    mx = ExitStack()
    kn = sb("kn", [128, 2, 768], F32, mx)
    qn = sb("qn", [128, 2, D], F32, mx)
    rtmp = sb("rtmp1", [128, 2, 4, 96], F32, mx)
    qT = sb("qT", [128, 16, S], F32, mx)
    att = sb("att1", [128, 2, D], F32, mx)
    sq = att
    pbuf = sb("pb1", [128, 3, 512], F32, mx)
    ptbuf = sb("pt1", [128, 2, 512], F32, mx)
    ffn_last = pe_done[-1]
    for e in ("act", "dve", "pool"):
        P.wait(e, ffn_last)
    tzq = G(lambda: pool.memset(qT[:], 0.0))

    def out_rows(dst, b, n, c, t, tc, eng):
        if eng == "act":
            u = C(lambda: act.activation(dst, bank[b][:, 0:n], ACT.Copy, scale=c), t, tc)
        else:
            u = V(lambda: dve.tensor_scalar(dst, bank[b][:, 0:n], c, None, ALU.mult), t, tc)
        free[b] = [u]
        return u

    BQ = [[0, 1], [2, 3]]
    BV = [[4, 5], [6, 0]]
    KB = [[4, 5], [6, 0]]
    t = run(lin_B(X1, DA["w_kv"], 8, 0, 768, KB))
    tkv = [(out_rows(kn[:, tt, 0:512], KB[tt][0], 512, Nkv.col[tt], t, Nkv.t_col, "act"),
            out_rows(kn[:, tt, 512:768], KB[tt][1], 256, Nkv.col[tt], t, Nkv.t_col, "act")) for tt in range(2)]
    BQ = [[1, 2], [3, 4]]
    gq = lin_B(X0, DA["b_w_in"][0], 8, 0, D, BQ)
    next(gq)
    tkr = []
    kg = heads_rms([(kn[:, tt, :], 12, 32 + 64 * tt, hg[:, 4, :], thg[4], kn[:, tt, :], list(tkv[tt]),
                     sq[:, tt, 0:768]) for tt in range(2)])
    for tt in range(2):
        next(kg)
        next(gq)
    for tt in range(2):
        tkr.append(rope(kn[:, tt, :], tt, 12, rtmp[:, tt], next(kg)))
        next(gq)
    for t in gq:
        pass
    x0_last = t
    rp = [(out_rows(qn[:, tt, 0:512], BQ[tt][0], 512, N.col[tt], t, N.t_col, "act"),
           out_rows(qn[:, tt, 512:1024], BQ[tt][1], 512, N.col[tt], t, N.t_col, "dve")) for tt in range(2)]
    BV = [[5, 6], [7, 0]]
    gv = lin_B(X1, DA["w_kv"], 8, 768, 768, BV)
    hold(8)
    C(lambda: act.activation(small[0:1, 319:320], ones[0:1, 0:1], ACT.Exp), t_ones)
    next(gv)
    tkT = []
    for tt in range(2):
        tkT.append(plain_T(lambda j: kn[:, tt, j * 128:(j + 1) * 128], 4,
                           kT[:, 0:4, tt * 128:(tt + 1) * 128], [tkr[tt]], 1))
        tkT.append(plain_T(lambda j: kn[:, tt, (4 + j) * 128:(5 + j) * 128], 2,
                           kT[:, 4:6, tt * 128:(tt + 1) * 128], [tkr[tt]], 2))
    tq_ = [None, None]
    qjobs = []
    for tt in range(2):
        u, w = rp[tt]
        qjobs.append((qn[:, tt, 0:768], 12, 32 + 64 * tt, hg[:, 5, :], thg[5], qn[:, tt, 0:768], [u, w],
                      sq[:, tt, 0:768]))
        qjobs.append((qn[:, tt, 768:], 4, 44 + 64 * tt, hg[:, 1, :], thg[1], qn[:, tt, 768:], [w], sq[:, tt, 768:]))
    qg = heads_rms(qjobs)
    for i in range(4):
        next(qg)
        if i % 2:
            next(gv)
    for tt in range(2):
        v1 = rope(qn[:, tt, 0:768], tt, 12, rtmp[:, tt], next(qg))
        v2 = next(qg)
        tq_[tt] = [v1, v2, tzq]
        next(gv)
        if tt:
            let_go()
            next(gv)
    tqT = []
    for tt in range(2):
        if tt == 1:
            for t in gv:
                pass
            x1_last = t
        tqT.append([padded_T(lambda j: qn[:, tt, (j0 + j) * 128:(j0 + j + 1) * 128], 4, qT, j0, tt,
                             tq_[tt], 1 + tt * 2 + j0 // 4) for j0 in (0, 4)][-1])
    for tt in range(2):
        t_vn = [out_rows(vn[:, tt, 0:512], BV[tt][0], 512, Nkv.col[tt], t, Nkv.t_col, "act"),
                out_rows(vn[:, tt, 512:768], BV[tt][1], 256, Nkv.col[tt], t, Nkv.t_col, "dve")]
    dump("kn", kn[:], tkr[-1])
    dump("vn", vn[:], *t_vn)
    dump("qn", qn[:], v1, v2)
    jobs = []
    for tt in range(2):
        for c in range(6):
            heads = [(lambda tt, c=c, h=h: qT[:, 2 * c + h, tt * 128:(tt + 1) * 128],
                      lambda kw, c=c: kT[:, c, 0:kw],
                      lambda k, c=c, h=h: vn[:, k, (2 * c + h) * 64:(2 * c + h + 1) * 64]) for h in range(2)]
            jobs.append((tt, True, heads, c * 128, [tqT[tt]] + t_vn + tkT))
        jobs += [j for j in mem_jobs(1, qT[:, 12:16, :], [tqT[tt]], 768) if j[0] == tt]
    P.wait("act", x1_last)
    P.wait("dve", x1_last)
    ga_ = attend(jobs, pbuf, ptbuf, att, 160, [0, 2, 4, 6], 5)
    for n_, tatt in enumerate(ga_):
        if n_ == 11:
            to_T(lambda c: att[:, 0, c * 128:(c + 1) * 128], 8, X1, 0, [tatt], [7], 0)
    dump("att", att[:], tatt)
    to_T(lambda c: att[:, 1, c * 128:(c + 1) * 128], 8, X1, 0, [tatt], [0, 1], 1)
    for p in range(4):
        t = lin_A(X1, DA["w_o"][1], 8, p * 256, [2, 3, 4, 5][p])
        add_h(p, [2, 3, 4, 5][p], t, 1.0, None, [(6, X0, x0_last)], None, None)
    x1_last = pe_done[-1]
    N = norm(6)
    mx.close()
    kv.close()
    for e in ("act", "dve", "pool"):
        P.wait(e, t, *dumps)
    dump("h5", hT[:], *h_done)

    x0_last = run_ffn("ffn2", 1, X0, N, [(7, X0, None)])
    N = norm(4)
    dump("h6", hT[:], *h_done)

    mx = ExitStack()
    va = sb("va", [128, 2, 512], F32, mx)
    vb = sb("vb", [128, 2, 512], F32, mx)
    zob = sb("zob", [128, 3, 2, 512], F32, mx)
    qk = sb("qk", [128, 8, 3 + S], F32, mx)
    qkc = sb("qkc", [128, 8, S], F32, mx)
    aq = sb("aq", [128, 8, S], F32, mx)
    ak = sb("ak", [128, 4, S], F32, mx)
    ctap = sb("ctap", [128, 8, 4], F32, mx)
    lam = sb("lam", [128, 8], F32, mx)
    gt = sb("gt", [128, 2, 8], F32, mx)
    gates = sb("gates", [128, 2, 64], F32, mx)
    bif = sb("bif", [128, 8], F32, mx)
    oa = sb("oa", [128, 2, 512], F32, mx)
    ob = sb("ob", [128, 2, 512], F32, mx)
    pbuf = sb("pb2", [128, 3, 512], F32, mx)
    ptbuf = sb("pt2", [128, 2, 256], F32, mx)
    crow = pbuf[0:4, 0:2, :].rearrange("p a b -> p (a b)")
    lamr = ptbuf[:, 0, :].rearrange("p (a d) -> p a d", a=4)
    ga_t = qk[:].rearrange("p a b -> p (a b)")[:, 0:2048].rearrange("p (a b) -> p a b", b=S)
    gb_t = aq
    nab = va
    ffn_last = pe_done[-1]
    for e in ("act", "dve", "pool"):
        P.wait(e, ffn_last)

    t_crow = load(crow, A["conv_qk_2"][0], eng="act")
    t_lam = load(ptbuf[:, 0, :], rows128(A["lambda_qk_2"].rearrange("a b d -> (a b d)")), eng="act")
    t_bif = load(bif[:], rows128(A["b_if_2"][0]), eng="act")
    tz = G(lambda: pool.memset(qk[:, :, 0:3], 0.0))
    tzq = G(lambda: pool.memset(aq[:], 0.0))

    def load_ctap():
        take(5)
        P.wait("pe", t_crow)
        for c in range(8):
            t = T(lambda: pe.transpose(bank[5][:, c * 4:(c + 1) * 4], crow[:, c * 128:(c + 1) * 128], ident[0:4, 0:4]))
        st_["ctap"] = V(lambda: dve.tensor_copy(ctap[:].rearrange("p a b -> p (a b)"), bank[5][:, 0:32]), t)
        free[5] = [st_["ctap"]]
        st_["pf0"] = t
    at_slot(3, load_ctap)

    tcv4 = [None] * 8

    def conv4():
        for c2 in range(0, 8, 2):
            t = {}
            for k in range(4):
                for c in (c2, c2 + 1):
                    if k == 0:
                        t[c] = V(lambda: dve.tensor_scalar(qkc[:, c, :], qk[:, c, 0:S], ctap[:, c, 0:1], None,
                                                           ALU.mult), tqk[c // 2], st_["ctap"], tz)
                    else:
                        t[c] = V(lambda: dve.scalar_tensor_tensor(
                            out=qkc[:, c, :], in0=qk[:, c, k:k + S], scalar=ctap[:, c, k:k + 1], in1=qkc[:, c, :],
                            op0=ALU.mult, op1=ALU.add), t[c])
                    tcv4[c] = t[c]
                    yield

    def scaled(o, b, t, q=slice(0, 128)):
        return V(lambda: dve.tensor_tensor(o, bank[b][q, :].rearrange("p (a n) -> p a n", a=2),
                                           wide(N.row[q], 1, 2), ALU.mult), t, N.t_row)

    tqk = []
    cg = conv4()
    tl_ = []
    for c in range(5):
        if c < 4:
            tl_.append(lin_A(X0, win, 8, 2048 + c * 256, c))
        if c > 0:
            t = scaled(qk[:, 2 * c - 2:2 * c, 3:3 + S], c - 1, tl_[c - 1])
            free[c - 1] = [t]
            tqk.append(t)
            some(cg, 8)

    l12 = lamr[:, 0:3:2, :]
    t = V(lambda: dve.tensor_tensor(l12, l12, lamr[:, 1:4:2, :], ALU.mult), t_lam)
    t = V(lambda: dve.reduce_sum(lam[:, 0:2], l12, AX), t)
    t = C(lambda: act.activation(lam[:, 2:4], lam[:, 0:2], ACT.Exp), t)
    t = V(lambda: dve.tensor_tensor(lam[:, 4:5], lam[:, 3:4], lam[:, 2:3], ALU.subtract), t)
    lam_init = 0.8 - 0.6
    t_lamn = V(lambda: dve.tensor_scalar(lam[:, 5:6], lam[:, 4:5], -lam_init, None, ALU.add), t)

    take(6)
    take(5)
    s = next_slot((0, 8, 4608, 8))
    P.wait("pe", s.th, s.tl)
    for tt in range(2):
        b = 5 + tt
        for k in range(8):
            l = [X0[i][:, k, tt * 128:(tt + 1) * 128] for i in range(2)]
            o = bank[b][:, 0:8]
            MM(o, l[0], s.hi[:, k, :], k == 0, False)
            MM(o, l[1], s.hi[:, k, :], False, False)
            t = T(lambda: pe.matmul(o, l[0], s.lo[:, k, :], start=False, stop=k == 7, skip_group_check=True), sem="w")
        u = V(lambda: dve.scalar_tensor_tensor(out=gt[:, tt, :], in0=bank[b][:, 0:8], scalar=N.col[tt], in1=bif[:],
                                               op0=ALU.mult, op1=ALU.add), t, t_bif, N.t_col)
        free[b] = [u]
    pe_done.append(t)
    t_gt = u

    taT = []
    for c in range(4):
        b = c
        t = lin_A(X0, win, 8, c * 256, b)
        if c < 2:
            for e in range(2):
                q = slice(64 * e, 64 * e + 64)
                u = scaled(aq[q, 4 * c + e:4 * c + e + 3:2, :], b, t, q)
                P.wait("dve", tzq)
        else:
            u = scaled(ak[:, 2 * c - 4:2 * c - 2, :], b, t)
        free[b] = [u]
        taT.append(u)
    some(cg, 100)
    tcc = []
    for h in range(2):
        tcc.append(C(lambda: act.activation(qkc[:, 4 * h:4 * h + 4, :], qkc[:, 4 * h:4 * h + 4, :], ACT.Silu),
                     tcv4[4 * h + 3], tcv4[4 * h + 2]))
    tcc.append(V(lambda: dve.tensor_scalar(qkc[:, 4:8, :], qkc[:, 4:8, :], 128.0 ** -0.5, None, ALU.mult), tcc[1]))

    fg = gt[:, :, 4:8]
    e1 = gates[:, :, 0:4]
    e2 = gates[:, :, 4:8]
    lf = gates[:, :, 8:12]
    Fc = gates[:, :, 12:16]
    w_ = gates[:, :, 16:20]
    t = V(lambda: dve.tensor_scalar(e1, fg, -1.0, None, ALU.mult), t_gt)
    t = V(lambda: dve.tensor_tensor(e1, e1, fg, ALU.min), t)
    t = C(lambda: act.activation(e2, e1, ACT.Exp), t)
    t = C(lambda: act.activation(e2, e2, ACT.Ln, bias=1.0), t)
    u = V(lambda: dve.tensor_scalar(lf, fg, 0.0, None, ALU.min), t_gt)
    t_lf = V(lambda: dve.tensor_tensor(lf, lf, e2, ALU.subtract), t, u)

    gv = lin_B(X0, win, 8, 3072, 512, [[5], [6]])
    next(gv)
    for t in gv:
        pass
    for tt in range(2):
        u = V(lambda: dve.tensor_scalar(vb[:, tt, :], bank[5 + tt][:], N.col[tt], None, ALU.mult), t, N.t_col)
        free[5 + tt] = [u]
    t_vb = u
    t = run(lin_B(X0, win, 8, 1024, 512, [[4], [7]]))
    for tt, b in enumerate((4, 7)):
        u = V(lambda: dve.tensor_scalar(va[:, tt, :], bank[b][:], N.col[tt], None, ALU.mult), t, N.t_col)
        free[b] = [u]
    t_va = u
    take(4)
    MM(bank[4][:, 0:4], upper[:], gates[:, 0, 8:12], True, True, t_lf, t_upper)
    MM(bank[4][:, 4:8], ones[:], gates[:, 0, 8:12], True, False)
    t = MMi(bank[4][:, 4:8], upper[:], gates[:, 1, 8:12], False, True)
    t = V(lambda: dve.tensor_copy(Fc, bank[4][:, 0:8].rearrange("p (a b) -> p a b", a=2)), t)
    free[4] = [t]
    t_w = V(lambda: dve.tensor_tensor(w_, gt[:, :, 0:4], Fc, ALU.subtract), t)
    dump("F", gates[:], t_w)

    tzo = [[], [], []]
    tgab = []

    pending = []

    def flush():
        while pending:
            pending.pop(0)()

    def rest():
        def rows_out(i, t):
            for tt in range(2):
                if tt:
                    u = V(lambda: dve.tensor_scalar(zob[:, i, tt, :], bank[6 + tt][:], N.col[tt], None, ALU.mult), t)
                else:
                    u = C(lambda: act.activation(zob[:, i, tt, :], bank[6 + tt][:], ACT.Copy, scale=N.col[tt]), t,
                          N.t_col)
                free[6 + tt] = [u]
                tzo[i].append(u)

        def cols_out(c, b, t):
            g_ = ga_t if c < 4 else gb_t
            u = scaled(g_[:, 2 * (c % 4):2 * (c % 4) + 2, :], b, t)
            free[b] = [u]
            tgab.append(u)

        for i, c0 in enumerate((1536, 3584, 4096)):
            for k, t in enumerate(lin_B(X0, win, 8, c0, 512, [[6], [7]])):
                if k == 3:
                    pending.append(lambda i=i, t=t: rows_out(i, t))
                yield
                flush()
        for c in range(8):
            b = 6 + c % 2
            for k, t in enumerate(lin_A_steps(X0, win, 8, 4616 + c * 256, b)):
                if k == 1:
                    pending.append(lambda c=c, b=b, t=t: cols_out(c, b, t))
                yield
                flush()
    rg = rest()

    st = [dict() for _ in range(8)]
    pf, ptf = [st_["pf0"]] * 3, [None] * 2
    toa = []

    def d_scores(i):
        tt, h = i // 4, i % 4
        kw = 128 * (tt + 1)
        b = 2 * (i % 2)
        take(b)
        take(b + 1)
        P.wait("pe", t_alib, t_identb, *taT)
        ps = psum[:, b:b + 2, 0:kw]
        for c in range(2):
            MM(ps[:, c, :], aq[:, 2 * h + c, tt * 128:(tt + 1) * 128], ak[:, h, 0:kw], True, False)
            t = MMi(ps[:, c, :], identb[:], alib[:, tt, h, 0:kw], False, True)
        col0 = 160 + 12 * (i % 3)
        mx_, nb, sm, rc = (small[:, col0 + 2 * q:col0 + 2 * q + 2] for q in range(4))
        t = V(lambda: dve.reduce_max(mx_, ps, AX), t, st[i - 3]["fin"] if i >= 3 else None)
        t = V(lambda: dve.tensor_scalar(nb, mx_, -0.125, None, ALU.mult), t)
        p = pbuf[:, i % 3, 0:2 * kw].rearrange("p (c k) -> p c k", c=2)
        for c in range(2):
            te = C(lambda: act.activation(p[:, c, :], ps[:, c, :], ACT.Exp, bias=nb[:, c:c + 1], scale=0.125,
                                          accum_out=sm[:, c:c + 1]), t, pf[i % 3])
        free[b] = free[b + 1] = [te]
        t = V(lambda: dve.reciprocal(rc, sm), te)
        t = V(lambda: dve.tensor_scalar(rc[:, 1:2], rc[:, 1:2], lam[:, 5:6], None, ALU.mult), t, t_lamn)
        t = V(lambda: dve.tensor_scalar(p[:, 1, :], p[:, 1, :], rc[:, 1:2], None, ALU.mult), t)
        t = V(lambda: dve.scalar_tensor_tensor(out=p[:, 0, :], in0=p[:, 0, :], scalar=rc[:, 0:1], in1=p[:, 1, :],
                                               op0=ALU.mult, op1=ALU.add), t)
        st[i].update(p=p[:, 0, :], tp=t, kw=kw)

    def pv_turn(st, i):
        s = st[i]
        nk = s["kw"] // 128
        take(4)
        P.wait("pe", s["tp"])
        for k in range(nk):
            t = T(lambda: pe.transpose(bank[4][:, k * 128:(k + 1) * 128], s["p"][:, k * 128:(k + 1) * 128], ident[:]))
        pf[i % 3] = t
        s["pt"] = C(lambda: act.copy(ptbuf[:, i % 2, 0:nk * 128], bank[4][:, 0:nk * 128]), t, ptf[i % 2])
        free[4] = [s["pt"]]

    def pv_values(st, i, v, tv, b):
        h = i % 4
        s = st[i]
        nk = s["kw"] // 128
        take(b)
        P.wait("pe", s["pt"], tv)
        for k in range(nk):
            t = T(lambda: pe.matmul(bank[b][:, 0:128], ptbuf[:, i % 2, k * 128:(k + 1) * 128],
                                    v[:, k, h * 128:(h + 1) * 128], start=k == 0, stop=k == nk - 1,
                                    skip_group_check=True))
        ptf[i % 2] = t
        return t

    def diff():
        for i in range(10):
            flush()
            if i < 8:
                d_scores(i)
            if 0 <= i - 1 < 8:
                pv_turn(st, i - 1)
            if 0 <= i - 2 < 8:
                j = i - 2
                t = pv_values(st, j, va, t_va, 5)
                u = V(lambda: dve.tensor_copy(oa[:, j // 4, (j % 4) * 128:(j % 4 + 1) * 128], bank[5][:, 0:128]), t)
                free[5] = [u]
                st[j]["fin"] = u
                toa.append(u)
            yield
    for _ in diff():
        next(rg, None)
    dump("oa", oa[:], toa[-1])
    t_na = load(nab[:, 0, :], rows128(A["norm_a_2"][0]), toa[-1], eng="act")
    t_nb = load(nab[:, 1, :], rows128(A["norm_b_2"][0]), toa[-1], eng="act")

    flat = lambda a: a.rearrange("p a b -> p (a b)")

    st2 = [dict() for _ in range(8)]
    tob = []
    wdf = [[None, None], [None, None]]
    wds = [diag, flat(ak[:])[:, 0:256].rearrange("p (k n) -> p k n", k=2)]
    wdt = {}

    def diag_w(i):
        if i < 8:
            tt, h = i // 4, i % 4
            wdt[i] = [V(lambda: dve.tensor_scalar(wds[i % 2][:, k, :], ident[:], gates[:, k, 16 + h:17 + h], None,
                                                  ALU.mult), t_w, wdf[i % 2][k], t_ident) for k in range(tt + 1)]

    diag_w(0)

    def m_scores(i):
        tt, h = i // 4, i % 4
        kw = 128 * (tt + 1)
        b = i % 3
        wd, td = wds[i % 2], wdt[i]
        take(b)
        P.wait("pe", *tcc)
        MM(bank[b][:, 0:kw], qkc[:, h, tt * 128:(tt + 1) * 128], qkc[:, 4 + h, 0:kw], True, False)
        for k in range(tt + 1):
            t = MMi(bank[b][:, kw + k * 128:kw + (k + 1) * 128], ones[:], wd[:, k, :], False, False, td[k], t_ones)
            wdf[i % 2][k] = t
        t = MMi(bank[b][:, 2 * kw - 128:2 * kw], identb[:], maskb[:], False, True)
        wr = bank[b][:, kw:2 * kw]
        col0 = 160 + 12 * (i % 3)
        M, nM, e, den, r = (small[:, col0 + q:col0 + q + 1] for q in range(5))
        t = V(lambda: dve.reduce_max(M, wr, AX), t, st2[i - 3]["fin"] if i >= 3 else None)
        t = V(lambda: dve.tensor_scalar(nM, M, 0.0, -1.0, ALU.max, ALU.mult), t)
        p = pbuf[:, i % 3, 0:2 * kw].rearrange("p (c k) -> p c k", c=2)
        te = C(lambda: act.activation(p[:, 1, :], wr, ACT.Exp, bias=nM), t, pf[i % 3])
        diag_w(i + 1)
        tF = V(lambda: dve.tensor_tensor(e, nM, gates[:, tt, 12 + h:13 + h], ALU.subtract), t)
        tF = C(lambda: act.activation(e, e, ACT.Exp), tF)
        t = V(lambda: dve.tensor_tensor(p[:, 0, :], bank[b][:, 0:kw], p[:, 1, :], ALU.mult), te, pf[i % 3])
        free[b] = [te, t]
        st2[i].update(p=p[:, 0, :], tp=t, kw=kw)
        t = V(lambda: dve.reduce_sum(den, p[:, 0, :], AX), t)
        t = V(lambda: dve.tensor_scalar(M, den, -1.0, None, ALU.mult), t)
        t = V(lambda: dve.tensor_tensor(den, den, M, ALU.max), t)
        t = V(lambda: dve.tensor_tensor(den, den, e, ALU.max), t, tF)
        t = V(lambda: dve.reciprocal(r, den), t)
        st2[i].update(r=r, tr=t)

    def mlstm():
        for i in range(10):
            flush()
            if i < 8:
                m_scores(i)
            if 0 <= i - 1 < 8:
                pv_turn(st2, i - 1)
            if 0 <= i - 2 < 8:
                j = i - 2
                t = pv_values(st2, j, vb, t_vb, 5)
                u = V(lambda: dve.tensor_scalar(ob[:, j // 4, (j % 4) * 128:(j % 4 + 1) * 128],
                                                bank[5][:, 0:128], st2[j]["r"], None, ALU.mult), t, st2[j]["tr"])
                free[5] = [u]
                st2[j]["fin"] = u
                tob.append(u)
            yield

    f1 = lambda i: zob[:, i].rearrange("p a b -> p (a b)")
    flat = lambda a: a.rearrange("p a b -> p (a b)")
    tsg = C(lambda: act.activation(f1(1), f1(1), ACT.Sigmoid), *tzo[1])
    tsa = C(lambda: act.activation(f1(0), f1(0), ACT.Silu), *tzo[0])

    def head128(x, z, ng, tng, mul, ready, tz_, c0, scratch, res):
        v = x.rearrange("p (g d) -> p g d", d=128)
        q = scratch.rearrange("p (g d) -> p g d", d=128)
        ss, r_ = small[:, c0:c0 + 8], small[:, c0 + 8:c0 + 16]
        t = V(lambda: dve.tensor_tensor(q, v, v, ALU.mult), *ready)
        yield
        t = V(lambda: dve.reduce_sum(ss, q, AX), t)
        t = rstd_of(ss, r_, 128, t, 8)
        yield
        if mul != 1.0:
            t = V(lambda: dve.tensor_scalar(r_, r_, mul, None, ALU.mult), t)
        t = V(lambda: dve.tensor_tensor(v, v, wide(r_, 2, 128), ALU.mult), t)
        yield
        v2 = x.rearrange("p (t n) -> p t n", t=2)
        t = V(lambda: dve.tensor_tensor(v2, v2, wide(ng, 1, 2), ALU.mult), t, tng)
        yield
        res.append(V(lambda: dve.tensor_tensor(x, x, z, ALU.mult), t, tz_))

    toaf, tobf = [], []

    def ya_steps():
        yield from head128(flat(oa[:]), f1(0), nab[:, 0, :], t_na, 1.0 - lam_init, toa, tsa, 200,
                           flat(aq)[:, 0:1024], toaf)
        dump("ya", oa[:], toaf[0])
        P.wait("act", x1_last)
        P.wait("dve", x1_last)
        for tt in range(2):
            yield
            to_T(lambda c: oa[:, tt, c * 128:(c + 1) * 128], 4, X1, 0, [toaf[0]], [3], tt)

    ya = ya_steps()
    some(rg, 2)
    for i, _ in enumerate(mlstm()):
        next(rg, None)
        if i > 0:
            next(ya, None)
            next(rg, None)
    some(ya, 9)
    dump("ob", ob[:], tob[-1])
    for _ in rg:
        pass
    tsb = C(lambda: act.activation(f1(2), f1(2), ACT.Silu), *tzo[2])
    t = V(lambda: dve.tensor_tensor(flat(ob[:]), flat(ob[:]), f1(1), ALU.mult), tsg, *tob)
    run(head128(flat(ob[:]), f1(2), nab[:, 1, :], t_nb, 1.0, [t], tsb, 216, flat(qkc[:])[:, 0:1024], tobf))
    dump("yb", ob[:], tobf[0])
    tgs = []
    for c in range(4):
        v = (ga_t if c < 2 else gb_t)[:, 4 * (c % 2):4 * (c % 2) + 4, :]
        tgs.append(C(lambda: act.activation(v, v, ACT.Sigmoid), tgab[2 * c + 1], tgab[2 * c]))
    xrow = [flat(ak[:]), flat(vb[:])]
    for tt in range(2):
        for j in range(2):
            b = 4 + 2 * tt + j
            take(b)
            P.wait("pe", *h_done)
            for c in range(4):
                t = T(lambda: pe.transpose(bank[b][:, c * 128:(c + 1) * 128],
                                           hT[:, 4 * j + c, tt * 128:(tt + 1) * 128], ident[:]))
            t = C(lambda: act.copy(xrow[tt][:, j * 512:(j + 1) * 512], bank[b][:]), t)
            free[b] = [t]
    t_xrow = t
    YA = (xh[1], xl[1], X1[2])
    x0_last = ("pe_w", P.counts["pe_w"])
    P.wait("act", x0_last)
    P.wait("dve", x0_last)
    gn = f1(0)
    t_gn = load(gn, rows128(A["norm_post_2"][0]), toaf[0], eng="act")
    ta_ = [lin_A(YA, DA["w_a_2"][0], 4, c * 256, c) for c in range(4)]
    for tt in range(2):
        to_T(lambda c: ob[:, tt, c * 128:(c + 1) * 128], 4, X1, 4, [tobf[0]], [4 + tt], tt)
    YB = (xh[1][:, 4:8, :], xl[1][:, 4:8, :], X1[2][4:8])
    ua = []
    for c in range(4):
        ga_c = flat(ga_t[:, 2 * c:2 * c + 2, :])
        ua.append(V(lambda: dve.tensor_tensor(ga_c, ga_c, bank[c][:], ALU.mult), ta_[c], *tgs))
        free[c] = [ua[c]]
    for c in range(4):
        bb = 4 + (c + 2) % 4
        t2 = lin_A(YB, DA["w_b_2"][0], 4, c * 256, bb)
        oa_ = ga_t[:, 2 * c:2 * c + 2, :].rearrange("p a b -> p (a b)")
        ob_ = gb_t[:, 2 * c:2 * c + 2, :].rearrange("p a b -> p (a b)")
        u2 = V(lambda: dve.tensor_tensor(ob_, ob_, bank[bb][:], ALU.mult), t2)
        free[bb] = [u2]
        u = V(lambda: dve.tensor_tensor(oa_, oa_, ob_, ALU.add), ua[c], u2)
        oh = X0[0][:, 2 * c:2 * c + 2, :].rearrange("p a b -> p (a b)")
        ol = X0[1][:, 2 * c:2 * c + 2, :].rearrange("p a b -> p (a b)")
        th = C(lambda: act.copy(oh, oa_), u)
        tl = V(lambda: dve.tensor_tensor(ol, oa_, oh.bitcast(F32), ALU.subtract), th)
        X0[2][2 * c] = X0[2][2 * c + 1] = [th, tl]
    t = run(lin_B(X0, DA["w_out_2"][0], 8, 0, D, LOWB, tail=4))
    outs = []
    for tt in range(2):
        sq_, fin = flat(aq)[:, tt * 1024:(tt + 1) * 1024], flat(qkc[:])[:, tt * 1024:(tt + 1) * 1024]
        ss, rr = small[:, 240 + 4 * tt:242 + 4 * tt], small[:, 242 + 4 * tt:243 + 4 * tt]
        q = [slice(j * 512, (j + 1) * 512) for j in range(2)]
        u, v = [], []
        for j in range(2):
            b = 2 * tt + j
            u.append(C(lambda: act.activation(sq_[:, q[j]], bank[b][:], ACT.Square, accum_out=ss[:, j:j + 1]),
                       tail_done[tt][j]))
            v.append(V(lambda: dve.tensor_tensor(fin[:, q[j]], bank[b][:], gn[:, q[j]], ALU.mult), u[j], t_gn))
        r_ = G(lambda: pool.tensor_tensor(rr, ss[:, 0:1], ss[:, 1:2], ALU.add), *u)
        r_ = rstd_of(rr, rr, D, r_)
        for j in range(2):
            w = V(lambda: dve.scalar_tensor_tensor(out=fin[:, q[j]], in0=fin[:, q[j]], scalar=rr,
                                                   in1=xrow[tt][:, q[j]], op0=ALU.mult, op1=ALU.add),
                  r_, v[j], t_xrow)
            outs.append(load(out[0, tt * 128:(tt + 1) * 128, q[j]], fin[:, q[j]], w, eng="sp" if j else "act"))
    mx.close()
    P.wait("sp", *outs, *dumps)
    assert state["used"] == len(plan) and not hooks


_INS = ['x', 'mem', 'positions', 'ffn1_norm_g', 'ffn1_w_gate', 'ffn1_w_up', 'ffn1_w_down', 'mix_norm_g',
        'mem_norm_g', 'w_mem_kv', 'mem_q_norm_g', 'mem_k_norm_g', 'w_o', 'ffn2_norm_g', 'ffn2_w_gate',
        'ffn2_w_up', 'ffn2_w_down', 'a_w_in', 'a_dw_kernel', 'a_dw_bias', 'a_ln_g', 'a_ln_b', 'kv_norm_g',
        'w_kv', 'k_norm_g', 'b_w_in', 'b_q_norm_g', 'norm_pre_2', 'norm_post_2', 'w_in_2', 'b_if_2',
        'conv_qk_2', 'lambda_qk_2', 'norm_a_2', 'norm_b_2', 'w_a_2', 'w_b_2', 'w_out_2']


def kernel(**inputs):
    import numpy as _np
    import concourse.bacc as _bacc
    from concourse import mybir as _mybir
    from concourse.bass_utils import run_bass_kernel_spmd as _run

    nc = _bacc.Bacc("TRN2", target_bir_lowering=False, num_devices=1)
    arrays, args = {}, {}
    for name in _INS:
        a = _np.ascontiguousarray(inputs[name])
        arrays[f"in_{name}"] = a
        args[name] = nc.dram_tensor(f"in_{name}", a.shape, _mybir.dt.from_np(a.dtype), kind="ExternalInput").ap()
    out = nc.dram_tensor("out_0", (1, S, D), _mybir.dt.float32, kind="ExternalOutput").ap()
    program(nc, args, out)
    r = _run(nc, [arrays], core_ids=[0])
    return r.results[0]["out_0"]
```
